# Optimizing a Trainium2 kernel written in Bass

```python
import math
import jax, jax.numpy as jnp
from jax import lax
import numpy as np

D_MODEL = 1024
BATCH = 1
SEQ = 512
DEPTH = 2

DIFF_HEADS = 4
DIFF_QK_DIM = 32
DIFF_V_DIM = 64
MLA_HEADS = 6
MLA_Q_RANK = 256
MLA_KV_RANK = 128
MLA_NOPE_DIM = 64
MLA_ROPE_DIM = 32
MLA_V_DIM = 64
DIL_HEADS = 6
DIL_HEAD_DIM = 64
DIL_PAIRS = ((128, 1), (512, 4), (2048, 16))
BAND_BLOCK = 64
Q_BLOCK = 128
ROPE_THETA = 10000.0
A_QK_WIDTH = DIFF_HEADS * 2 * DIFF_QK_DIM
A_WIDTH = DIFF_HEADS * DIFF_V_DIM
B_WIDTH = MLA_HEADS * MLA_V_DIM
C_WIDTH = DIL_HEADS * DIL_HEAD_DIM
MIX_WIDTH = A_WIDTH + B_WIDTH + C_WIDTH
IN_WIDTH = 2 * A_QK_WIDTH + A_WIDTH + MLA_Q_RANK + MLA_KV_RANK + MLA_ROPE_DIM + 3 * C_WIDTH
PEER_HEADS = 8
PEER_N_KEYS = 128
PEER_N_EXPERTS = PEER_N_KEYS * PEER_N_KEYS
PEER_QUERY_DIM = 256
PEER_HALF_DIM = PEER_QUERY_DIM // 2
PEER_TOPK = 16
PEER_CHUNK = 128
DEEPNORM_ALPHA = (2 * DEPTH) ** 0.25
DEEPNORM_BETA = (8 * DEPTH) ** -0.25
LN_EPS = 1e-5
NEG_INF = -1e30

kernel_name = 'hybrid_diff_mla_dilated_peer_encoder'

def rms_norm(x, g):
    x32 = x.astype(jnp.float32)
    y = x32 * lax.rsqrt(jnp.mean(x32 * x32, axis=-1, keepdims=True) + LN_EPS)
    return (y * g.astype(jnp.float32)).astype(x.dtype)

def layer_norm(x, g, b):
    x32 = x.astype(jnp.float32)
    xc = x32 - jnp.mean(x32, axis=-1, keepdims=True)
    var = jnp.mean(xc * xc, axis=-1, keepdims=True)
    y = xc * lax.rsqrt(var + LN_EPS) * g.astype(jnp.float32) + b.astype(jnp.float32)
    return y.astype(x.dtype)

def rope(t, pos):
    half = t.shape[-1] // 2
    inv_freq = jnp.exp(-math.log(ROPE_THETA) * jnp.arange(half, dtype=jnp.float32) / half)
    ang = pos.astype(jnp.float32)[:, None] * inv_freq[None, :]
    cos, sin = jnp.cos(ang), jnp.sin(ang)
    t32 = t.astype(jnp.float32)
    t1, t2 = t32[..., :half], t32[..., half:]
    return jnp.concatenate([t1 * cos - t2 * sin, t2 * cos + t1 * sin], axis=-1).astype(t.dtype)

def to_heads(t, n_heads):
    b, s, _ = t.shape
    return t.reshape(b, s, n_heads, -1).transpose(0, 2, 1, 3)

def from_heads(t):
    b, h, s, d = t.shape
    return t.transpose(0, 2, 1, 3).reshape(b, s, h * d)

def dense_attention(q, k, v, scale):
    b, h, s, dk = q.shape
    nb = s // Q_BLOCK
    qb = q.reshape(b, h, nb, Q_BLOCK, dk).transpose(2, 0, 1, 3, 4)

    def block(qi):
        sc = jnp.einsum('bhqd,bhkd->bhqk', qi, k, preferred_element_type=jnp.float32) * scale
        p = jax.nn.softmax(sc, axis=-1)
        return jnp.einsum('bhqk,bhkd->bhqd', p.astype(v.dtype), v)

    o = lax.map(block, qb)
    return o.transpose(1, 2, 0, 3, 4).reshape(b, h, s, v.shape[-1])

def banded_attention(q, k, v, half, scale):
    lead = q.shape[:-2]
    length, dk = q.shape[-2], q.shape[-1]
    dv = v.shape[-1]
    nb = -(-length // BAND_BLOCK)
    lp = nb * BAND_BLOCK
    span = BAND_BLOCK + 2 * half
    pad_q = [(0, 0)] * (q.ndim - 2) + [(0, lp - length), (0, 0)]
    pad_kv = [(0, 0)] * (q.ndim - 2) + [(half, half + lp - length), (0, 0)]
    qb = jnp.pad(q, pad_q).reshape(*lead, nb, BAND_BLOCK, dk)
    starts = jnp.arange(nb) * BAND_BLOCK
    idx = starts[:, None] + jnp.arange(span)[None, :]
    kb = jnp.take(jnp.pad(k, pad_kv), idx, axis=-2)
    vb = jnp.take(jnp.pad(v, pad_kv), idx, axis=-2)
    sc = jnp.einsum('...nqd,...nkd->...nqk', qb, kb, preferred_element_type=jnp.float32) * scale
    t = jnp.arange(BAND_BLOCK)[:, None]
    j = jnp.arange(span)[None, :]
    in_band = jnp.abs(j - half - t) <= half
    key_pos = starts[:, None, None] + j[None] - half
    mask = in_band[None] & (key_pos >= 0) & (key_pos < length)
    sc = jnp.where(mask, sc, NEG_INF)
    lse = jax.nn.logsumexp(sc, axis=-1)
    p = jnp.exp(sc - lse[..., None])
    o = jnp.einsum('...nqk,...nkd->...nqd', p.astype(v.dtype), vb)
    o = o.reshape(*lead, lp, dv)[..., :length, :]
    lse = lse.reshape(*lead, lp)[..., :length]
    return o, lse

def to_strided(t, dil):
    b, h, s, d = t.shape
    return t.reshape(b, h, s // dil, dil, d).swapaxes(2, 3)

def diff_attention(q, k, v, lam, subln_g, lambda_init, pos):
    b, s, _ = q.shape
    q = rope(to_heads(q, 2 * DIFF_HEADS), pos).reshape(b, DIFF_HEADS, 2, s, DIFF_QK_DIM)
    k = rope(to_heads(k, 2 * DIFF_HEADS), pos).reshape(b, DIFF_HEADS, 2, s, DIFF_QK_DIM)
    v = to_heads(v, DIFF_HEADS)
    scale = DIFF_QK_DIM ** -0.5
    o1 = dense_attention(q[:, :, 0], k[:, :, 0], v, scale)
    o2 = dense_attention(q[:, :, 1], k[:, :, 1], v, scale)
    lam32 = lam.astype(jnp.float32)
    lam_full = (jnp.exp(jnp.sum(lam32[0] * lam32[1])) - jnp.exp(jnp.sum(lam32[2] * lam32[3]))
                + lambda_init)
    o = o1 - lam_full.astype(o1.dtype) * o2
    o = rms_norm(o, subln_g) * (1.0 - lambda_init)
    return from_heads(o)

def mla_attention(c_q, c_kv, k_rope, q_norm_g, kv_norm_g, w_uq, w_ukv, pos):
    b, s, _ = c_q.shape
    q = to_heads(rms_norm(c_q, q_norm_g) @ w_uq, MLA_HEADS)
    q = jnp.concatenate([q[..., :MLA_NOPE_DIM], rope(q[..., MLA_NOPE_DIM:], pos)], axis=-1)
    kv = to_heads(rms_norm(c_kv, kv_norm_g) @ w_ukv, MLA_HEADS)
    k_nope, v = kv[..., :MLA_NOPE_DIM], kv[..., MLA_NOPE_DIM:]
    k_pe = rope(k_rope[:, None], pos)
    k = jnp.concatenate([k_nope, jnp.broadcast_to(k_pe, (b, MLA_HEADS, s, MLA_ROPE_DIM))], axis=-1)
    o = dense_attention(q, k, v, (MLA_NOPE_DIM + MLA_ROPE_DIM) ** -0.5)
    return from_heads(o)

def dilated_attention(q, k, v, pos):
    b, s, _ = q.shape
    q = rope(to_heads(q, DIL_HEADS), pos)
    k = rope(to_heads(k, DIL_HEADS), pos)
    v = to_heads(v, DIL_HEADS)
    scale = DIL_HEAD_DIM ** -0.5
    outs, lses = [], []
    for window, dil in DIL_PAIRS:
        half = window // (2 * dil)
        o, lse = banded_attention(to_strided(q, dil), to_strided(k, dil), to_strided(v, dil), half, scale)
        outs.append(o.swapaxes(2, 3).reshape(b, DIL_HEADS, s, DIL_HEAD_DIM))
        lses.append(lse.swapaxes(2, 3).reshape(b, DIL_HEADS, s))
    wts = jax.nn.softmax(jnp.stack(lses), axis=0)
    o = jnp.einsum('pbhs,pbhsd->bhsd', wts.astype(v.dtype), jnp.stack(outs))
    return from_heads(o)

def peer_ffn(x, w_q, sub_keys, u, v):
    b, s, d = x.shape
    xt = x.reshape(-1, PEER_CHUNK, d)
    kk = PEER_TOPK

    def chunk(xc):
        c = xc.shape[0]
        q = (xc @ w_q).reshape(c, PEER_HEADS, 2, PEER_HALF_DIM)
        sc = jnp.einsum('chpd,hpnd->chpn', q, sub_keys, preferred_element_type=jnp.float32)
        top_s, top_i = lax.top_k(sc, kk)
        cand = top_s[:, :, 0, :, None] + top_s[:, :, 1, None, :]
        cand_s, cand_i = lax.top_k(cand.reshape(c, PEER_HEADS, kk * kk), kk)
        i1 = jnp.take_along_axis(top_i[:, :, 0], cand_i // kk, axis=-1)
        i2 = jnp.take_along_axis(top_i[:, :, 1], cand_i % kk, axis=-1)
        experts = i1 * PEER_N_KEYS + i2
        gates = jax.nn.softmax(cand_s, axis=-1)
        ue = jnp.take(u, experts, axis=0)
        ve = jnp.take(v, experts, axis=0)
        act = jax.nn.gelu(jnp.einsum('chkd,cd->chk', ue, xc), approximate=False)
        return jnp.einsum('chk,chkd->cd', gates.astype(xc.dtype) * act, ve)

    return lax.map(chunk, xt).reshape(b, s, d)

def setup_inputs(seed: int = 0) -> dict:
    key = jax.random.key(seed)
    ks = jax.random.split(key, 17)

    def nrm(k, shape, scale):
        return jax.random.normal(k, shape, jnp.float32) * scale

    L = DEPTH
    return {
        'x': nrm(ks[0], (BATCH, SEQ, D_MODEL), 1.0),
        'w_in': nrm(ks[1], (L, D_MODEL, IN_WIDTH), D_MODEL ** -0.5),
        'diff_lambda': nrm(ks[2], (L, 4, DIFF_QK_DIM), 0.1),
        'diff_subln_g': 1.0 + nrm(ks[3], (L, DIFF_V_DIM), 0.02),
        'mla_q_norm_g': 1.0 + nrm(ks[4], (L, MLA_Q_RANK), 0.02),
        'mla_kv_norm_g': 1.0 + nrm(ks[5], (L, MLA_KV_RANK), 0.02),
        'mla_w_uq': nrm(ks[6], (L, MLA_Q_RANK, MLA_HEADS * (MLA_NOPE_DIM + MLA_ROPE_DIM)), MLA_Q_RANK ** -0.5),
        'mla_w_ukv': nrm(ks[7], (L, MLA_KV_RANK, MLA_HEADS * (MLA_NOPE_DIM + MLA_V_DIM)), MLA_KV_RANK ** -0.5),
        'w_o': nrm(ks[8], (L, MIX_WIDTH, D_MODEL), MIX_WIDTH ** -0.5 * DEEPNORM_BETA),
        'ln1_g': 1.0 + nrm(ks[9], (L, D_MODEL), 0.02),
        'ln1_b': nrm(ks[10], (L, D_MODEL), 0.02),
        'peer_w_q': nrm(ks[11], (L, D_MODEL, PEER_HEADS * PEER_QUERY_DIM), D_MODEL ** -0.5),
        'peer_sub_keys': nrm(ks[12], (L, PEER_HEADS, 2, PEER_N_KEYS, PEER_HALF_DIM), PEER_HALF_DIM ** -0.5),
        'peer_u': nrm(ks[13], (L, PEER_N_EXPERTS, D_MODEL), D_MODEL ** -0.5),
        'peer_v': nrm(ks[14], (L, PEER_N_EXPERTS, D_MODEL), DEEPNORM_BETA),
        'ln2_g': 1.0 + nrm(ks[15], (L, D_MODEL), 0.02),
        'ln2_b': nrm(ks[16], (L, D_MODEL), 0.02),
    }

def reference(x, w_in, diff_lambda, diff_subln_g, mla_q_norm_g, mla_kv_norm_g, mla_w_uq, mla_w_ukv,
              w_o, ln1_g, ln1_b, peer_w_q, peer_sub_keys, peer_u, peer_v, ln2_g, ln2_b):
    pos = jnp.arange(x.shape[1], dtype=jnp.int32)
    sizes = (A_QK_WIDTH, A_QK_WIDTH, A_WIDTH, MLA_Q_RANK, MLA_KV_RANK, MLA_ROPE_DIM,
             C_WIDTH, C_WIDTH, C_WIDTH)
    cuts = np.cumsum(sizes)[:-1].tolist()
    for l in range(DEPTH):
        lambda_init = 0.8 - 0.6 * math.exp(-0.3 * (l + 1))
        h = x @ w_in[l]
        a_q, a_k, a_v, b_cq, b_ckv, b_kr, c_q, c_k, c_v = jnp.split(h, cuts, axis=-1)
        out_a = diff_attention(a_q, a_k, a_v, diff_lambda[l], diff_subln_g[l], lambda_init, pos)
        out_b = mla_attention(b_cq, b_ckv, b_kr, mla_q_norm_g[l], mla_kv_norm_g[l],
                              mla_w_uq[l], mla_w_ukv[l], pos)
        out_c = dilated_attention(c_q, c_k, c_v, pos)
        mix = jnp.concatenate([out_a, out_b, out_c], axis=-1) @ w_o[l]
        x = layer_norm(DEEPNORM_ALPHA * x + mix, ln1_g[l], ln1_b[l])
        ffn = peer_ffn(x, peer_w_q[l], peer_sub_keys[l], peer_u[l], peer_v[l])
        x = layer_norm(DEEPNORM_ALPHA * x + ffn, ln2_g[l], ln2_b[l])
    return x


_drawn_inputs = setup_inputs


def setup_inputs(seed=0):
    import zlib

    import numpy as np

    out = dict(_drawn_inputs(seed))
    spreads = {}
    factors = {'diff_subln_g': 2.941, 'mla_q_norm_g': 5.79, 'mla_kv_norm_g': 5.149}
    for name, (base, spread) in spreads.items():
        noise = np.random.default_rng([zlib.crc32(name.encode()), seed]).standard_normal(out[name].shape)
        drawn = base * np.exp(spread * noise) if base else spread * noise
        out[name] = __import__('jax').numpy.asarray(drawn.astype(out[name].dtype))
    for name, factor in factors.items():
        out[name] = (out[name] * factor).astype(out[name].dtype)
    return out
```

```python
import math
from contextlib import ExitStack

import numpy as np

import concourse.bass as bass
from concourse import mybir

F32 = mybir.dt.float32
F32R = mybir.dt.float32r
U32 = mybir.dt.uint32
BF16 = mybir.dt.bfloat16
ALU = mybir.AluOpType
ACT = mybir.ActivationFunctionType
AX_X = mybir.AxisListType.X
ds = bass.ds

P = 128
L = 2
T = 512
D = 1024
TB = T // P
DC = D // P
AH, ADK, ADV = 4, 32, 64
BH, BNOPE, BROPE, BV = 6, 64, 32, 64
QR, KVR = 256, 128
CH, CDK = 6, 64
A_W, C_W = AH * ADV, CH * CDK
COL_AQ, COL_AK, COL_AV = 0, 256, 512
COL_CQ = 768
COL_CKV = COL_CQ + QR
COL_KR = COL_CKV + KVR
COL_C = COL_KR + BROPE
IN_W = COL_C + 3 * C_W
UQ_W = BH * (BNOPE + BROPE)
UKV_W = BH * (BNOPE + BV)
PH, NK, TOPK = 8, 128, 16
NEXP = NK * NK
ALPHA = (2 * L) ** 0.25
LN_EPS = 1e-5

IN_G, IN_N = 8, IN_W // 8
O_G, O_N = 4, D // 4
W_PER = IN_G + O_G
JA, JB, JC = 2 * AH, BH, CH
JOBS = JA + JB + JC
DK = BNOPE + BROPE
VD = 64
MAPS = JOBS * TB
QB = 2 * PH
EB = NEXP // P
ST_PER = QB + EB
UNITS = TB * PH
BLOCKS_TOPK = 2 * UNITS
WIN, WIN_T = 8, T // 8
BODY_T = 16
OH = 8
BODIES = WIN_T // BODY_T
assert IN_G * IN_N == IN_W and BLOCKS_TOPK + 2 * WIN * BODIES == EB
PRIME = 2
BIG = 1.0e30
NEG = -3.0e38
MASK_W = T + 3 * P


class Steps:

    def __init__(self, eng, sem):
        self.eng, self.sem, self.base, self.n = eng, sem, 0, 0

    def at(self, base):
        self.base, self.n = base, 0

    def done(self, ins):
        ins.then_inc(self.sem, 1)
        self.n += 1

    def wait(self):
        self.eng.wait_ge(self.sem, self.base + self.n)

    def wait_apart(self, waited):
        self.wait()
        self.eng.sem_inc(waited, 1)


def build(nc, a, out):
    ctx = ExitStack()
    base = (nc.sbuf_base + 63) // 64 * 64
    limit = nc.sbuf_usable_end

    class Region:
        def __init__(self, start):
            self.start, self.end = start, start

        def tile(self, name, shape, dt):
            size = int(np.prod(shape[1:])) * (2 if dt == BF16 else 4)
            t = nc.alloc_sbuf_tensor_at(name, list(shape), dt, offset=self.end)
            self.end += (size + 63) // 64 * 64
            assert self.end <= limit, (name, self.end, limit)
            return t

    keep = Region(base)
    x_tok = keep.tile("x_tok", [P, TB, D], F32)
    t_hi = keep.tile("t_hi", [P, DC, T], F32R)
    t_lo = keep.tile("t_lo", [P, DC, T], F32R)
    ident = keep.tile("ident", [P, P], F32)
    iota = keep.tile("iota", [P, P], F32)
    zeros = keep.tile("zeros", [P, T], F32)
    zeros_bf = zeros[:].bitcast(BF16)
    neg_max = keep.tile("neg_max", [P, 2], F32)
    row_sum = keep.tile("row_sum", [P, 2, TB], F32)
    row_inv = keep.tile("row_inv", [P, 2, TB], F32)
    lat_sq = keep.tile("lat_sq", [P, 2, TB], F32)
    lat_rms = keep.tile("lat_rms", [P, 2, TB], F32)
    lat_inv = keep.tile("lat_inv", [P, 2, TB], F32)
    sub_sq = keep.tile("sub_sq", [P, TB * AH], F32)
    sub_rms = keep.tile("sub_rms", [P, TB * AH], F32)
    sub_inv = keep.tile("sub_inv", [P, TB * AH], F32)
    lam_dot = keep.tile("lam_dot", [P, 2], F32)
    lam_exp = keep.tile("lam_exp", [P, 2], F32)
    lam_neg = keep.tile("lam_neg", [P, 2], F32)
    bn = keep.tile("bn", [P, TB, 2, 6], F32)
    mean_var = keep.tile("mean_var", [P, TB, 2], F32)
    ln_dev = keep.tile("ln_dev", [P, TB], F32)
    ln_inv = keep.tile("ln_inv", [P, TB], F32)
    eps = keep.tile("eps", [P, 1], F32)

    att = Region(keep.end)
    w_raw = att.tile("w_raw", [P, 2, DC * IN_N], F32)
    h = att.tile("h", [P, TB, IN_W], F32)
    ln_rows = nc.alloc_sbuf_tensor_at("ln_rows", [P, 2, D], F32, offset=att.end)
    ln_rows_at = att.end
    q_b = att.tile("q_b", [P, TB, UQ_W], F32)
    kv_b = att.tile("kv_b", [P, TB, UKV_W], F32)
    o_all = att.tile("o_all", [P, TB, JOBS * VD], F32)
    w_uq = att.tile("w_uq", [P, 2, UQ_W], F32)
    w_ukv = att.tile("w_ukv", [P, UKV_W], F32)
    g_lat = att.tile("g_lat", [P, 4], F32)
    rope32 = att.tile("rope32", [P, 2, TB, 32], F32)
    rope64 = att.tile("rope64", [P, 2, TB, 64], F32)
    mask = att.tile("mask", [P, MASK_W], F32)
    lam_in = att.tile("lam_in", [P, 4, ADK], F32)
    sub_g = att.tile("sub_g", [P, ADV], F32)
    lam_c = att.tile("lam_c", [P, 2], F32)
    w_split = Region(att.end)
    w_hi = w_split.tile("w_hi", [P, 2, DC * IN_N], F32R)
    w_lo = w_split.tile("w_lo", [P, 2, DC * IN_N], F32R)
    hd = Region(att.end)
    lat_n = hd.tile("lat_n", [P, TB, QR + KVR], F32)
    lat_t = hd.tile("lat_t", [P, 3, T], F32)
    rq = hd.tile("rq", [P, 2, TB, 2, DK], F32)
    q_t = hd.tile("q_t", [P, 2, T], F32)
    k_t = hd.tile("k_t", [P, 2, T], F32)
    v_s = hd.tile("v_s", [P, 2, TB, VD], F32)
    sc_s = hd.tile("sc_s", [P, 2], F32)
    masked = hd.tile("masked", [P, 2, T], F32)
    probs = hd.tile("probs", [P, 2, T], F32)
    p_t = hd.tile("p_t", [P, 2, TB, P], F32)
    rt_a = lat_n[:].rearrange("p t d -> p (t d)")[:, 0:TB * 2 * 64].rearrange("p (t k d) -> p t k d", t=TB, k=2)
    rt_b = lat_n[:].rearrange("p t d -> p (t d)")[:, TB * 2 * 64:TB * 4 * 64].rearrange("p (t k d) -> p t k d", t=TB, k=2)
    kpe = hd.tile("kpe", [P, TB, BROPE], F32)
    o_f = lat_t[:].rearrange("p t d -> p (t d)")[:, 0:TB * A_W].rearrange("p (t h d) -> p t h d", t=TB, h=AH)
    o_q = q_t[:].rearrange("p s d -> p (s d)").rearrange("p (t h d) -> p t h d", t=TB, h=AH)

    pr = Region(keep.end)
    st_raw = pr.tile("st_raw", [P, 2, DC * P], F32)
    st_hi = pr.tile("st_hi", [P, 2, DC, P], F32R)
    st_lo = pr.tile("st_lo", [P, 2, DC, P], F32R)
    h_out = pr.tile("h_out", [P, 2, T], F32)
    shared = pr.end
    keys = pr.tile("keys", [P, QB, NK], F32)
    k_hi = pr.tile("k_hi", [P, QB, NK], F32R)
    k_lo = pr.tile("k_lo", [P, QB, NK], F32R)
    pq_hi = pr.tile("pq_hi", [P, 2, T], F32R)
    pq_lo = pr.tile("pq_lo", [P, 2, T], F32R)
    scores = pr.tile("scores", [P, UNITS, 2, NK], F32)
    tk = Region(pr.end)
    opt16 = tk.tile("opt16", [P, 2, TOPK, TOPK], BF16)
    wk = tk.tile("wk", [P, 2, NK], F32)
    wk2 = tk.tile("wk2", [P, 2, NK], F32)
    v16 = tk.tile("v16", [P, 2, TOPK], F32)
    x16 = tk.tile("x16", [P, 2, TOPK], U32)
    x16f = tk.tile("x16f", [P, 2, TOPK], F32)
    cand = tk.tile("cand", [P, TOPK, TOPK], F32)
    cand2 = tk.tile("cand2", [P, TOPK * TOPK], F32)
    c16 = tk.tile("c16", [P, TOPK], F32)
    ci = tk.tile("ci", [P, TOPK], U32)
    cab = tk.tile("cab", [P, 2, TOPK], U32)
    cabf = tk.tile("cabf", [P, 2, TOPK], BF16)
    eq = tk.tile("eq", [P, 2, TOPK, TOPK], F32)
    c_all = tk.tile("c_all", [P, UNITS, TOPK], F32)
    i_all = tk.tile("i_all", [P, 2, UNITS * TOPK], F32)
    e_all = tk.tile("e_all", [P, UNITS, TOPK], F32)
    c_top = tk.tile("c_top", [P, UNITS], F32)
    z_all = tk.tile("z_all", [P, 2, UNITS], F32)
    ga = Region(shared)
    g_stage = ga.tile("g_stage", [P, 2, NK, WIN_T], F32)
    gb = Region(max(tk.end, ga.end))
    i_t = gb.tile("i_t", [P, 2, T], F32)
    g_hi = gb.tile("g_hi", [P, T], F32R)
    g_lo = gb.tile("g_lo", [P, T], F32R)
    oh = gb.tile("oh", [P, OH, 3, P], F32R)
    vp = Region(keep.end)
    v_raw = vp.tile("v_raw", [P, 2, D], F32)
    v_hi = vp.tile("v_hi", [P, 2, D], F32R)
    v_lo = vp.tile("v_lo", [P, 2, D], F32R)
    g_in = vp.tile("g_in", [P, 2, T], F32)
    h_in = vp.tile("h_in", [P, 2, T], F32)
    w_f = vp.tile("w_f", [P, 2, T], F32)
    wt_hi = vp.tile("wt_hi", [P, 2, T], F32R)
    wt_lo = vp.tile("wt_lo", [P, 2, T], F32R)
    assert vp.end <= ln_rows_at

    ps = ctx.enter_context(nc.psum_tensor("ps", [P, 8, 512], F32))
    gates_d = nc.dram_tensor("gates_d", [EB, P, T], F32, kind="Internal").ap()
    gelu_d = nc.dram_tensor("gelu_d", [EB, P, T], F32, kind="Internal").ap()

    def sem(name):
        return ctx.enter_context(nc.semaphore(name))

    s_x = sem("s_x")
    eps_set = sem("eps_set")
    s_lay = sem("s_lay")
    s_keys, s_ln = sem("s_keys"), sem("s_ln")
    s_wraw = [sem(f"s_wraw{s}") for s in range(2)]
    s_straw = [sem(f"s_straw{s}") for s in range(2)]
    s_vraw = [sem(f"s_vraw{s}") for s in range(2)]
    s_gh = [sem(f"s_gh{s}") for s in range(2)]
    s_hst = [sem(f"s_hst{s}") for s in range(2)]
    s_gst = [sem(f"s_gst{s}") for s in range(2)]
    s_out = sem("s_out")
    tr_ps, tr_hi, tr_lo = sem("tr_ps"), sem("tr_hi"), sem("tr_lo")
    wc_hi, wc_lo = sem("wc_hi"), sem("wc_lo")
    pj_ps, pj_act, pj_dve, pj_res = sem("pj_ps"), sem("pj_act"), sem("pj_dve"), sem("pj_res")
    lat_ss, lat_sd, lat_ready, lat_tr, lat_ev, lat_ps, lat_qev, lat_kev = (sem(n) for n in (
        "lat_ss", "lat_sd", "lat_ready", "lat_tr", "lat_ev", "lat_ps", "lat_qev", "lat_kev"))
    rope_done, qk_tr, q_ev, k_ev, s_ps, s_min, s_exp, pt_ps, pt_dve, pt_act, pv_done, o_ev = (sem(n) for n in (
        "rope_done", "qk_tr", "q_ev", "k_ev", "s_ps", "s_min", "s_exp", "pt_ps", "pt_dve", "pt_act", "pv_done",
        "o_ev"))
    sub_ss, sub_sd, mix_ready = sem("sub_ss"), sem("sub_sd"), sem("mix_ready")
    lam_s, lam_e = sem("lam_s"), sem("lam_e")
    ln_var, ln_sd, ln_done = sem("ln_var"), sem("ln_sd"), sem("ln_done")
    keys_hi, keys_lo = sem("keys_hi"), sem("keys_lo")
    st_h, st_l, st_used = sem("st_h"), sem("st_l"), sem("st_used")
    pq_h, pq_l, sc_ps, sc_ev = sem("pq_h"), sem("pq_l"), sem("sc_ps"), sem("sc_ev")
    gelu_done = sem("gelu_done")
    topk_done, gate_sub, gate_exp, gate_ready, sel_tr, sel_act, sel_dve = (sem(n) for n in (
        "topk_done", "gate_sub", "gate_exp", "gate_ready", "sel_tr", "sel_act", "sel_dve"))
    oh_ready, g_tok, g_ev = sem("oh_ready"), sem("g_tok"), sem("g_ev")
    v_h, v_l, wt_f, wt_h, wt_l, v_used = (sem(n) for n in ("v_h", "v_l", "wt_f", "wt_h", "wt_l", "v_used"))
    ffn_done = sem("ffn_done")
    waited = sem("waited")
    dve_step, pool_step = sem("dve_step"), sem("pool_step")

    block = ctx.enter_context(nc.Block())

    @block.sync
    def _(sp):
        for dst, src in ((x_tok[:], a["x"]), (ident[:], a["ident"]), (iota[:], a["iota"])):
            sp.dma_start(dst, src).then_inc(s_x, 16)
        with sp.Fori(0, L) as l:
            sp.wait_ge(ln_done, 2 * TB * l + PRIME)
            for dst, src in (
                (w_uq[:], a["mla_w_uq"][l]), (w_ukv[:], a["mla_w_ukv"][l]), (g_lat[:], a["g_lat"][l]),
                (lam_in[:], a["diff_lambda"][l].partition_broadcast(P)),
                (sub_g[:], a["diff_subln_g"][l].partition_broadcast(P)),
                (lam_c[:], a["lam_c"][l].partition_broadcast(P)),
                (rope32[:], a["rope32"]), (rope64[:], a["rope64"]), (mask[:], a["mask"]),
            ):
                sp.dma_start(dst, src).then_inc(s_lay, 16)

            def w_load(n, s, src):
                sp.wait_ge(wc_lo, W_PER * l + n + 1)
                sp.dma_start(w_raw[:, s, 0:src.shape[1]], src).then_inc(s_wraw[s], 16)

            with sp.Fori(0, IN_G // 2) as i:
                for s in range(2):
                    w_load(2 * i + s, s, a["w_in"][l, 2 * i + s])
            for k in range(O_G):
                w_load(IN_G + k, k % 2, a["w_o"][l, k])
                if k == 1:
                    sp.wait_ge(rope_done, JOBS * (l + 1))
                    sp.dma_start(ln_rows[:], a["ln1"][l].partition_broadcast(P)).then_inc(s_ln, 16)
            sp.wait_ge(pj_res, O_G * TB * (l + 1))
            sp.dma_start(keys[:], a["peer_keys"][l]).then_inc(s_keys, 16)

            def st_load(n, s, src):
                sp.wait_ge(st_l, ST_PER * l + n + 1)
                sp.dma_start(st_raw[:, s], src).then_inc(s_straw[s], 16)

            with sp.Fori(0, QB // 2) as i:
                for s in range(2):
                    st_load(2 * i + s, s, a["peer_w_q"][l, 2 * i + s])
            def gelu_store(i, s):
                sp.wait_ge(gelu_done, EB * l + 2 * i + s + 1 + PRIME)
                sp.dma_start(gelu_d[2 * i + s], h_out[:, s]).then_inc(s_hst[s], 16)

            for s in range(2):
                st_load(QB + s, s, a["peer_u"][l, s])
            with sp.Fori(0, EB // 2 - 1) as i:
                for s in range(2):
                    st_load(QB + 2 * i + 2 + s, s, a["peer_u"][l, 2 * i + 2 + s])
                for s in range(2):
                    gelu_store(i, s)
            for s in range(2):
                gelu_store(EB // 2 - 1, s)
            for s in range(2):
                sp.wait_ge(s_hst[s], 16 * (EB // 2 * (l + 1) + 1))
                sp.sem_inc(waited, 1)
                sp.wait_ge(s_gst[s], 16 * (WIN // 2 * (l + 1) + 1))
                sp.sem_inc(waited, 1)
            sp.wait_ge(st_used, ST_PER * (l + 1) + PRIME)
            sp.dma_start(ln_rows[:], a["ln2"][l].partition_broadcast(P)).then_inc(s_ln, 16)
            with sp.Fori(0, EB // 2) as i:
                for s in range(2):
                    b = 2 * i + s
                    sp.wait_ge(v_l, EB * l + b + 1)
                    sp.dma_start(v_raw[:, s], a["peer_v"][l, b]).then_inc(s_vraw[s], 16)
                    sp.wait_ge(wt_f, EB * l + b + 1)
                    sp.dma_start(g_in[:, s], gates_d[b]).then_inc(s_gh[s], 16)
                    sp.dma_start(h_in[:, s], gelu_d[b]).then_inc(s_gh[s], 16)
        sp.wait_ge(ln_done, 2 * TB * L + PRIME)
        sp.dma_start(out, x_tok[:]).then_inc(s_out, 16)
        sp.wait_ge(s_out, 16)

    @block.gpsimd
    def _(pool):
        step = Steps(pool, pool_step)
        n_a, n_b, n_c = 5, 8, 5
        per = 2 + n_a * JA + 4 + n_b * JB + 2 + n_c * JC
        with pool.Fori(0, L) as l:
            pool.wait_ge(lat_qev, TB * (l + 1))
            pool.wait_ge(lat_kev, TB * (l + 1))
            pool.wait_ge(s_lay, 16 * 9 * (l + 1))
            at = per * l
            step.at(at)
            pool.sem_inc(waited, 1)
            for s in range(2):
                step.done(nc.gpsimd.memset(rq[:, s, :, :, ADK:DK], 0.0))
            step.wait_apart(waited)
            at = at + 2

            def slot_free(j):
                pool.wait_ge(qk_tr, JOBS * l + j + 1)
                pool.wait_ge(q_ev, JOBS * l + j + 1)
                pool.wait_ge(pv_done, JOBS * l + j + 1)

            def rotate(dst, src, first, second, table, w):
                nk = dst.shape[2]
                cos = table[:, 0].unsqueeze(2).to_broadcast([P, TB, nk, w])
                sin = table[:, 1].unsqueeze(2).to_broadcast([P, TB, nk, w])
                ta, tb_ = rt_a[:, :, 0:nk, 0:w], rt_b[:, :, 0:nk, 0:w]
                step.done(nc.gpsimd.tensor_tensor(ta, src, cos, ALU.mult))
                step.done(nc.gpsimd.tensor_tensor(tb_[:, :, :, 0:w // 2], second, sin[:, :, :, 0:w // 2], ALU.mult))
                step.done(nc.gpsimd.tensor_tensor(tb_[:, :, :, w // 2:w], first, sin[:, :, :, w // 2:w], ALU.mult))
                step.wait()
                step.done(nc.gpsimd.tensor_tensor(dst, ta, tb_, ALU.add))

            def rotate_pair(s, col, width, j, w, table):
                v = h[:, :, col:col + 2 * width].rearrange("p t (k f) -> p t k f", k=2)
                half = w // 2
                rotate(rq[:, s, :, :, 0:w], v[:, :, :, ds(j * w, w)], v[:, :, :, ds(j * w, half)],
                       v[:, :, :, ds(j * w + half, half)], table, w)

            def finish(s, dk, v_src):
                step.done(nc.gpsimd.memset(sc_s[:, s:s + 1], -dk ** -0.5))
                step.wait_apart(waited)
                nc.gpsimd.tensor_copy(v_s[:, s], v_src).then_inc(rope_done, 1)

            with pool.Fori(0, AH) as i:
                for s in range(2):
                    j = 2 * i + s
                    step.at(at + n_a * j)
                    slot_free(j)
                    rotate_pair(s, COL_AQ, COL_AK - COL_AQ, j, ADK, rope32)
                    finish(s, ADK, h[:, :, ds(i * ADV + COL_AV, ADV)])
                    assert step.n == n_a
            at = at + n_a * JA
            step.at(at)
            kr = h[:, :, COL_KR:COL_KR + BROPE].unsqueeze(2)
            rotate(kpe[:].unsqueeze(2), kr, kr[:, :, :, 0:BROPE // 2], kr[:, :, :, BROPE // 2:BROPE], rope32, BROPE)
            step.wait_apart(waited)
            at = at + 4
            with pool.Fori(0, JB // 2) as i:
                for s in range(2):
                    j = 2 * i + s
                    step.at(at + n_b * j)
                    slot_free(j + JA)
                    qv = q_b[:].unsqueeze(2)
                    q0, kv0 = j * DK, j * (BNOPE + BV)
                    rotate(rq[:, s, :, 0:1, BNOPE:DK], qv[:, :, :, ds(q0 + BNOPE, BROPE)],
                           qv[:, :, :, ds(q0 + BNOPE, BROPE // 2)],
                           qv[:, :, :, ds(q0 + BNOPE + BROPE // 2, BROPE // 2)], rope32, BROPE)
                    step.done(nc.gpsimd.tensor_copy(rq[:, s, :, 0, 0:BNOPE], q_b[:, :, ds(q0, BNOPE)]))
                    step.done(nc.gpsimd.tensor_copy(rq[:, s, :, 1, 0:BNOPE], kv_b[:, :, ds(kv0, BNOPE)]))
                    step.done(nc.gpsimd.tensor_copy(rq[:, s, :, 1, BNOPE:DK], kpe[:]))
                    finish(s, DK, kv_b[:, :, ds(kv0 + BNOPE, BV)])
                    assert step.n == n_b
            at = at + n_b * JB
            step.at(at)
            pool.wait_ge(qk_tr, JOBS * l + JA + JB + PRIME)
            pool.sem_inc(waited, 1)
            for s in range(2):
                step.done(nc.gpsimd.memset(rq[:, s, :, :, CDK:DK], 0.0))
            step.wait_apart(waited)
            at = at + 2
            with pool.Fori(0, JC // 2) as i:
                for s in range(2):
                    j = 2 * i + s
                    step.at(at + n_c * j)
                    slot_free(j + JA + JB)
                    rotate_pair(s, COL_C, C_W, j, CDK, rope64)
                    finish(s, CDK, h[:, :, ds(j * CDK + COL_C + 2 * C_W, CDK)])
                    assert step.n == n_c

    @block.scalar
    def _(act):
        act.sem_inc(q_ev, PRIME)
        act.sem_inc(s_exp, PRIME)
        act.sem_inc(pj_act, 2 * PRIME)
        act.sem_inc(gelu_done, PRIME)
        act.sem_inc(sc_ev, PRIME)
        act.sem_inc(g_ev, 4)
        for s in range(2):
            act.sem_inc(s_gst[s], 16)
            act.sem_inc(s_hst[s], 16)
        act.wait_ge(eps_set, 1)
        with act.Fori(0, L) as l:

            def round_chunks(u):
                for c in range(DC):
                    act.wait_ge(tr_ps, DC * (3 * l + u) + c + 1)
                    nc.scalar.copy(t_hi[:, c], ps[:, c]).then_inc(tr_hi, 1)

            def round_group(n, s, size):
                act.wait_ge(s_wraw[s], 16 * (W_PER // 2 * l + (n - s) // 2 + 1))
                act.wait_ge(pj_ps, TB * (W_PER * l + n + 1))
                nc.scalar.copy(w_hi[:, s, 0:size], w_raw[:, s, 0:size]).then_inc(wc_hi, 1)

            def keep_h(n, s):
                for tb in range(TB // 2):
                    act.wait_ge(pj_ps, (W_PER * l + n) * TB + tb + 1 + PRIME * TB)
                    nc.scalar.copy(h[:, tb, ds(n * IN_N, IN_N)], ps[:, TB * s + tb, 0:IN_N]).then_inc(pj_act, 1)

            round_chunks(0)
            round_group(0, 0, DC * IN_N)
            with act.Fori(0, IN_G // 2 - 1) as i:
                round_group(2 * i + 1, 1, DC * IN_N)
                keep_h(2 * i, 0)
                round_group(2 * i + 2, 0, DC * IN_N)
                keep_h(2 * i + 1, 1)
            round_group(IN_G - 1, 1, DC * IN_N)
            keep_h(IN_G - 2, 0)
            keep_h(IN_G - 1, 1)
            act.wait_ge(lat_ss, l + 1)
            nc.scalar.activation(lat_rms[:, 0], lat_sq[:, 0], ACT.Sqrt, bias=eps[:], scale=1.0 / QR)
            nc.scalar.activation(lat_rms[:, 1], lat_sq[:, 1], ACT.Sqrt, bias=eps[:], scale=1.0 / KVR).then_inc(lat_sd, 1)
            act.wait_ge(s_lay, 16 * 9 * (l + 1))
            for k in range(3):
                act.wait_ge(lat_tr, 3 * l + k + 1)
                nc.scalar.activation(lat_t[:, k], ps[:, k], ACT.Copy, scale=g_lat[:, k:k + 1]).then_inc(lat_ev, 1)
            for tb in range(TB):
                bank = 4 * ((tb + 1) % 2)
                act.wait_ge(lat_ps, 2 * TB * l + 2 * tb + 1)
                nc.scalar.copy(q_b[:, tb].rearrange("p (k f) -> p k f", k=2),
                               ps[:, bank:bank + 2, 0:UQ_W // 2]).then_inc(lat_qev, 1)
            act.wait_ge(lam_s, l + 1)
            nc.scalar.activation(lam_exp[:], lam_dot[:], ACT.Exp).then_inc(lam_e, 1)

            def scale_q(j, s):
                act.wait_ge(qk_tr, JOBS * l + j + 1 + PRIME)
                nc.scalar.activation(q_t[0:DK, s], ps[0:DK, 4], ACT.Copy, scale=sc_s[0:DK, s:s + 1]).then_inc(q_ev, 1)

            def exponent(j, s, qb):
                n = TB * j + qb
                act.wait_ge(s_min, MAPS * l + n + 1 + PRIME)
                act.wait_ge(pt_ps, MAPS * l + n + 1)
                nc.scalar.activation(probs[:, qb % 2], masked[:, qb % 2], ACT.Exp, bias=neg_max[:, qb % 2:qb % 2 + 1],
                                     scale=-1.0, accum_out=row_sum[:, s, qb:qb + 1]).then_inc(s_exp, 1)

            def keep_pt(j, qb):
                act.wait_ge(pt_ps, MAPS * l + TB * j + qb + 1 + PRIME)
                nc.scalar.copy(p_t[:, qb % 2].rearrange("p k q -> p (k q)"), ps[:, 2 + qb % 2]).then_inc(pt_act, 1)

            def job(j, s, ahead):
                exponent(j, s, 2)
                if ahead:
                    scale_q(j + 1, 1 - s)
                exponent(j, s, 3)
                if ahead:
                    exponent(j + 1, 1 - s, 0)
                    exponent(j + 1, 1 - s, 1)
                keep_pt(j, 3)

            scale_q(0, 0)
            exponent(0, 0, 0)
            exponent(0, 0, 1)
            with act.Fori(0, JOBS // 2 - 1) as i:
                job(2 * i, 0, True)
                job(2 * i + 1, 1, True)
            job(JOBS - 2, 0, True)
            job(JOBS - 1, 1, False)
            act.wait_ge(sub_ss, l + 1)
            nc.scalar.activation(sub_rms[:], sub_sq[:], ACT.Sqrt, bias=eps[:], scale=1.0 / ADV).then_inc(sub_sd, 1)
            round_chunks(1)
            for k in range(O_G):
                round_group(IN_G + k, k % 2, DC * O_N)

            def deviation(u):
                act.wait_ge(ln_var, 2 * l + u + 1)
                nc.scalar.activation(ln_dev[:], mean_var[:, :, 1], ACT.Sqrt, bias=eps[:]).then_inc(ln_sd, 1)

            deviation(0)
            act.wait_ge(s_keys, 16 * (l + 1))
            nc.scalar.copy(k_hi[:], keys[:]).then_inc(keys_hi, 1)
            round_chunks(2)

            def round_block(m, s):
                act.wait_ge(s_straw[s], (ST_PER // 2 * l + m + 1) * 16)
                act.wait_ge(st_used, ST_PER * l + 2 * m + s + 1)
                nc.scalar.copy(st_hi[:, s].rearrange("p c f -> p (c f)"), st_raw[:, s]).then_inc(st_h, 1)

            def round_query(f, s):
                act.wait_ge(st_used, ST_PER * l + f + 1 + PRIME)
                nc.scalar.copy(pq_hi[:, s], ps[:, s]).then_inc(pq_h, 1)

            def keep_scores(f, s):
                act.wait_ge(sc_ps, QB * l + f + 1)
                dst = scores[:].rearrange("p (t h) k n -> p t (h k) n", t=TB)[:, :, ds(f, 1), :]
                nc.scalar.copy(dst, ps[:, 2 + s].rearrange("p (t o n) -> p t o n", t=TB, o=1)).then_inc(sc_ev, 1)

            def gelu(m, s):
                b = 2 * m + s
                act.wait_ge(st_used, ST_PER * l + QB + b + 1 + PRIME)
                act.wait_ge(s_hst[s], (EB // 2 * l + m + 1) * 16)
                nc.scalar.activation(h_out[:, s], ps[:, s], ACT.Gelu).then_inc(gelu_done, 1)

            round_block(0, 0)
            with act.Fori(0, QB // 2) as i:
                round_block(i, 1)
                round_query(2 * i, 0)
                round_block(i + 1, 0)
                round_query(2 * i + 1, 1)
                keep_scores(2 * i, 0)
                keep_scores(2 * i + 1, 1)
            with act.Fori(0, UNITS) as i:
                round_block(i + QB // 2, 1)
                gelu(i, 0)
                round_block(i + QB // 2 + 1, 0)
                gelu(i, 1)
            act.wait_ge(gate_sub, l + 1)
            nc.scalar.activation(e_all[:], c_all[:], ACT.Exp).then_inc(gate_exp, 1)
            for k in range(2):
                act.wait_ge(sel_tr, 3 * l + k + 1)
                nc.scalar.copy(i_t[:, k], ps[:, 5 + k]).then_inc(sel_act, 1)
            act.wait_ge(sel_tr, 3 * l + 3)
            nc.scalar.copy(g_hi[:], ps[:, 7]).then_inc(sel_act, 1)

            def keep_gates(sw, q, body):
                for g in range(BODY_T // 4):
                    act.wait_ge(g_tok, T * l + BODY_T * body + 4 * (g + 1) + OH)
                    nc.scalar.copy(g_stage[:, sw, :, ds(q * BODY_T + 4 * g, 4)],
                                   ps[:, 2 + g].rearrange("p (t n) -> p n t", t=4)).then_inc(g_ev, 1)

            def spread(w2, sw, q, last=False):
                body = (2 * w2 + sw) * BODIES + q
                m = body + UNITS
                round_block(m + QB // 2, 1)
                gelu(m, 0)
                if not last:
                    round_block(m + QB // 2 + 1, 0)
                gelu(m, 1)
                keep_gates(sw, q, body)

            def store_window(w2, sw):
                w = 2 * w2 + sw
                act.wait_ge(g_ev, T // 4 * l + WIN_T // 4 * (w + 1) + 4)
                act.dma_start(gates_d[:, :, ds(w * WIN_T, WIN_T)].rearrange("n p t -> p n t"),
                              g_stage[:, sw]).then_inc(s_gst[sw], 16)

            with act.Fori(0, WIN // 2 - 1) as w2:
                for sw in range(2):
                    act.wait_ge(s_gst[sw], (WIN // 2 * l + w2 + 1) * 16)
                    with act.Fori(0, BODIES) as q:
                        spread(w2, sw, q)
                    store_window(w2, sw)
            for sw in range(2):
                w2 = WIN // 2 - 1
                act.wait_ge(s_gst[sw], (WIN // 2 * l + w2 + 1) * 16)
                with act.Fori(0, BODIES - sw) as q:
                    spread(w2, sw, q)
                if sw:
                    spread(w2, sw, BODIES - 1, last=True)
                store_window(w2, sw)
            with act.Fori(0, EB // 2) as i:
                for s in range(2):
                    b = 2 * i + s
                    act.wait_ge(s_vraw[s], (EB // 2 * l + i + 1) * 16)
                    act.wait_ge(v_used, EB * l + b + 1)
                    nc.scalar.copy(v_hi[:, s], v_raw[:, s]).then_inc(v_h, 1)
                    act.wait_ge(wt_f, EB * l + b + 1 + PRIME)
                    nc.scalar.copy(wt_hi[:, s], w_f[:, s]).then_inc(wt_h, 1)
            deviation(1)

    @block.vector
    def _(dve):
        step = Steps(dve, dve_step)
        dve.sem_inc(wc_lo, PRIME)
        dve.sem_inc(pj_dve, 2 * PRIME)
        dve.sem_inc(k_ev, PRIME)
        dve.sem_inc(s_min, PRIME)
        dve.sem_inc(o_ev, PRIME)
        dve.sem_inc(st_l, PRIME)
        dve.sem_inc(v_l, PRIME)
        dve.sem_inc(wt_f, PRIME)
        dve.sem_inc(ln_done, PRIME)
        nc.vector.memset(eps[:], LN_EPS).then_inc(eps_set, 1)
        nc.vector.memset(zeros[:], 0.0).then_inc(eps_set, 1)
        n_pre, n_sub, n_ln, n_unit, n_gate = 4, 4, 2 + TB, 25, 4
        per = n_pre + JOBS + n_sub + 2 * n_ln + 1 + UNITS * n_unit + n_gate
        with dve.Fori(0, L) as l:
            at = per * l

            def rest_chunks(u):
                for c in range(DC):
                    dve.wait_ge(tr_hi, DC * (3 * l + u) + c + 1)
                    nc.vector.tensor_tensor(t_lo[:, c], ps[:, c], t_hi[:, c].bitcast(F32),
                                            ALU.subtract).then_inc(tr_lo, 1)

            def rest_group(n, s, size):
                dve.wait_ge(wc_hi, W_PER * l + n + 1)
                nc.vector.tensor_tensor(w_lo[:, s, 0:size], w_raw[:, s, 0:size], w_hi[:, s, 0:size].bitcast(F32),
                                        ALU.subtract).then_inc(wc_lo, 1)

            def keep_h(n, s):
                for tb in range(TB // 2, TB):
                    dve.wait_ge(pj_ps, (W_PER * l + n) * TB + tb + 1 + PRIME * TB)
                    nc.vector.tensor_copy(h[:, tb, ds(n * IN_N, IN_N)], ps[:, TB * s + tb, 0:IN_N]).then_inc(pj_dve, 1)

            rest_chunks(0)
            rest_group(0, 0, DC * IN_N)
            with dve.Fori(0, IN_G // 2 - 1) as i:
                rest_group(2 * i + 1, 1, DC * IN_N)
                keep_h(2 * i, 0)
                rest_group(2 * i + 2, 0, DC * IN_N)
                keep_h(2 * i + 1, 1)
            rest_group(IN_G - 1, 1, DC * IN_N)
            keep_h(IN_G - 2, 0)
            keep_h(IN_G - 1, 1)
            step.at(at)
            dve.wait_ge(s_lay, 16 * 9 * (l + 1))
            for k in range(2):
                ins = nc.vector.tensor_tensor_reduce(out=lam_in[:, 2 * k], in0=lam_in[:, 2 * k],
                                                     in1=lam_in[:, 2 * k + 1], scale=1.0, scalar=0.0, op0=ALU.mult,
                                                     op1=ALU.add, accum_out=lam_dot[:, k:k + 1])
            ins.then_inc(lam_s, 1)
            step.done(nc.vector.tensor_scalar(sub_g[:], sub_g[:], lam_c[:, 1:2], None, ALU.mult))
            dve.wait_ge(pj_act, IN_G * 2 * (l + 1) + 2 * PRIME)
            dve.wait_ge(pj_dve, IN_G * 2 * (l + 1) + 2 * PRIME)
            for tb in range(TB):
                for k, (c0, w) in enumerate(((COL_CQ, QR), (COL_CKV, KVR))):
                    src = h[:, tb, c0:c0 + w]
                    ins = nc.vector.tensor_tensor_reduce(out=lat_n[:, tb, k * QR:k * QR + w], in0=src, in1=src,
                                                         scale=1.0, scalar=0.0, op0=ALU.mult, op1=ALU.add,
                                                         accum_out=lat_sq[:, k, tb:tb + 1])
            ins.then_inc(lat_ss, 1)
            dve.wait_ge(lat_sd, l + 1)
            step.done(nc.vector.reciprocal(lat_inv[:], lat_rms[:]))
            step.wait()
            for tb in range(TB):
                for k, (c0, w) in enumerate(((COL_CQ, QR), (COL_CKV, KVR))):
                    ins = nc.vector.tensor_scalar(lat_n[:, tb, k * QR:k * QR + w], h[:, tb, c0:c0 + w],
                                                  lat_inv[:, k, tb:tb + 1], None, ALU.mult)
            ins.then_inc(lat_ready, 1)
            for tb in range(TB):
                bank = 4 * ((tb + 1) % 2) + 2
                dve.wait_ge(lat_ps, 2 * TB * l + 2 * tb + 2)
                nc.vector.tensor_copy(kv_b[:, tb].rearrange("p (k f) -> p k f", k=2),
                                      ps[:, bank:bank + 2, 0:UKV_W // 2]).then_inc(lat_kev, 1)
            dve.wait_ge(lam_e, l + 1)
            step.done(nc.vector.tensor_tensor(lam_neg[:, 0:1], lam_exp[:, 1:2], lam_exp[:, 0:1], ALU.subtract))
            step.wait()
            step.done(nc.vector.tensor_scalar(lam_neg[:, 1:2], lam_neg[:, 0:1], lam_c[:, 0:1], None, ALU.add))
            assert step.n == n_pre
            at = at + n_pre

            def keep_k(j, s):
                dve.wait_ge(qk_tr, JOBS * l + j + 1 + PRIME)
                nc.vector.tensor_copy(k_t[0:DK, s], ps[0:DK, 5]).then_inc(k_ev, 1)

            def score(j, qb, dilated):
                n = TB * j + qb
                table = mask[:, (TB - 1 - qb) * P:(TB - 1 - qb) * P + T] if dilated else zeros[:]
                dve.wait_ge(s_exp, MAPS * l + n + 1)
                dve.wait_ge(s_ps, MAPS * l + n + 1)
                dve.sem_inc(waited, 1)
                nc.vector.tensor_tensor_reduce(out=masked[:, qb % 2], in0=ps[:, qb % 2], in1=table, scale=1.0,
                                               scalar=-NEG, op0=ALU.add, op1=ALU.min,
                                               accum_out=neg_max[:, qb % 2:qb % 2 + 1]).then_inc(s_min, 1)

            def keep_pt(j, qb):
                dve.wait_ge(pt_ps, MAPS * l + TB * j + qb + 1 + PRIME)
                nc.vector.tensor_copy(p_t[:, qb % 2].rearrange("p k q -> p (k q)"),
                                      ps[:, 2 + qb % 2]).then_inc(pt_dve, 1)

            def job(j, s, kind, ahead):
                score(j, 2, kind)
                keep_pt(j, 0)
                if ahead is not None:
                    keep_k(j + 1, 1 - s)
                score(j, 3, kind)
                keep_pt(j, 1)
                if ahead is not None:
                    score(j + 1, 0, ahead)
                keep_pt(j, 2)
                if ahead is not None:
                    score(j + 1, 1, ahead)
                step.at(at + j)
                dve.wait_ge(s_exp, MAPS * l + TB * j + TB + PRIME)
                step.done(nc.vector.reciprocal(row_inv[:, s], row_sum[:, s]))
                step.wait()
                dve.wait_ge(pv_done, JOBS * l + j + 1 + PRIME)
                nc.vector.tensor_tensor(o_all[:, :, ds(j * VD, VD)],
                                        ps[:, 6 + s, 0:TB * VD].rearrange("p (t d) -> p t d", t=TB),
                                        row_inv[:, s].unsqueeze(2).to_broadcast([P, TB, VD]),
                                        ALU.mult).then_inc(o_ev, 1)

            plain = JA + JB
            keep_k(0, 0)
            score(0, 0, False)
            score(0, 1, False)
            with dve.Fori(0, plain // 2 - 1) as i:
                job(2 * i, 0, False, False)
                job(2 * i + 1, 1, False, False)
            job(plain - 2, 0, False, False)
            job(plain - 1, 1, False, True)
            with dve.Fori(plain // 2, JOBS // 2 - 1) as i:
                job(2 * i, 0, True, True)
                job(2 * i + 1, 1, True, True)
            job(JOBS - 2, 0, True, True)
            job(JOBS - 1, 1, True, None)
            at = at + JOBS
            step.at(at)
            dve.wait_ge(o_ev, JOBS * (l + 1) + PRIME)
            dve.wait_ge(k_ev, JOBS * (l + 1) + PRIME)
            dve.wait_ge(s_ps, MAPS * (l + 1))
            for tb in range(TB):
                pair = o_all[:, tb, 0:JA * VD].rearrange("p (h k d) -> p h k d", h=AH, k=2)
                last = nc.vector.scalar_tensor_tensor(out=o_f[:, tb], in0=pair[:, :, 1], scalar=lam_neg[:, 1:2],
                                                      in1=pair[:, :, 0], op0=ALU.mult, op1=ALU.add)
            step.done(last)
            step.wait()
            step.done(nc.vector.tensor_tensor(o_q, o_f, o_f, ALU.mult))
            step.wait()
            nc.vector.tensor_reduce(sub_sq[:], o_q.rearrange("p t h d -> p (t h) d"), AX_X, ALU.add).then_inc(sub_ss, 1)
            dve.wait_ge(sub_sd, l + 1)
            step.done(nc.vector.reciprocal(sub_inv[:], sub_rms[:]))
            step.wait()
            step.done(nc.vector.tensor_tensor(
                o_f.rearrange("p t h d -> p (t h) d"), o_f.rearrange("p t h d -> p (t h) d"),
                sub_inv[:].unsqueeze(2).to_broadcast([P, TB * AH, ADV]), ALU.mult))
            step.wait()
            nc.vector.tensor_tensor(o_all[:, :, A_W:2 * A_W].rearrange("p t (h d) -> p t h d", h=AH), o_f,
                                    sub_g[:].unsqueeze(1).unsqueeze(1).to_broadcast([P, TB, AH, ADV]),
                                    ALU.mult).then_inc(mix_ready, 1)
            assert step.n == n_sub
            at = at + n_sub
            rest_chunks(1)
            rest_group(IN_G, 0, DC * O_N)
            for k in range(O_G):
                if k + 1 < O_G:
                    rest_group(IN_G + k + 1, (k + 1) % 2, DC * O_N)
                for tb in range(TB):
                    dve.wait_ge(pj_ps, (W_PER * l + IN_G + k) * TB + tb + 1 + PRIME * TB)
                    xs = x_tok[:, tb, k * O_N:(k + 1) * O_N]
                    nc.vector.scalar_tensor_tensor(out=xs, in0=xs, scalar=ALPHA, in1=ps[:, TB * (k % 2) + tb, 0:O_N],
                                                   op0=ALU.mult, op1=ALU.add).then_inc(pj_res, 1)

            def layer_norm(u, at):
                step.at(at)
                for tb in range(TB):
                    for k in range(2):
                        last = nc.vector.bn_stats(bn[:, tb, k], x_tok[:, tb, k * 512:(k + 1) * 512])
                step.done(last)
                step.wait_apart(waited)
                for tb in range(TB):
                    last = nc.vector.bn_aggr(mean_var[:, tb], bn[:, tb])
                last.then_inc(ln_var, 1)
                dve.wait_ge(ln_sd, 2 * l + u + 1)
                step.done(nc.vector.reciprocal(ln_inv[:], ln_dev[:]))
                step.wait()
                dve.wait_ge(s_ln, 16 * (2 * l + u + 1))
                for tb in range(TB):
                    xs = x_tok[:, tb]
                    step.done(nc.vector.scalar_tensor_tensor(out=xs, in0=xs, scalar=mean_var[:, tb, 0:1],
                                                             in1=ln_rows[:, 0], op0=ALU.subtract, op1=ALU.mult))
                for tb in range(TB):
                    xs = x_tok[:, tb]
                    if tb == 0:
                        step.wait()
                    nc.vector.scalar_tensor_tensor(out=xs, in0=xs, scalar=ln_inv[:, tb:tb + 1], in1=ln_rows[:, 1],
                                                   op0=ALU.mult, op1=ALU.add).then_inc(ln_done, 1)
                assert step.n == n_ln

            dve.wait_ge(pj_res, O_G * TB * (l + 1))
            layer_norm(0, at)
            at = at + n_ln
            dve.wait_ge(keys_hi, l + 1)
            nc.vector.tensor_tensor(k_lo[:], keys[:], k_hi[:].bitcast(F32), ALU.subtract).then_inc(keys_lo, 1)
            rest_chunks(2)

            def rest_block(n, s):
                dve.wait_ge(st_h, ST_PER * l + n + 1)
                nc.vector.tensor_tensor(st_lo[:, s].rearrange("p c f -> p (c f)"), st_raw[:, s],
                                        st_hi[:, s].rearrange("p c f -> p (c f)").bitcast(F32),
                                        ALU.subtract).then_inc(st_l, 1)

            def rest_query(f, s):
                dve.wait_ge(pq_h, QB * l + f + 1)
                nc.vector.tensor_tensor(pq_lo[:, s], ps[:, s], pq_hi[:, s].bitcast(F32), ALU.subtract).then_inc(pq_l, 1)

            step.at(at)
            step.done(nc.vector.tensor_copy(opt16[:].rearrange("p a b c -> p (a b) c"),
                                            iota[:, 0:TOPK].unsqueeze(1).to_broadcast([P, 2 * TOPK, TOPK])))
            at = at + 1
            rest_block(0, 0)
            with dve.Fori(0, QB // 2) as i:
                rest_block(2 * i + 1, 1)
                rest_query(2 * i, 0)
                rest_block(2 * i + 2, 0)
                rest_query(2 * i + 1, 1)
            dve.wait_ge(sc_ev, QB * (l + 1) + PRIME)
            dve.sem_inc(waited, 1)

            def top16(values, spare, src, idx):
                step.done(nc.vector.max(values[:, 0:8], src))
                step.wait_apart(waited)
                step.done(nc.vector.max_index(idx[:, 0:8], values[:, 0:8], src))
                step.done(nc.vector.match_replace(spare, values[:, 0:8], src, NEG))
                step.wait_apart(waited)
                step.done(nc.vector.max(values[:, 8:16], spare))
                step.wait_apart(waited)
                step.done(nc.vector.max_index(idx[:, 8:16], values[:, 8:16], spare))

            with dve.Fori(0, UNITS) as i:
                n = 2 * i + QB
                rest_block(n + 1, 1)
                step.at(at + n_unit * i)
                step.done(nc.vector.tensor_copy(wk[:].rearrange("p a b -> p (a b)"),
                                                scores[:, ds(i, 1)].rearrange("p u a b -> p (u a b)")))
                step.wait_apart(waited)
                for k in range(2):
                    top16(v16[:, k], wk2[:, k], wk[:, k], x16[:, k])
                step.wait()
                step.done(nc.vector.tensor_copy(x16f[:].rearrange("p a b -> p (a b)"),
                                                x16[:].rearrange("p a b -> p (a b)")))
                step.done(nc.vector.tensor_tensor(cand[:], v16[:, 0].unsqueeze(2).to_broadcast([P, TOPK, TOPK]),
                                                  v16[:, 1].unsqueeze(1).to_broadcast([P, TOPK, TOPK]), ALU.add))
                rest_block(n + 2, 0)
                step.wait_apart(waited)
                top16(c16, cand2[:], cand[:].rearrange("p a b -> p (a b)"), ci)
                step.wait()
                step.done(nc.vector.tensor_scalar(cab[:, 0], ci[:], 4, None, ALU.logical_shift_right))
                step.done(nc.vector.tensor_scalar(cab[:, 1], ci[:], TOPK - 1, None, ALU.bitwise_and))
                step.done(nc.vector.tensor_copy(c_all[:, ds(i, 1)], c16[:].unsqueeze(1)))
                step.wait()
                step.done(nc.vector.tensor_copy(cabf[:].rearrange("p a b -> p (a b)"),
                                                cab[:].rearrange("p a b -> p (a b)")))
                step.wait()
                ab = "p a b c -> p (a b) c"
                step.done(nc.vector.tensor_tensor(
                    eq[:].rearrange(ab), opt16[:].rearrange(ab),
                    cabf[:].rearrange("p a b -> p (a b)").unsqueeze(2).to_broadcast([P, 2 * TOPK, TOPK]),
                    ALU.is_equal))
                step.wait()
                step.done(nc.vector.tensor_tensor(
                    eq[:], eq[:], x16f[:].unsqueeze(2).to_broadcast([P, 2, TOPK, TOPK]), ALU.mult))
                step.wait()
                step.done(nc.vector.tensor_reduce(i_all[:, :, ds(i * TOPK, TOPK)], eq[:], AX_X, ALU.add))
                step.wait()
                assert step.n == n_unit
            at = at + n_unit * UNITS
            step.at(at)
            step.done(nc.vector.tensor_copy(c_top[:].unsqueeze(2), c_all[:, :, 0:1]))
            step.wait()
            nc.vector.tensor_tensor(c_all[:], c_all[:], c_top[:].unsqueeze(2).to_broadcast([P, UNITS, TOPK]),
                                    ALU.subtract).then_inc(gate_sub, 1)
            dve.wait_ge(gate_exp, l + 1)
            step.done(nc.vector.tensor_reduce(z_all[:, 0], e_all[:], AX_X, ALU.add))
            step.wait()
            step.done(nc.vector.reciprocal(z_all[:, 1], z_all[:, 0]))
            step.wait()
            nc.vector.tensor_tensor(e_all[:], e_all[:], z_all[:, 1].unsqueeze(2).to_broadcast([P, UNITS, TOPK]),
                                    ALU.mult).then_inc(gate_ready, 1)
            dve.wait_ge(sel_act, 3 * (l + 1))
            step.done(nc.vector.tensor_tensor(g_lo[:], ps[:, 7], g_hi[:].bitcast(F32), ALU.subtract))
            step.wait_apart(waited)
            assert step.n == n_gate
            at = at + n_gate

            def spread(w2, sw, q, last=False):
                body = (2 * w2 + sw) * BODIES + q
                n = 2 * (body + UNITS) + QB
                for half in range(2):
                    if half == 0:
                        rest_block(n + 1, 1)
                    elif not last:
                        rest_block(n + 2, 0)
                    for k in range(BODY_T // 2):
                        t = body * BODY_T + half * (BODY_T // 2) + k
                        dve.wait_ge(g_tok, T * l + t + 1)
                        nc.vector.tensor_scalar(oh[:, k, 0], iota[:], i_t[:, 1, ds(t, 1)], None, ALU.is_equal)
                        nc.vector.tensor_scalar(oh[:, k, 1], iota[:], i_t[:, 0, ds(t, 1)],
                                                g_hi[:, ds(t, 1)].bitcast(F32), ALU.is_equal, ALU.mult)
                        nc.vector.tensor_scalar(oh[:, k, 2], iota[:], i_t[:, 0, ds(t, 1)],
                                                g_lo[:, ds(t, 1)].bitcast(F32), ALU.is_equal,
                                                ALU.mult).then_inc(oh_ready, 1)

            with dve.Fori(0, WIN // 2 - 1) as w2:
                for sw in range(2):
                    with dve.Fori(0, BODIES) as q:
                        spread(w2, sw, q)
            for sw in range(2):
                with dve.Fori(0, BODIES - sw) as q:
                    spread(WIN // 2 - 1, sw, q)
            spread(WIN // 2 - 1, 1, BODIES - 1, last=True)
            with dve.Fori(0, EB // 2) as i:
                for s in range(2):
                    b = 2 * i + s
                    dve.wait_ge(s_gh[s], (EB // 2 * l + i + 1) * 32)
                    nc.vector.tensor_tensor(w_f[:, s], g_in[:, s], h_in[:, s], ALU.mult).then_inc(wt_f, 1)
                    dve.wait_ge(v_h, EB * l + b + 1)
                    nc.vector.tensor_tensor(v_lo[:, s], v_raw[:, s], v_hi[:, s].bitcast(F32),
                                            ALU.subtract).then_inc(v_l, 1)
                    dve.wait_ge(wt_h, EB * l + b + 1)
                    nc.vector.tensor_tensor(wt_lo[:, s], w_f[:, s], wt_hi[:, s].bitcast(F32),
                                            ALU.subtract).then_inc(wt_l, 1)
            dve.wait_ge(v_used, EB * (l + 1) + PRIME)
            for tb in range(TB):
                xs = x_tok[:, tb]
                last = nc.vector.scalar_tensor_tensor(
                    out=xs, in0=xs, scalar=ALPHA, in1=ps[:, 2 * tb:2 * tb + 2].rearrange("p b n -> p (b n)"),
                    op0=ALU.mult, op1=ALU.add)
            last.then_inc(ffn_done, 1)
            dve.wait_ge(ffn_done, l + 1)
            layer_norm(1, at)

    @block.tensor
    def _(pe):
        pe.sem_inc(pj_ps, PRIME * TB)
        pe.sem_inc(qk_tr, PRIME)
        pe.sem_inc(pt_ps, PRIME)
        pe.sem_inc(pv_done, PRIME)
        pe.sem_inc(st_used, PRIME)
        pe.sem_inc(v_used, PRIME)
        pe.sem_inc(g_tok, OH)
        pe.wait_ge(s_x, 3 * 16)
        pe.wait_ge(eps_set, 2)

        def product(dst, lhs, rhs, first, last):
            nc.tensor.matmul(dst, lhs[0], rhs[0], start=first, stop=False)
            nc.tensor.matmul(dst, lhs[0], rhs[1], start=False, stop=False)
            return nc.tensor.matmul(dst, lhs[1], rhs[0], start=False, stop=last)

        with pe.Fori(0, L) as l:

            def turn(src):
                for c in range(DC):
                    for tb in range(TB):
                        last = nc.tensor.transpose(ps[:, c, tb * P:(tb + 1) * P], src[:, tb, c * P:(c + 1) * P],
                                                   ident[:])
                    last.then_inc(tr_ps, 1)

            def group(n, s, width):
                pe.wait_ge(wc_lo, W_PER * l + n + 1 + PRIME)
                for tb in range(TB):
                    rows = slice(tb * P, (tb + 1) * P)
                    for c in range(DC):
                        cols = slice(c * width, (c + 1) * width)
                        last = product(ps[:, TB * s + tb, 0:width], (t_hi[:, c, rows], t_lo[:, c, rows]),
                                       (w_hi[:, s, cols], w_lo[:, s, cols]), c == 0, c == DC - 1)
                    last.then_inc(pj_ps, 1)

            pe.wait_ge(ln_done, 2 * TB * l + PRIME)
            turn(x_tok)
            pe.wait_ge(tr_lo, DC * 3 * l + DC)
            pe.sem_inc(waited, 1)
            with pe.Fori(0, IN_G // 2) as i:
                for s in range(2):
                    n = 2 * i + s
                    pe.wait_ge(pj_act, 2 * (IN_G * l + n + 1))
                    pe.wait_ge(pj_dve, 2 * (IN_G * l + n + 1))
                    group(n, s, IN_N)
            pe.wait_ge(lat_ready, l + 1)
            for k in range(3):
                for tb in range(TB):
                    last = nc.tensor.transpose(ps[:, k, tb * P:(tb + 1) * P], lat_n[:, tb, k * P:(k + 1) * P], ident[:])
                last.then_inc(lat_tr, 1)
            pe.wait_ge(s_lay, 16 * 9 * (l + 1))
            pe.wait_ge(lat_ev, 3 * (l + 1))
            for tb in range(TB):
                bank = 4 * ((tb + 1) % 2)
                rows = slice(tb * P, (tb + 1) * P)
                if tb >= 2:
                    pe.wait_ge(lat_qev, TB * l + tb - 1)
                    pe.wait_ge(lat_kev, TB * l + tb - 1)
                w = UQ_W // 2
                for half in range(2):
                    for k in range(2):
                        last = nc.tensor.matmul(ps[:, bank + half, 0:w], lat_t[:, k, rows],
                                                w_uq[:, k, half * w:(half + 1) * w], start=k == 0, stop=k == 1)
                last.then_inc(lat_ps, 1)
                w = UKV_W // 2
                for half in range(2):
                    last = nc.tensor.matmul(ps[:, bank + 2 + half, 0:w], lat_t[:, 2, rows],
                                            w_ukv[:, half * w:(half + 1) * w], start=True, stop=True)
                last.then_inc(lat_ps, 1)
            pe.wait_ge(lat_qev, TB * (l + 1))
            pe.wait_ge(lat_kev, TB * (l + 1))

            def turn_qk(j, s):
                pe.wait_ge(rope_done, JOBS * l + j + 1)
                for k in range(2):
                    for tb in range(TB):
                        last = nc.tensor.transpose(ps[0:DK, 4 + k, tb * P:(tb + 1) * P], rq[:, s, tb, k], ident[:])
                last.then_inc(qk_tr, 1)

            def score(j, s, qb):
                if qb == 0:
                    pe.wait_ge(q_ev, JOBS * l + j + 1 + PRIME)
                    pe.wait_ge(k_ev, JOBS * l + j + 1 + PRIME)
                pe.wait_ge(s_min, MAPS * l + TB * j + qb + 1)
                nc.tensor.matmul(ps[:, qb % 2], q_t[0:DK, s, qb * P:(qb + 1) * P], k_t[0:DK, s], start=True,
                                 stop=True).then_inc(s_ps, 1)

            def turn_p(j, qb):
                pe.wait_ge(s_exp, MAPS * l + TB * j + qb + 1 + PRIME)
                for k in range(TB):
                    last = nc.tensor.transpose(ps[:, 2 + qb % 2, k * P:(k + 1) * P],
                                               probs[:, qb % 2, k * P:(k + 1) * P], ident[:])
                last.then_inc(pt_ps, 1)

            def values(j, s, qb):
                if qb == 0:
                    pe.wait_ge(o_ev, JOBS * l + j + 1)
                if qb < 3:
                    pe.wait_ge(pt_dve, 3 * (JOBS * l + j) + qb + 1)
                else:
                    pe.wait_ge(pt_act, JOBS * l + j + 1)
                for k in range(TB):
                    last = nc.tensor.matmul(ps[:, 6 + s, qb * VD:(qb + 1) * VD], p_t[:, qb % 2, k], v_s[:, s, k],
                                            start=k == 0, stop=k == TB - 1)
                if qb == TB - 1:
                    last.then_inc(pv_done, 1)

            def job(j, s, ahead):
                score(j, s, 2)
                turn_p(j, 0)
                if ahead:
                    turn_qk(j + 1, 1 - s)
                score(j, s, 3)
                turn_p(j, 1)
                values(j, s, 0)
                if ahead:
                    score(j + 1, 1 - s, 0)
                turn_p(j, 2)
                values(j, s, 1)
                if ahead:
                    score(j + 1, 1 - s, 1)
                turn_p(j, 3)
                values(j, s, 2)
                values(j, s, 3)

            turn_qk(0, 0)
            score(0, 0, 0)
            score(0, 0, 1)
            with pe.Fori(0, JOBS // 2 - 1) as i:
                job(2 * i, 0, True)
                job(2 * i + 1, 1, True)
            job(JOBS - 2, 0, True)
            job(JOBS - 1, 1, False)
            pe.wait_ge(mix_ready, l + 1)
            turn(o_all[:, :, A_W:A_W + D])
            pe.wait_ge(tr_lo, DC * 3 * l + 2 * DC)
            for k in range(O_G):
                if k >= 2:
                    pe.wait_ge(pj_res, TB * (O_G * l + k - 1))
                group(IN_G + k, k % 2, O_N)
            pe.wait_ge(ln_done, 2 * TB * l + TB + PRIME)
            turn(x_tok)
            pe.wait_ge(tr_lo, DC * 3 * l + 3 * DC)
            pe.wait_ge(keys_lo, l + 1)
            pe.sem_inc(waited, 1)

            def stationary(n, s, dst):
                pe.wait_ge(st_l, ST_PER * l + n + 1 + PRIME)
                for c in range(DC):
                    last = product(dst, (st_hi[:, s, c], st_lo[:, s, c]), (t_hi[:, c], t_lo[:, c]), c == 0,
                                   c == DC - 1)
                last.then_inc(st_used, 1)

            def key_scores(f, s):
                pe.wait_ge(pq_l, QB * l + f + 1)
                pe.wait_ge(sc_ev, QB * l + f + 1)
                for tb in range(TB):
                    rows = slice(tb * P, (tb + 1) * P)
                    last = product(ps[:, 2 + s, tb * NK:(tb + 1) * NK], (pq_hi[:, s, rows], pq_lo[:, s, rows]),
                                   (k_hi[:, ds(f, 1)].rearrange("p o n -> p (o n)"),
                                    k_lo[:, ds(f, 1)].rearrange("p o n -> p (o n)")), True, True)
                last.then_inc(sc_ps, 1)

            with pe.Fori(0, QB // 2) as i:
                for s in range(2):
                    stationary(2 * i + s, s, ps[:, s])
                for s in range(2):
                    key_scores(2 * i + s, s)

            def experts(m, s):
                pe.wait_ge(gelu_done, EB * l + 2 * m + s + 1)
                stationary(2 * m + s + QB, s, ps[:, s])

            with pe.Fori(0, UNITS) as i:
                for s in range(2):
                    experts(i, s)
            pe.wait_ge(gate_ready, l + 1)
            for k in range(3):
                src = e_all[:].rearrange("p u k -> p (u k)") if k == 2 else i_all[:, k]
                for tb in range(TB):
                    last = nc.tensor.transpose(ps[:, 5 + k, tb * P:(tb + 1) * P], src[:, tb * P:(tb + 1) * P], ident[:])
                last.then_inc(sel_tr, 1)

            def spread(body):
                for half in range(2):
                    experts(body + UNITS, half)
                    for k in range(BODY_T // 2):
                        g = half * 2 + k // 4
                        if k % 4 == 0:
                            pe.wait_ge(g_ev, T // 4 * l + BODY_T // 4 * body + g + 1)
                        pe.wait_ge(oh_ready, T * l + BODY_T * body + half * (BODY_T // 2) + k + 1)
                        dst = ps[:, 2 + g, (k % 4) * P:(k % 4 + 1) * P]
                        nc.tensor.matmul(dst, oh[:, k, 0], oh[:, k, 1], start=True, stop=False)
                        nc.tensor.matmul(dst, oh[:, k, 0], oh[:, k, 2], start=False, stop=True).then_inc(g_tok, 1)

            with pe.Fori(0, WIN * BODIES) as body:
                spread(body)
            pe.wait_ge(gelu_done, EB * (l + 1) + PRIME)
            pe.wait_ge(g_ev, T // 4 * (l + 1) + 4)
            for bank in range(8):
                nc.tensor.matmul(ps[:, bank], zeros_bf[:, 0:P], zeros_bf[:, 0:T], start=True, stop=True,
                                 skip_group_check=True)
            with pe.Fori(0, EB // 2) as i:
                for s in range(2):
                    b = 2 * i + s
                    pe.wait_ge(v_l, EB * l + b + 1 + PRIME)
                    pe.wait_ge(wt_l, EB * l + b + 1)
                    for tb in range(TB):
                        rows = slice(tb * P, (tb + 1) * P)
                        for w, v in ((wt_hi, v_hi), (wt_hi, v_lo), (wt_lo, v_hi)):
                            for half in range(2):
                                last = nc.tensor.matmul(ps[:, 2 * tb + half], w[:, s, rows],
                                                        v[:, s, half * 512:(half + 1) * 512], start=False,
                                                        stop=True, skip_group_check=True)
                    last.then_inc(v_used, 1)

    ctx.close()


def rope_table(width):
    half = width // 2
    inv = np.exp(np.float32(-math.log(10000.0)) * np.arange(half, dtype=np.float32) / np.float32(half))
    ang = np.arange(T, dtype=np.float32)[:, None] * inv.astype(np.float32)[None, :]
    cos, sin = np.cos(ang), np.sin(ang)
    both = np.stack([np.concatenate([cos, cos], 1), np.concatenate([-sin, sin], 1)])
    return np.ascontiguousarray(both.reshape(2, TB, P, width).transpose(2, 0, 1, 3).astype(np.float32))


def mask_table():
    delta = np.abs(np.arange(MASK_W)[None, :] - 3 * P - np.arange(P)[:, None])
    count = sum((delta % dil == 0) & (delta // dil <= window // (2 * dil))
                for window, dil in ((128, 1), (512, 4), (2048, 16)))
    return np.where(count > 0, -np.log(np.maximum(count, 1)), BIG).astype(np.float32)


def kernel(**inputs):
    import concourse.bacc as bacc
    from concourse.bass_utils import run_bass_kernel_spmd

    x = {k: np.asarray(v) for k, v in inputs.items()}

    def columns(w, groups):
        n_l, k, n = w.shape
        w = w.reshape(n_l, k // P, P, groups, n // groups).transpose(0, 3, 2, 1, 4)
        return w.reshape(n_l, groups, P, k // P * (n // groups))

    lam = [0.8 - 0.6 * math.exp(-0.3 * (k + 1)) for k in range(L)]
    gains = [x["mla_q_norm_g"][:, 0:P], x["mla_q_norm_g"][:, P:QR], x["mla_kv_norm_g"], x["mla_kv_norm_g"]]
    arrays = {
        "x": x["x"].reshape(TB, P, D).transpose(1, 0, 2),
        "ident": np.eye(P, dtype=np.float32),
        "iota": np.tile(np.arange(P, dtype=np.float32), (P, 1)),
        "rope32": rope_table(32), "rope64": rope_table(64), "mask": mask_table(),
        "lam_c": np.array([[-v, 1.0 - v] for v in lam], np.float32),
        "w_in": columns(x["w_in"], IN_G), "w_o": columns(x["w_o"], O_G),
        "mla_w_uq": x["mla_w_uq"].reshape(L, 2, P, UQ_W).transpose(0, 2, 1, 3),
        "mla_w_ukv": x["mla_w_ukv"], "g_lat": np.stack(gains, axis=-1),
        "diff_lambda": x["diff_lambda"], "diff_subln_g": x["diff_subln_g"],
        "ln1": np.stack([x["ln1_g"], x["ln1_b"]], 1), "ln2": np.stack([x["ln2_g"], x["ln2_b"]], 1),
        "peer_w_q": columns(x["peer_w_q"], QB),
        "peer_keys": x["peer_sub_keys"].transpose(0, 4, 1, 2, 3).reshape(L, P, QB, NK),
        "peer_u": x["peer_u"].reshape(L, EB, P, DC, P).transpose(0, 1, 4, 3, 2).reshape(L, EB, P, DC * P),
        "peer_v": x["peer_v"].reshape(L, EB, P, D),
    }
    nc = bacc.Bacc("TRN2", target_bir_lowering=False, num_devices=1)
    arrays = {f"in_{k}": np.ascontiguousarray(v) for k, v in arrays.items()}
    aps = {k[3:]: nc.dram_tensor(k, v.shape, mybir.dt.from_np(v.dtype), kind="ExternalInput").ap()
           for k, v in arrays.items()}
    out = nc.dram_tensor("out_tokens", (TB, P, D), F32, kind="ExternalOutput").ap()
    build(nc, aps, out.rearrange("t p d -> p t d"))
    r = run_bass_kernel_spmd(nc, [arrays], core_ids=[0])
    return r.results[0]["out_tokens"].reshape(1, T, D)
```

```python
import math
from contextlib import ExitStack

import numpy as np

import concourse.bass as bass
from concourse import mybir

F32 = mybir.dt.float32
F32R = mybir.dt.float32r
U32 = mybir.dt.uint32
BF16 = mybir.dt.bfloat16
ALU = mybir.AluOpType
ACT = mybir.ActivationFunctionType
AX_X = mybir.AxisListType.X
ds = bass.ds

P = 128
L = 2
T = 512
D = 1024
TB = T // P
DC = D // P
AH, ADK, ADV = 4, 32, 64
BH, BNOPE, BROPE, BV = 6, 64, 32, 64
QR, KVR = 256, 128
CH, CDK = 6, 64
A_W, C_W = AH * ADV, CH * CDK
COL_AQ, COL_AK, COL_AV = 0, 256, 512
COL_CQ = 768
COL_CKV = COL_CQ + QR
COL_KR = COL_CKV + KVR
COL_C = COL_KR + BROPE
IN_W = COL_C + 3 * C_W
UQ_W = BH * (BNOPE + BROPE)
UKV_W = BH * (BNOPE + BV)
PH, NK, TOPK = 8, 128, 16
NEXP = NK * NK
ALPHA = (2 * L) ** 0.25
LN_EPS = 1e-5

IN_G, IN_N = 8, IN_W // 8
O_G, O_N = 4, D // 4
W_PER = IN_G + O_G
JA, JB, JC = 2 * AH, BH, CH
JOBS = JA + JB + JC
DK = BNOPE + BROPE
VD = 64
MAPS = JOBS * TB
QB = 2 * PH
EB = NEXP // P
ST_PER = QB + 2 * EB
UNITS = TB * PH
BLOCKS_TOPK = 2 * UNITS
WIN, WIN_T = 8, T // 8
GRP = 4
BODY_T = 16
GROUPS = BODY_T // GRP
BODIES = WIN_T // BODY_T
WIN_D = WIN // 2 - 1
T_D = 2 * WIN_D * WIN_T
assert IN_G * IN_N == IN_W and BLOCKS_TOPK + 2 * WIN * BODIES == EB
PRIME = 2
BIG = 1.0e30
NEG = -3.0e38
MASK_W = T + 3 * P


class Steps:

    def __init__(self, eng, sem):
        self.eng, self.sem, self.base, self.n = eng, sem, 0, 0

    def at(self, base):
        self.base, self.n = base, 0

    def done(self, ins):
        ins.then_inc(self.sem, 1)
        self.n += 1

    def wait(self):
        self.eng.wait_ge(self.sem, self.base + self.n)

    def wait_apart(self, waited):
        self.wait()
        self.eng.sem_inc(waited, 1)


def build(nc, a, out):
    ctx = ExitStack()
    base = (nc.sbuf_base + 63) // 64 * 64
    limit = nc.sbuf_usable_end

    class Region:
        def __init__(self, start):
            self.start, self.end = start, start

        def tile(self, name, shape, dt):
            size = int(np.prod(shape[1:])) * (2 if dt == BF16 else 4)
            t = nc.alloc_sbuf_tensor_at(name, list(shape), dt, offset=self.end)
            self.end += (size + 63) // 64 * 64
            assert self.end <= limit, (name, self.end, limit)
            return t

    keep = Region(base)
    x_tok = keep.tile("x_tok", [P, TB, D], F32)
    t_hi = keep.tile("t_hi", [P, DC, T], F32R)
    t_lo = keep.tile("t_lo", [P, DC, T], F32R)
    ident = keep.tile("ident", [P, P], F32)
    iota = keep.tile("iota", [P, P], F32)
    zeros = keep.tile("zeros", [P, T], F32)
    zeros_bf = zeros[:].bitcast(BF16)
    neg_max = keep.tile("neg_max", [P, 2], F32)
    row_sum = keep.tile("row_sum", [P, 2, TB], F32)
    row_inv = keep.tile("row_inv", [P, 2, TB], F32)
    lat_sq = keep.tile("lat_sq", [P, 2, TB], F32)
    lat_rms = keep.tile("lat_rms", [P, 2, TB], F32)
    lat_inv = keep.tile("lat_inv", [P, 2, TB], F32)
    sub_sq = keep.tile("sub_sq", [P, TB * AH], F32)
    sub_rms = keep.tile("sub_rms", [P, TB * AH], F32)
    sub_inv = keep.tile("sub_inv", [P, TB * AH], F32)
    lam_dot = keep.tile("lam_dot", [P, 2], F32)
    lam_exp = keep.tile("lam_exp", [P, 2], F32)
    lam_neg = keep.tile("lam_neg", [P, 2], F32)
    bn = keep.tile("bn", [P, TB, 2, 6], F32)
    mean_var = keep.tile("mean_var", [P, TB, 2], F32)
    ln_dev = keep.tile("ln_dev", [P, TB], F32)
    ln_inv = keep.tile("ln_inv", [P, TB], F32)
    eps = keep.tile("eps", [P, 1], F32)

    att = Region(keep.end)
    w_raw = att.tile("w_raw", [P, 2, DC * IN_N], F32)
    h = att.tile("h", [P, TB, IN_W], F32)
    ln_rows = nc.alloc_sbuf_tensor_at("ln_rows", [P, 2, D], F32, offset=att.end)
    ln_rows_at = att.end
    q_b = att.tile("q_b", [P, TB, UQ_W], F32)
    kv_b = att.tile("kv_b", [P, TB, UKV_W], F32)
    o_all = att.tile("o_all", [P, TB, JOBS * VD], F32)
    w_uq = att.tile("w_uq", [P, 2, UQ_W], F32)
    w_ukv = att.tile("w_ukv", [P, UKV_W], F32)
    g_lat = att.tile("g_lat", [P, 4], F32)
    rope32 = att.tile("rope32", [P, 2, TB, 32], F32)
    rope64 = att.tile("rope64", [P, 2, TB, 64], F32)
    mask = att.tile("mask", [P, MASK_W], F32)
    lam_in = att.tile("lam_in", [P, 4, ADK], F32)
    sub_g = att.tile("sub_g", [P, ADV], F32)
    lam_c = att.tile("lam_c", [P, 2], F32)
    w_split = Region(att.end)
    w_hi = w_split.tile("w_hi", [P, 2, DC * IN_N], F32R)
    w_lo = w_split.tile("w_lo", [P, 2, DC * IN_N], F32R)
    hd = Region(att.end)
    lat_n = hd.tile("lat_n", [P, TB, QR + KVR], F32)
    lat_t = hd.tile("lat_t", [P, 3, T], F32)
    rq = hd.tile("rq", [P, 2, TB, 2, DK], F32)
    q_t = hd.tile("q_t", [P, 2, T], F32)
    k_t = hd.tile("k_t", [P, 2, T], F32)
    v_s = hd.tile("v_s", [P, 2, TB, VD], F32)
    sc_s = hd.tile("sc_s", [P, 2], F32)
    masked = hd.tile("masked", [P, 2, T], F32)
    probs = hd.tile("probs", [P, 2, T], F32)
    p_t = hd.tile("p_t", [P, 2, TB, P], F32)
    rt_a = lat_n[:].rearrange("p t d -> p (t d)")[:, 0:TB * 2 * 64].rearrange("p (t k d) -> p t k d", t=TB, k=2)
    rt_b = lat_n[:].rearrange("p t d -> p (t d)")[:, TB * 2 * 64:TB * 4 * 64].rearrange("p (t k d) -> p t k d", t=TB, k=2)
    kpe = hd.tile("kpe", [P, TB, BROPE], F32)
    o_f = lat_t[:].rearrange("p t d -> p (t d)")[:, 0:TB * A_W].rearrange("p (t h d) -> p t h d", t=TB, h=AH)
    o_q = q_t[:].rearrange("p s d -> p (s d)").rearrange("p (t h d) -> p t h d", t=TB, h=AH)

    pr = Region(keep.end)
    st_raw = pr.tile("st_raw", [P, 2, DC * P], F32)
    st_hi = pr.tile("st_hi", [P, 2, DC, P], F32R)
    st_lo = pr.tile("st_lo", [P, 2, DC, P], F32R)
    h_out = pr.tile("h_out", [P, 2, T], F32)
    shared = pr.end
    keys = pr.tile("keys", [P, QB, NK], F32)
    k_hi = pr.tile("k_hi", [P, QB, NK], F32R)
    k_lo = pr.tile("k_lo", [P, QB, NK], F32R)
    pq_hi = pr.tile("pq_hi", [P, 2, T], F32R)
    pq_lo = pr.tile("pq_lo", [P, 2, T], F32R)
    scores = pr.tile("scores", [P, UNITS, 2, NK], F32)
    tk = Region(pr.end)
    opt16 = tk.tile("opt16", [P, 2, TOPK, TOPK], BF16)
    wk = tk.tile("wk", [P, 2, NK], F32)
    wk2 = tk.tile("wk2", [P, 2, NK], F32)
    v16 = tk.tile("v16", [P, 2, TOPK], F32)
    x16 = tk.tile("x16", [P, 2, TOPK], U32)
    x16f = tk.tile("x16f", [P, 2, TOPK], F32)
    cand = tk.tile("cand", [P, TOPK, TOPK], F32)
    cand2 = tk.tile("cand2", [P, TOPK * TOPK], F32)
    c16 = tk.tile("c16", [P, TOPK], F32)
    ci = tk.tile("ci", [P, TOPK], U32)
    cab = tk.tile("cab", [P, 2, TOPK], U32)
    cabf = tk.tile("cabf", [P, 2, TOPK], BF16)
    eq = tk.tile("eq", [P, 2, TOPK, TOPK], F32)
    c_all = tk.tile("c_all", [P, UNITS, TOPK], F32)
    i_all = tk.tile("i_all", [P, 2, UNITS * TOPK], F32)
    e_all = tk.tile("e_all", [P, UNITS, TOPK], F32)
    c_top = tk.tile("c_top", [P, UNITS], F32)
    z_all = tk.tile("z_all", [P, 2, UNITS], F32)
    gb = Region(shared)
    i_t = gb.tile("i_t", [P, 2, T], F32)
    g_t = gb.tile("g_t", [P, T], F32)
    oh = gb.tile("oh", [P, BODY_T, 2, P], F32)
    assert gb.end <= ln_rows_at
    vp = Region(ln_rows_at + 2 * D * 4)
    g_in = vp.tile("g_in", [P, 2, T_D], F32)
    h_in = vp.tile("h_in", [P, 2, T], F32)
    w_f = vp.tile("w_f", [P, 2, T], F32)
    wt_hi = vp.tile("wt_hi", [P, 2, T], F32R)
    wt_lo = vp.tile("wt_lo", [P, 2, T], F32R)
    ga = Region((limit - 2 * NK * WIN_T * 4) // 64 * 64)
    g_stage = ga.tile("g_stage", [P, 2, NK, WIN_T], F32)
    assert vp.end <= ga.start

    ps = ctx.enter_context(nc.psum_tensor("ps", [P, 8, 512], F32))
    gates_d = nc.dram_tensor("gates_d", [EB, P, T_D], F32, kind="Internal").ap()
    gelu_d = nc.dram_tensor("gelu_d", [EB, P, T], F32, kind="Internal").ap()

    def sem(name):
        return ctx.enter_context(nc.semaphore(name))

    s_x = sem("s_x")
    eps_set = sem("eps_set")
    s_lay = sem("s_lay")
    s_keys, s_ln = sem("s_keys"), sem("s_ln")
    s_wraw = [sem(f"s_wraw{s}") for s in range(2)]
    s_straw = [sem(f"s_straw{s}") for s in range(2)]
    s_gh = [sem(f"s_gh{s}") for s in range(2)]
    s_hst = [sem(f"s_hst{s}") for s in range(2)]
    s_gst = [sem(f"s_gst{s}") for s in range(2)]
    s_out = sem("s_out")
    tr_ps, tr_hi, tr_lo = sem("tr_ps"), sem("tr_hi"), sem("tr_lo")
    wc_hi, wc_lo = sem("wc_hi"), sem("wc_lo")
    pj_ps, pj_act, pj_dve, pj_res = sem("pj_ps"), sem("pj_act"), sem("pj_dve"), sem("pj_res")
    lat_ss, lat_sd, lat_ready, lat_tr, lat_ev, lat_ps, lat_qev, lat_kev = (sem(n) for n in (
        "lat_ss", "lat_sd", "lat_ready", "lat_tr", "lat_ev", "lat_ps", "lat_qev", "lat_kev"))
    v_ready = sem("v_ready")
    rope_done, qk_tr, q_ev, k_ev, s_ps, s_min, s_exp, pt_ps, pt_dve, pt_act, pv_done, o_ev = (sem(n) for n in (
        "rope_done", "qk_tr", "q_ev", "k_ev", "s_ps", "s_min", "s_exp", "pt_ps", "pt_dve", "pt_act", "pv_done",
        "o_ev"))
    sub_ss, sub_sd, mix_ready = sem("sub_ss"), sem("sub_sd"), sem("mix_ready")
    lam_s, lam_e = sem("lam_s"), sem("lam_e")
    ln_var, ln_sd, ln_done = sem("ln_var"), sem("ln_sd"), sem("ln_done")
    keys_hi, keys_lo = sem("keys_hi"), sem("keys_lo")
    st_h, st_used = sem("st_h"), sem("st_used")
    st_l = [sem(f"st_l{s}") for s in range(2)]
    pq_h, pq_l, sc_ps, sc_ev = sem("pq_h"), sem("pq_l"), sem("sc_ps"), sem("sc_ev")
    gelu_done = sem("gelu_done")
    topk_done, gate_sub, gate_exp, gate_ready, sel_tr, sel_act, sel_dve = (sem(n) for n in (
        "topk_done", "gate_sub", "gate_exp", "gate_ready", "sel_tr", "sel_act", "sel_dve"))
    oh_ready, g_tok, g_ev = sem("oh_ready"), sem("g_tok"), sem("g_ev")
    wt_f, wt_h, wt_l = sem("wt_f"), sem("wt_h"), sem("wt_l")
    ffn_done = sem("ffn_done")
    waited = sem("waited")
    dve_step, pool_step = sem("dve_step"), sem("pool_step")

    block = ctx.enter_context(nc.Block())

    @block.sync
    def _(sp):
        for dst, src in ((x_tok[:], a["x"]), (ident[:], a["ident"]), (iota[:], a["iota"])):
            sp.dma_start(dst, src).then_inc(s_x, 16)
        with sp.Fori(0, L) as l:
            sp.wait_ge(ln_done, 2 * TB * l + PRIME)
            for dst, src in (
                (w_uq[:], a["mla_w_uq"][l]), (w_ukv[:], a["mla_w_ukv"][l]), (g_lat[:], a["g_lat"][l]),
                (lam_in[:], a["diff_lambda"][l].partition_broadcast(P)),
                (sub_g[:], a["diff_subln_g"][l].partition_broadcast(P)),
                (lam_c[:], a["lam_c"][l].partition_broadcast(P)),
                (rope32[:], a["rope32"]), (rope64[:], a["rope64"]), (mask[:], a["mask"]),
            ):
                sp.dma_start(dst, src).then_inc(s_lay, 16)

            def w_load(n, s, src):
                sp.wait_ge(wc_lo, W_PER * l + n + 1)
                sp.dma_start(w_raw[:, s, 0:src.shape[1]], src).then_inc(s_wraw[s], 16)

            with sp.Fori(0, IN_G // 2) as i:
                for s in range(2):
                    w_load(2 * i + s, s, a["w_in"][l, 2 * i + s])
            for k in range(O_G):
                w_load(IN_G + k, k % 2, a["w_o"][l, k])
                if k == 1:
                    sp.wait_ge(v_ready, JOBS * (l + 1))
                    sp.dma_start(ln_rows[:], a["ln1"][l].partition_broadcast(P)).then_inc(s_ln, 16)
            sp.wait_ge(pj_res, O_G * TB * (l + 1))
            sp.dma_start(keys[:], a["peer_keys"][l]).then_inc(s_keys, 16)

            def st_load(m, s, src):
                sp.wait_ge(st_l[s], ST_PER // 2 * l + m + 1)
                sp.dma_start(st_raw[:, s], src).then_inc(s_straw[s], 16)

            def gelu_store(i, s):
                sp.wait_ge(gelu_done, EB * l + 2 * i + s + 1 + PRIME)
                sp.dma_start(gelu_d[2 * i + s], h_out[:, s]).then_inc(s_hst[s], 16)

            def gated_load(i, s):
                sp.wait_ge(wt_f, EB * l + 2 * i + s + 1)
                sp.dma_start(g_in[:, s], gates_d[2 * i + s]).then_inc(s_gh[s], 16)
                sp.dma_start(h_in[:, s], gelu_d[2 * i + s]).then_inc(s_gh[s], 16)

            with sp.Fori(0, QB // 2) as i:
                for s in range(2):
                    st_load(i, s, a["peer_w_q"][l, 2 * i + s])
            for s in range(2):
                st_load(QB // 2, s, a["peer_u"][l, s])
            with sp.Fori(0, EB // 2 - 1) as i:
                for s in range(2):
                    st_load(i + QB // 2 + 1, s, a["peer_u"][l, 2 * i + 2 + s])
                for s in range(2):
                    gelu_store(i, s)
            for s in range(2):
                st_load((QB + EB) // 2, s, a["peer_v"][l, s])
            for s in range(2):
                sp.wait_ge(s_gst[s], 16 * (BODIES * WIN_D * (l + 1) + 1))
                sp.wait_ge(s_hst[s], 16 * (EB // 2 * l + 1 + 1))
                sp.sem_inc(waited, 1)
            for s in range(2):
                gated_load(0, s)
            sp.dma_start(ln_rows[:], a["ln2"][l].partition_broadcast(P)).then_inc(s_ln, 16)
            for s in range(2):
                gelu_store(EB // 2 - 1, s)
            for s in range(2):
                sp.wait_ge(s_hst[s], 16 * (EB // 2 * (l + 1) + 1))
                sp.sem_inc(waited, 1)
            with sp.Fori(1, EB // 2) as i:
                for s in range(2):
                    st_load(i + (QB + EB) // 2, s, a["peer_v"][l, 2 * i + s])
                    gated_load(i, s)
        sp.wait_ge(ln_done, 2 * TB * L + PRIME)
        sp.dma_start(out, x_tok[:]).then_inc(s_out, 16)
        sp.wait_ge(s_out, 16)

    @block.gpsimd
    def _(pool):
        step = Steps(pool, pool_step)
        pool.sem_inc(st_l[1], 1)
        n_a, n_b, n_c = 4, 7, 4
        per = 2 + n_a * JA + 4 + n_b * JB + 2 + n_c * JC
        with pool.Fori(0, L) as l:
            pool.wait_ge(lat_qev, TB * (l + 1))
            pool.wait_ge(lat_kev, TB * (l + 1))
            pool.wait_ge(s_lay, 16 * 9 * (l + 1))
            at = per * l
            step.at(at)
            pool.sem_inc(waited, 1)
            for s in range(2):
                step.done(nc.gpsimd.memset(rq[:, s, :, :, ADK:DK], 0.0))
            step.wait_apart(waited)
            at = at + 2

            def slot_free(j):
                pool.wait_ge(qk_tr, JOBS * l + j + 1)
                pool.wait_ge(q_ev, JOBS * l + j + 1)

            def rotate(dst, src, first, second, table, w):
                nk = dst.shape[2]
                cos = table[:, 0].unsqueeze(2).to_broadcast([P, TB, nk, w])
                sin = table[:, 1].unsqueeze(2).to_broadcast([P, TB, nk, w])
                ta, tb_ = rt_a[:, :, 0:nk, 0:w], rt_b[:, :, 0:nk, 0:w]
                step.done(nc.gpsimd.tensor_tensor(ta, src, cos, ALU.mult))
                step.done(nc.gpsimd.tensor_tensor(tb_[:, :, :, 0:w // 2], second, sin[:, :, :, 0:w // 2], ALU.mult))
                step.done(nc.gpsimd.tensor_tensor(tb_[:, :, :, w // 2:w], first, sin[:, :, :, w // 2:w], ALU.mult))
                step.wait()
                step.done(nc.gpsimd.tensor_tensor(dst, ta, tb_, ALU.add))

            def rotate_pair(s, col, width, j, w, table):
                v = h[:, :, col:col + 2 * width].rearrange("p t (k f) -> p t k f", k=2)
                half = w // 2
                rotate(rq[:, s, :, :, 0:w], v[:, :, :, ds(j * w, w)], v[:, :, :, ds(j * w, half)],
                       v[:, :, :, ds(j * w + half, half)], table, w)

            def finish(j, s, dk, v_src):
                step.wait_apart(waited)
                nc.gpsimd.memset(sc_s[:, s:s + 1], -dk ** -0.5).then_inc(rope_done, 1)
                pool.wait_ge(pv_done, JOBS * l + j + 1)
                pool.sem_inc(waited, 1)
                nc.gpsimd.tensor_copy(v_s[:, s], v_src).then_inc(v_ready, 1)

            with pool.Fori(0, AH) as i:
                for s in range(2):
                    j = 2 * i + s
                    step.at(at + n_a * j)
                    slot_free(j)
                    rotate_pair(s, COL_AQ, COL_AK - COL_AQ, j, ADK, rope32)
                    finish(j, s, ADK, h[:, :, ds(i * ADV + COL_AV, ADV)])
                    assert step.n == n_a
            at = at + n_a * JA
            step.at(at)
            kr = h[:, :, COL_KR:COL_KR + BROPE].unsqueeze(2)
            rotate(kpe[:].unsqueeze(2), kr, kr[:, :, :, 0:BROPE // 2], kr[:, :, :, BROPE // 2:BROPE], rope32, BROPE)
            step.wait_apart(waited)
            at = at + 4
            with pool.Fori(0, JB // 2) as i:
                for s in range(2):
                    j = 2 * i + s
                    step.at(at + n_b * j)
                    slot_free(j + JA)
                    qv = q_b[:].unsqueeze(2)
                    q0, kv0 = j * DK, j * (BNOPE + BV)
                    rotate(rq[:, s, :, 0:1, BNOPE:DK], qv[:, :, :, ds(q0 + BNOPE, BROPE)],
                           qv[:, :, :, ds(q0 + BNOPE, BROPE // 2)],
                           qv[:, :, :, ds(q0 + BNOPE + BROPE // 2, BROPE // 2)], rope32, BROPE)
                    step.done(nc.gpsimd.tensor_copy(rq[:, s, :, 0, 0:BNOPE], q_b[:, :, ds(q0, BNOPE)]))
                    step.done(nc.gpsimd.tensor_copy(rq[:, s, :, 1, 0:BNOPE], kv_b[:, :, ds(kv0, BNOPE)]))
                    step.done(nc.gpsimd.tensor_copy(rq[:, s, :, 1, BNOPE:DK], kpe[:]))
                    finish(j + JA, s, DK, kv_b[:, :, ds(kv0 + BNOPE, BV)])
                    assert step.n == n_b
            at = at + n_b * JB
            step.at(at)
            pool.wait_ge(qk_tr, JOBS * l + JA + JB + PRIME)
            pool.sem_inc(waited, 1)
            for s in range(2):
                step.done(nc.gpsimd.memset(rq[:, s, :, :, CDK:DK], 0.0))
            step.wait_apart(waited)
            at = at + 2
            with pool.Fori(0, JC // 2) as i:
                for s in range(2):
                    j = 2 * i + s
                    step.at(at + n_c * j)
                    slot_free(j + JA + JB)
                    rotate_pair(s, COL_C, C_W, j, CDK, rope64)
                    finish(j + JA + JB, s, CDK, h[:, :, ds(j * CDK + COL_C + 2 * C_W, CDK)])
                    assert step.n == n_c
            with pool.Fori(0, ST_PER // 2) as m:
                pool.wait_ge(st_h, ST_PER * l + 2 * m + 2)
                nc.gpsimd.tensor_tensor(st_lo[:, 1].rearrange("p c f -> p (c f)"), st_raw[:, 1],
                                        st_hi[:, 1].rearrange("p c f -> p (c f)").bitcast(F32),
                                        ALU.subtract).then_inc(st_l[1], 1)

    @block.scalar
    def _(act):
        act.sem_inc(q_ev, PRIME)
        act.sem_inc(s_exp, PRIME)
        act.sem_inc(pj_act, 2 * PRIME)
        act.sem_inc(gelu_done, PRIME)
        act.sem_inc(sc_ev, PRIME)
        act.sem_inc(g_ev, GROUPS)
        for s in range(2):
            act.sem_inc(s_gst[s], 16)
            act.sem_inc(s_hst[s], 16)
        act.wait_ge(eps_set, 1)
        with act.Fori(0, L) as l:

            def round_chunks(u):
                for c in range(DC):
                    act.wait_ge(tr_ps, DC * (3 * l + u) + c + 1)
                    nc.scalar.copy(t_hi[:, c], ps[:, c]).then_inc(tr_hi, 1)

            def round_group(n, s, size):
                act.wait_ge(s_wraw[s], 16 * (W_PER // 2 * l + (n - s) // 2 + 1))
                act.wait_ge(pj_ps, TB * (W_PER * l + n + 1))
                nc.scalar.copy(w_hi[:, s, 0:size], w_raw[:, s, 0:size]).then_inc(wc_hi, 1)

            def keep_h(n, s):
                for tb in range(TB // 2):
                    act.wait_ge(pj_ps, (W_PER * l + n) * TB + tb + 1 + PRIME * TB)
                    nc.scalar.copy(h[:, tb, ds(n * IN_N, IN_N)], ps[:, TB * s + tb, 0:IN_N]).then_inc(pj_act, 1)

            round_chunks(0)
            round_group(0, 0, DC * IN_N)
            with act.Fori(0, IN_G // 2 - 1) as i:
                round_group(2 * i + 1, 1, DC * IN_N)
                keep_h(2 * i, 0)
                round_group(2 * i + 2, 0, DC * IN_N)
                keep_h(2 * i + 1, 1)
            round_group(IN_G - 1, 1, DC * IN_N)
            keep_h(IN_G - 2, 0)
            keep_h(IN_G - 1, 1)
            act.wait_ge(lat_ss, l + 1)
            nc.scalar.activation(lat_rms[:, 0], lat_sq[:, 0], ACT.Sqrt, bias=eps[:], scale=1.0 / QR)
            nc.scalar.activation(lat_rms[:, 1], lat_sq[:, 1], ACT.Sqrt, bias=eps[:], scale=1.0 / KVR).then_inc(lat_sd, 1)
            act.wait_ge(s_lay, 16 * 9 * (l + 1))
            for k in range(3):
                act.wait_ge(lat_tr, 3 * l + k + 1)
                nc.scalar.activation(lat_t[:, k], ps[:, k], ACT.Copy, scale=g_lat[:, k:k + 1]).then_inc(lat_ev, 1)
            for tb in range(TB):
                bank = 4 * ((tb + 1) % 2)
                act.wait_ge(lat_ps, 2 * TB * l + 2 * tb + 1)
                nc.scalar.copy(q_b[:, tb].rearrange("p (k f) -> p k f", k=2),
                               ps[:, bank:bank + 2, 0:UQ_W // 2]).then_inc(lat_qev, 1)
            act.wait_ge(lam_s, l + 1)
            nc.scalar.activation(lam_exp[:], lam_dot[:], ACT.Exp).then_inc(lam_e, 1)

            def scale_q(j, s):
                act.wait_ge(qk_tr, JOBS * l + j + 1 + PRIME)
                nc.scalar.activation(q_t[0:DK, s], ps[0:DK, 4], ACT.Copy, scale=sc_s[0:DK, s:s + 1]).then_inc(q_ev, 1)

            def exponent(j, s, qb):
                n = TB * j + qb
                act.wait_ge(s_min, MAPS * l + n + 1 + PRIME)
                act.wait_ge(pt_ps, MAPS * l + n + 1)
                nc.scalar.activation(probs[:, qb % 2], masked[:, qb % 2], ACT.Exp, bias=neg_max[:, qb % 2:qb % 2 + 1],
                                     scale=-1.0, accum_out=row_sum[:, s, qb:qb + 1]).then_inc(s_exp, 1)

            def keep_pt(j, qb):
                act.wait_ge(pt_ps, MAPS * l + TB * j + qb + 1 + PRIME)
                nc.scalar.copy(p_t[:, qb % 2].rearrange("p k q -> p (k q)"), ps[:, 2 + qb % 2]).then_inc(pt_act, 1)

            def job(j, s, ahead):
                exponent(j, s, 2)
                if ahead:
                    scale_q(j + 1, 1 - s)
                exponent(j, s, 3)
                if ahead:
                    exponent(j + 1, 1 - s, 0)
                    exponent(j + 1, 1 - s, 1)
                keep_pt(j, 3)

            scale_q(0, 0)
            exponent(0, 0, 0)
            exponent(0, 0, 1)
            with act.Fori(0, JOBS // 2 - 1) as i:
                job(2 * i, 0, True)
                job(2 * i + 1, 1, True)
            job(JOBS - 2, 0, True)
            job(JOBS - 1, 1, False)
            act.wait_ge(sub_ss, l + 1)
            nc.scalar.activation(sub_rms[:], sub_sq[:], ACT.Sqrt, bias=eps[:], scale=1.0 / ADV).then_inc(sub_sd, 1)
            round_chunks(1)
            for k in range(O_G):
                round_group(IN_G + k, k % 2, DC * O_N)

            def deviation(u):
                act.wait_ge(ln_var, 2 * l + u + 1)
                nc.scalar.activation(ln_dev[:], mean_var[:, :, 1], ACT.Sqrt, bias=eps[:]).then_inc(ln_sd, 1)

            deviation(0)
            act.wait_ge(s_keys, 16 * (l + 1))
            nc.scalar.copy(k_hi[:], keys[:]).then_inc(keys_hi, 1)
            round_chunks(2)

            def round_block(m, s):
                act.wait_ge(s_straw[s], (ST_PER // 2 * l + m + 1) * 16)
                act.wait_ge(st_used, ST_PER * l + 2 * m + s + 1)
                nc.scalar.copy(st_hi[:, s].rearrange("p c f -> p (c f)"), st_raw[:, s]).then_inc(st_h, 1)

            def round_query(f, s):
                act.wait_ge(st_used, ST_PER * l + f + 1 + PRIME)
                nc.scalar.copy(pq_hi[:, s], ps[:, s]).then_inc(pq_h, 1)

            def keep_scores(f, s):
                act.wait_ge(sc_ps, QB * l + f + 1)
                dst = scores[:].rearrange("p (t h) k n -> p t (h k) n", t=TB)[:, :, ds(f, 1), :]
                nc.scalar.copy(dst, ps[:, 2 + s].rearrange("p (t o n) -> p t o n", t=TB, o=1)).then_inc(sc_ev, 1)

            def gelu(m, s):
                b = 2 * m + s
                act.wait_ge(st_used, ST_PER * l + QB + b + 1 + PRIME)
                act.wait_ge(s_hst[s], (EB // 2 * l + m + 1) * 16)
                nc.scalar.activation(h_out[:, s], ps[:, s], ACT.Gelu).then_inc(gelu_done, 1)

            round_block(0, 0)
            with act.Fori(0, QB // 2) as i:
                round_block(i, 1)
                round_query(2 * i, 0)
                round_block(i + 1, 0)
                round_query(2 * i + 1, 1)
                keep_scores(2 * i, 0)
                keep_scores(2 * i + 1, 1)
            round_block(QB // 2, 1)
            with act.Fori(0, UNITS) as i:
                for s in range(2):
                    gelu(i, s)
                    round_block(i + QB // 2 + 1, s)
            act.wait_ge(gate_sub, l + 1)
            nc.scalar.activation(e_all[:], c_all[:], ACT.Exp).then_inc(gate_exp, 1)
            for k in range(3):
                act.wait_ge(sel_tr, 3 * l + k + 1)
                nc.scalar.copy(g_t[:] if k == 2 else i_t[:, k], ps[:, 5 + k]).then_inc(sel_act, 1)

            def keep_gates(sw, q, body, g):
                act.wait_ge(g_tok, T // GRP * l + GROUPS * body + g + 1 + GROUPS)
                nc.scalar.copy(g_stage[:, sw, :, ds(q * BODY_T + GRP * g, GRP)],
                               ps[:, 2 + g].rearrange("p (t n) -> p n t", t=GRP)).then_inc(g_ev, 1)

            def window(w, sw, store):
                with act.Fori(0, BODIES) as q:
                    body = w * BODIES + q
                    if store:
                        n_q = NK // BODIES
                        act.wait_ge(g_ev, T // GRP * l + WIN_T // GRP * w + GROUPS)
                        act.dma_start(gates_d[ds(q * n_q, n_q), :, ds(w * WIN_T - WIN_T, WIN_T)].rearrange("n p t -> p n t"),
                                      g_stage[:, 1 - sw, ds(q * n_q, n_q)]).then_inc(s_gst[1 - sw], 16)
                    for s in range(2):
                        gelu(body + UNITS, s)
                        round_block(body + UNITS + QB // 2 + 1, s)
                        if s == 0:
                            act.wait_ge(s_gst[sw], (BODIES * (WIN_D * l + (w - sw) // 2) + 1) * 16)
                        for g in range(s * GROUPS // 2, (s + 1) * GROUPS // 2):
                            keep_gates(sw, q, body, g)

            window(0, 0, False)
            with act.Fori(0, WIN_D) as w2:
                window(2 * w2 + 1, 1, True)
                window(2 * w2 + 2, 0, True)
            window(WIN - 1, 1, False)

            def round_gated(b, s):
                act.wait_ge(wt_f, EB * l + b + 1 + PRIME)
                act.wait_ge(st_used, ST_PER * l + QB + EB + b + 1)
                nc.scalar.copy(wt_hi[:, s], w_f[:, s]).then_inc(wt_h, 1)

            round_gated(0, 0)
            with act.Fori(0, EB // 2 - 1) as i:
                for s in range(2):
                    round_gated(2 * i + s + 1, 1 - s)
                    round_block(i + (QB + EB) // 2 + 1, s)
            round_gated(EB - 1, 1)
            deviation(1)

    @block.vector
    def _(dve):
        step = Steps(dve, dve_step)
        dve.sem_inc(wc_lo, PRIME)
        dve.sem_inc(pj_dve, 2 * PRIME)
        dve.sem_inc(k_ev, PRIME)
        dve.sem_inc(s_min, PRIME)
        dve.sem_inc(o_ev, PRIME)
        dve.sem_inc(st_l[0], 1)
        dve.sem_inc(wt_f, PRIME)
        dve.sem_inc(ln_done, PRIME)
        nc.vector.memset(eps[:], LN_EPS).then_inc(eps_set, 1)
        nc.vector.memset(zeros[:], 0.0).then_inc(eps_set, 1)
        n_pre, n_sub, n_ln, n_unit, n_gate = 4, 4, 2 + TB, 25, 3
        per = n_pre + JOBS + n_sub + 2 * n_ln + 1 + UNITS * n_unit + n_gate
        with dve.Fori(0, L) as l:
            at = per * l

            def rest_chunks(u):
                for c in range(DC):
                    dve.wait_ge(tr_hi, DC * (3 * l + u) + c + 1)
                    nc.vector.tensor_tensor(t_lo[:, c], ps[:, c], t_hi[:, c].bitcast(F32),
                                            ALU.subtract).then_inc(tr_lo, 1)

            def rest_group(n, s, size):
                dve.wait_ge(wc_hi, W_PER * l + n + 1)
                nc.vector.tensor_tensor(w_lo[:, s, 0:size], w_raw[:, s, 0:size], w_hi[:, s, 0:size].bitcast(F32),
                                        ALU.subtract).then_inc(wc_lo, 1)

            def keep_h(n, s):
                for tb in range(TB // 2, TB):
                    dve.wait_ge(pj_ps, (W_PER * l + n) * TB + tb + 1 + PRIME * TB)
                    nc.vector.tensor_copy(h[:, tb, ds(n * IN_N, IN_N)], ps[:, TB * s + tb, 0:IN_N]).then_inc(pj_dve, 1)

            rest_chunks(0)
            rest_group(0, 0, DC * IN_N)
            with dve.Fori(0, IN_G // 2 - 1) as i:
                rest_group(2 * i + 1, 1, DC * IN_N)
                keep_h(2 * i, 0)
                rest_group(2 * i + 2, 0, DC * IN_N)
                keep_h(2 * i + 1, 1)
            rest_group(IN_G - 1, 1, DC * IN_N)
            keep_h(IN_G - 2, 0)
            keep_h(IN_G - 1, 1)
            step.at(at)
            dve.wait_ge(s_lay, 16 * 9 * (l + 1))
            for k in range(2):
                ins = nc.vector.tensor_tensor_reduce(out=lam_in[:, 2 * k], in0=lam_in[:, 2 * k],
                                                     in1=lam_in[:, 2 * k + 1], scale=1.0, scalar=0.0, op0=ALU.mult,
                                                     op1=ALU.add, accum_out=lam_dot[:, k:k + 1])
            ins.then_inc(lam_s, 1)
            step.done(nc.vector.tensor_scalar(sub_g[:], sub_g[:], lam_c[:, 1:2], None, ALU.mult))
            dve.wait_ge(pj_act, IN_G * 2 * (l + 1) + 2 * PRIME)
            dve.wait_ge(pj_dve, IN_G * 2 * (l + 1) + 2 * PRIME)
            for tb in range(TB):
                for k, (c0, w) in enumerate(((COL_CQ, QR), (COL_CKV, KVR))):
                    src = h[:, tb, c0:c0 + w]
                    ins = nc.vector.tensor_tensor_reduce(out=lat_n[:, tb, k * QR:k * QR + w], in0=src, in1=src,
                                                         scale=1.0, scalar=0.0, op0=ALU.mult, op1=ALU.add,
                                                         accum_out=lat_sq[:, k, tb:tb + 1])
            ins.then_inc(lat_ss, 1)
            dve.wait_ge(lat_sd, l + 1)
            step.done(nc.vector.reciprocal(lat_inv[:], lat_rms[:]))
            step.wait()
            for tb in range(TB):
                for k, (c0, w) in enumerate(((COL_CQ, QR), (COL_CKV, KVR))):
                    ins = nc.vector.tensor_scalar(lat_n[:, tb, k * QR:k * QR + w], h[:, tb, c0:c0 + w],
                                                  lat_inv[:, k, tb:tb + 1], None, ALU.mult)
            ins.then_inc(lat_ready, 1)
            for tb in range(TB):
                bank = 4 * ((tb + 1) % 2) + 2
                dve.wait_ge(lat_ps, 2 * TB * l + 2 * tb + 2)
                nc.vector.tensor_copy(kv_b[:, tb].rearrange("p (k f) -> p k f", k=2),
                                      ps[:, bank:bank + 2, 0:UKV_W // 2]).then_inc(lat_kev, 1)
            dve.wait_ge(lam_e, l + 1)
            step.done(nc.vector.tensor_tensor(lam_neg[:, 0:1], lam_exp[:, 1:2], lam_exp[:, 0:1], ALU.subtract))
            step.wait()
            step.done(nc.vector.tensor_scalar(lam_neg[:, 1:2], lam_neg[:, 0:1], lam_c[:, 0:1], None, ALU.add))
            assert step.n == n_pre
            at = at + n_pre

            def keep_k(j, s):
                dve.wait_ge(qk_tr, JOBS * l + j + 1 + PRIME)
                nc.vector.tensor_copy(k_t[0:DK, s], ps[0:DK, 5]).then_inc(k_ev, 1)

            def score(j, qb, dilated):
                n = TB * j + qb
                table = mask[:, (TB - 1 - qb) * P:(TB - 1 - qb) * P + T] if dilated else zeros[:]
                dve.wait_ge(s_exp, MAPS * l + n + 1)
                dve.wait_ge(s_ps, MAPS * l + n + 1)
                dve.sem_inc(waited, 1)
                nc.vector.tensor_tensor_reduce(out=masked[:, qb % 2], in0=ps[:, qb % 2], in1=table, scale=1.0,
                                               scalar=-NEG, op0=ALU.add, op1=ALU.min,
                                               accum_out=neg_max[:, qb % 2:qb % 2 + 1]).then_inc(s_min, 1)

            def keep_pt(j, qb):
                dve.wait_ge(pt_ps, MAPS * l + TB * j + qb + 1 + PRIME)
                nc.vector.tensor_copy(p_t[:, qb % 2].rearrange("p k q -> p (k q)"),
                                      ps[:, 2 + qb % 2]).then_inc(pt_dve, 1)

            def job(j, s, kind, ahead):
                score(j, 2, kind)
                keep_pt(j, 0)
                if ahead is not None:
                    keep_k(j + 1, 1 - s)
                score(j, 3, kind)
                keep_pt(j, 1)
                if ahead is not None:
                    score(j + 1, 0, ahead)
                keep_pt(j, 2)
                if ahead is not None:
                    score(j + 1, 1, ahead)
                step.at(at + j)
                dve.wait_ge(s_exp, MAPS * l + TB * j + TB + PRIME)
                step.done(nc.vector.reciprocal(row_inv[:, s], row_sum[:, s]))
                step.wait()
                dve.wait_ge(pv_done, JOBS * l + j + 1 + PRIME)
                nc.vector.tensor_tensor(o_all[:, :, ds(j * VD, VD)],
                                        ps[:, 6 + s, 0:TB * VD].rearrange("p (t d) -> p t d", t=TB),
                                        row_inv[:, s].unsqueeze(2).to_broadcast([P, TB, VD]),
                                        ALU.mult).then_inc(o_ev, 1)

            plain = JA + JB
            keep_k(0, 0)
            score(0, 0, False)
            score(0, 1, False)
            with dve.Fori(0, plain // 2 - 1) as i:
                job(2 * i, 0, False, False)
                job(2 * i + 1, 1, False, False)
            job(plain - 2, 0, False, False)
            job(plain - 1, 1, False, True)
            with dve.Fori(plain // 2, JOBS // 2 - 1) as i:
                job(2 * i, 0, True, True)
                job(2 * i + 1, 1, True, True)
            job(JOBS - 2, 0, True, True)
            job(JOBS - 1, 1, True, None)
            at = at + JOBS
            step.at(at)
            dve.wait_ge(o_ev, JOBS * (l + 1) + PRIME)
            dve.wait_ge(k_ev, JOBS * (l + 1) + PRIME)
            dve.wait_ge(s_ps, MAPS * (l + 1))
            for tb in range(TB):
                pair = o_all[:, tb, 0:JA * VD].rearrange("p (h k d) -> p h k d", h=AH, k=2)
                last = nc.vector.scalar_tensor_tensor(out=o_f[:, tb], in0=pair[:, :, 1], scalar=lam_neg[:, 1:2],
                                                      in1=pair[:, :, 0], op0=ALU.mult, op1=ALU.add)
            step.done(last)
            step.wait()
            step.done(nc.vector.tensor_tensor(o_q, o_f, o_f, ALU.mult))
            step.wait()
            nc.vector.tensor_reduce(sub_sq[:], o_q.rearrange("p t h d -> p (t h) d"), AX_X, ALU.add).then_inc(sub_ss, 1)
            dve.wait_ge(sub_sd, l + 1)
            step.done(nc.vector.reciprocal(sub_inv[:], sub_rms[:]))
            step.wait()
            step.done(nc.vector.tensor_tensor(
                o_f.rearrange("p t h d -> p (t h) d"), o_f.rearrange("p t h d -> p (t h) d"),
                sub_inv[:].unsqueeze(2).to_broadcast([P, TB * AH, ADV]), ALU.mult))
            step.wait()
            nc.vector.tensor_tensor(o_all[:, :, A_W:2 * A_W].rearrange("p t (h d) -> p t h d", h=AH), o_f,
                                    sub_g[:].unsqueeze(1).unsqueeze(1).to_broadcast([P, TB, AH, ADV]),
                                    ALU.mult).then_inc(mix_ready, 1)
            assert step.n == n_sub
            at = at + n_sub
            rest_chunks(1)
            rest_group(IN_G, 0, DC * O_N)
            for k in range(O_G):
                if k + 1 < O_G:
                    rest_group(IN_G + k + 1, (k + 1) % 2, DC * O_N)
                for tb in range(TB):
                    dve.wait_ge(pj_ps, (W_PER * l + IN_G + k) * TB + tb + 1 + PRIME * TB)
                    xs = x_tok[:, tb, k * O_N:(k + 1) * O_N]
                    nc.vector.scalar_tensor_tensor(out=xs, in0=xs, scalar=ALPHA, in1=ps[:, TB * (k % 2) + tb, 0:O_N],
                                                   op0=ALU.mult, op1=ALU.add).then_inc(pj_res, 1)

            def layer_norm(u, at):
                step.at(at)
                for tb in range(TB):
                    for k in range(2):
                        last = nc.vector.bn_stats(bn[:, tb, k], x_tok[:, tb, k * 512:(k + 1) * 512])
                step.done(last)
                step.wait_apart(waited)
                for tb in range(TB):
                    last = nc.vector.bn_aggr(mean_var[:, tb], bn[:, tb])
                last.then_inc(ln_var, 1)
                dve.wait_ge(ln_sd, 2 * l + u + 1)
                step.done(nc.vector.reciprocal(ln_inv[:], ln_dev[:]))
                step.wait()
                dve.wait_ge(s_ln, 16 * (2 * l + u + 1))
                for tb in range(TB):
                    xs = x_tok[:, tb]
                    step.done(nc.vector.scalar_tensor_tensor(out=xs, in0=xs, scalar=mean_var[:, tb, 0:1],
                                                             in1=ln_rows[:, 0], op0=ALU.subtract, op1=ALU.mult))
                for tb in range(TB):
                    xs = x_tok[:, tb]
                    if tb == 0:
                        step.wait()
                    nc.vector.scalar_tensor_tensor(out=xs, in0=xs, scalar=ln_inv[:, tb:tb + 1], in1=ln_rows[:, 1],
                                                   op0=ALU.mult, op1=ALU.add).then_inc(ln_done, 1)
                assert step.n == n_ln

            dve.wait_ge(pj_res, O_G * TB * (l + 1))
            layer_norm(0, at)
            at = at + n_ln
            dve.wait_ge(keys_hi, l + 1)
            nc.vector.tensor_tensor(k_lo[:], keys[:], k_hi[:].bitcast(F32), ALU.subtract).then_inc(keys_lo, 1)
            rest_chunks(2)

            def rest_block(n):
                dve.wait_ge(st_h, ST_PER * l + n + 1)
                nc.vector.tensor_tensor(st_lo[:, 0].rearrange("p c f -> p (c f)"), st_raw[:, 0],
                                        st_hi[:, 0].rearrange("p c f -> p (c f)").bitcast(F32),
                                        ALU.subtract).then_inc(st_l[0], 1)

            def rest_query(f, s):
                dve.wait_ge(pq_h, QB * l + f + 1)
                nc.vector.tensor_tensor(pq_lo[:, s], ps[:, s], pq_hi[:, s].bitcast(F32), ALU.subtract).then_inc(pq_l, 1)

            step.at(at)
            step.done(nc.vector.tensor_copy(opt16[:].rearrange("p a b c -> p (a b) c"),
                                            iota[:, 0:TOPK].unsqueeze(1).to_broadcast([P, 2 * TOPK, TOPK])))
            at = at + 1
            rest_block(0)
            with dve.Fori(0, QB // 2) as i:
                rest_query(2 * i, 0)
                rest_block(2 * i + 2)
                rest_query(2 * i + 1, 1)
            dve.wait_ge(sc_ev, QB * (l + 1) + PRIME)
            dve.sem_inc(waited, 1)

            def top16(sets):
                for values, idx, spare, src in sets:
                    step.done(nc.vector.max(values[:, 0:8], src))
                step.wait_apart(waited)
                for values, idx, spare, src in sets:
                    step.done(nc.vector.max_index(idx[:, 0:8], values[:, 0:8], src))
                    step.done(nc.vector.match_replace(spare, values[:, 0:8], src, NEG))
                step.wait_apart(waited)
                for values, idx, spare, src in sets:
                    step.done(nc.vector.max(values[:, 8:16], spare))
                step.wait_apart(waited)
                for values, idx, spare, src in sets:
                    step.done(nc.vector.max_index(idx[:, 8:16], values[:, 8:16], spare))

            with dve.Fori(0, UNITS) as i:
                step.at(at + n_unit * i)
                step.done(nc.vector.tensor_copy(wk[:].rearrange("p a b -> p (a b)"),
                                                scores[:, ds(i, 1)].rearrange("p u a b -> p (u a b)")))
                step.wait_apart(waited)
                top16([(v16[:, k], x16[:, k], wk2[:, k], wk[:, k]) for k in range(2)])
                step.wait()
                step.done(nc.vector.tensor_copy(x16f[:].rearrange("p a b -> p (a b)"),
                                                x16[:].rearrange("p a b -> p (a b)")))
                step.done(nc.vector.tensor_tensor(cand[:], v16[:, 0].unsqueeze(2).to_broadcast([P, TOPK, TOPK]),
                                                  v16[:, 1].unsqueeze(1).to_broadcast([P, TOPK, TOPK]), ALU.add))
                rest_block(2 * i + QB + 2)
                step.wait_apart(waited)
                top16([(c16, ci, cand2[:], cand[:].rearrange("p a b -> p (a b)"))])
                step.wait()
                step.done(nc.vector.tensor_scalar(cab[:, 0], ci[:], 4, None, ALU.logical_shift_right))
                step.done(nc.vector.tensor_scalar(cab[:, 1], ci[:], TOPK - 1, None, ALU.bitwise_and))
                step.done(nc.vector.tensor_copy(c_all[:, ds(i, 1)], c16[:].unsqueeze(1)))
                step.wait()
                step.done(nc.vector.tensor_copy(cabf[:].rearrange("p a b -> p (a b)"),
                                                cab[:].rearrange("p a b -> p (a b)")))
                step.wait()
                ab = "p a b c -> p (a b) c"
                step.done(nc.vector.tensor_tensor(
                    eq[:].rearrange(ab), opt16[:].rearrange(ab),
                    cabf[:].rearrange("p a b -> p (a b)").unsqueeze(2).to_broadcast([P, 2 * TOPK, TOPK]),
                    ALU.is_equal))
                step.wait()
                step.done(nc.vector.tensor_tensor(
                    eq[:], eq[:], x16f[:].unsqueeze(2).to_broadcast([P, 2, TOPK, TOPK]), ALU.mult))
                step.wait()
                step.done(nc.vector.tensor_reduce(i_all[:, :, ds(i * TOPK, TOPK)], eq[:], AX_X, ALU.add))
                step.wait()
                assert step.n == n_unit
            at = at + n_unit * UNITS
            step.at(at)
            step.done(nc.vector.tensor_copy(c_top[:].unsqueeze(2), c_all[:, :, 0:1]))
            step.wait()
            nc.vector.tensor_tensor(c_all[:], c_all[:], c_top[:].unsqueeze(2).to_broadcast([P, UNITS, TOPK]),
                                    ALU.subtract).then_inc(gate_sub, 1)
            dve.wait_ge(gate_exp, l + 1)
            step.done(nc.vector.tensor_reduce(z_all[:, 0], e_all[:], AX_X, ALU.add))
            step.wait()
            step.done(nc.vector.reciprocal(z_all[:, 1], z_all[:, 0]))
            step.wait()
            nc.vector.tensor_tensor(e_all[:], e_all[:], z_all[:, 1].unsqueeze(2).to_broadcast([P, UNITS, TOPK]),
                                    ALU.mult).then_inc(gate_ready, 1)
            assert step.n == n_gate
            at = at + n_gate
            dve.wait_ge(sel_act, 3 * (l + 1))
            dve.sem_inc(waited, 1)
            with dve.Fori(0, WIN * BODIES) as body:
                for g in range(GROUPS):
                    if g == GROUPS // 2:
                        rest_block(2 * (body + UNITS) + QB + 2)
                    dve.wait_ge(g_tok, T // GRP * l + GROUPS * body + g + 1)
                    for k in range(GRP * g, GRP * (g + 1)):
                        t = body * BODY_T + k
                        nc.vector.tensor_scalar(oh[:, k, 0], iota[:], i_t[:, 1, ds(t, 1)], None, ALU.is_equal)
                        last = nc.vector.tensor_scalar(oh[:, k, 1], iota[:], i_t[:, 0, ds(t, 1)], g_t[:, ds(t, 1)],
                                                       ALU.is_equal, ALU.mult)
                    last.then_inc(oh_ready, 1)

            def gated(b, s):
                i = (b - s) // 2
                dve.wait_ge(s_gh[s], (EB // 2 * l + i + 1) * 32)
                dve.wait_ge(g_ev, T // GRP * (l + 1) + GROUPS)
                nc.vector.tensor_tensor(w_f[:, s, 0:T_D], g_in[:, s], h_in[:, s, 0:T_D], ALU.mult)
                nc.vector.tensor_tensor(
                    w_f[:, s, T_D:T].rearrange("p (w o t) -> p w o t", w=2, o=1), g_stage[:, :, ds(b, 1), :],
                    h_in[:, s, T_D:T].rearrange("p (w o t) -> p w o t", w=2, o=1), ALU.mult).then_inc(wt_f, 1)
                dve.wait_ge(wt_h, EB * l + b + 1)
                nc.vector.tensor_tensor(wt_lo[:, s], w_f[:, s], wt_hi[:, s].bitcast(F32), ALU.subtract).then_inc(wt_l, 1)

            gated(0, 0)
            with dve.Fori(0, EB // 2 - 1) as i:
                gated(2 * i + 1, 1)
                rest_block(2 * i + QB + EB + 2)
                gated(2 * i + 2, 0)
            gated(EB - 1, 1)
            dve.wait_ge(st_used, ST_PER * (l + 1) + PRIME)
            for tb in range(TB):
                xs = x_tok[:, tb]
                last = nc.vector.scalar_tensor_tensor(
                    out=xs, in0=xs, scalar=ALPHA, in1=ps[:, 2 * tb:2 * tb + 2].rearrange("p b n -> p (b n)"),
                    op0=ALU.mult, op1=ALU.add)
            last.then_inc(ffn_done, 1)
            dve.wait_ge(ffn_done, l + 1)
            layer_norm(1, at)

    @block.tensor
    def _(pe):
        pe.sem_inc(pj_ps, PRIME * TB)
        pe.sem_inc(qk_tr, PRIME)
        pe.sem_inc(pt_ps, PRIME)
        pe.sem_inc(pv_done, PRIME)
        pe.sem_inc(st_used, PRIME)
        pe.sem_inc(g_tok, GROUPS)
        pe.wait_ge(s_x, 3 * 16)
        pe.wait_ge(eps_set, 2)

        def product(dst, lhs, rhs, first, last):
            nc.tensor.matmul(dst, lhs[0], rhs[0], start=first, stop=False)
            nc.tensor.matmul(dst, lhs[0], rhs[1], start=False, stop=False)
            return nc.tensor.matmul(dst, lhs[1], rhs[0], start=False, stop=last)

        with pe.Fori(0, L) as l:

            def turn(src):
                for c in range(DC):
                    for tb in range(TB):
                        last = nc.tensor.transpose(ps[:, c, tb * P:(tb + 1) * P], src[:, tb, c * P:(c + 1) * P],
                                                   ident[:])
                    last.then_inc(tr_ps, 1)

            def group(n, s, width):
                pe.wait_ge(wc_lo, W_PER * l + n + 1 + PRIME)
                for tb in range(TB):
                    rows = slice(tb * P, (tb + 1) * P)
                    for c in range(DC):
                        cols = slice(c * width, (c + 1) * width)
                        last = product(ps[:, TB * s + tb, 0:width], (t_hi[:, c, rows], t_lo[:, c, rows]),
                                       (w_hi[:, s, cols], w_lo[:, s, cols]), c == 0, c == DC - 1)
                    last.then_inc(pj_ps, 1)

            pe.wait_ge(ln_done, 2 * TB * l + PRIME)
            turn(x_tok)
            pe.wait_ge(tr_lo, DC * 3 * l + DC)
            pe.sem_inc(waited, 1)
            with pe.Fori(0, IN_G // 2) as i:
                for s in range(2):
                    n = 2 * i + s
                    pe.wait_ge(pj_act, 2 * (IN_G * l + n + 1))
                    pe.wait_ge(pj_dve, 2 * (IN_G * l + n + 1))
                    group(n, s, IN_N)
            pe.wait_ge(lat_ready, l + 1)
            for k in range(3):
                for tb in range(TB):
                    last = nc.tensor.transpose(ps[:, k, tb * P:(tb + 1) * P], lat_n[:, tb, k * P:(k + 1) * P], ident[:])
                last.then_inc(lat_tr, 1)
            pe.wait_ge(s_lay, 16 * 9 * (l + 1))
            pe.wait_ge(lat_ev, 3 * (l + 1))
            for tb in range(TB):
                bank = 4 * ((tb + 1) % 2)
                rows = slice(tb * P, (tb + 1) * P)
                if tb >= 2:
                    pe.wait_ge(lat_qev, TB * l + tb - 1)
                    pe.wait_ge(lat_kev, TB * l + tb - 1)
                w = UQ_W // 2
                for half in range(2):
                    for k in range(2):
                        last = nc.tensor.matmul(ps[:, bank + half, 0:w], lat_t[:, k, rows],
                                                w_uq[:, k, half * w:(half + 1) * w], start=k == 0, stop=k == 1)
                last.then_inc(lat_ps, 1)
                w = UKV_W // 2
                for half in range(2):
                    last = nc.tensor.matmul(ps[:, bank + 2 + half, 0:w], lat_t[:, 2, rows],
                                            w_ukv[:, half * w:(half + 1) * w], start=True, stop=True)
                last.then_inc(lat_ps, 1)
            pe.wait_ge(lat_qev, TB * (l + 1))
            pe.wait_ge(lat_kev, TB * (l + 1))

            def turn_qk(j, s):
                pe.wait_ge(rope_done, JOBS * l + j + 1)
                for k in range(2):
                    for tb in range(TB):
                        last = nc.tensor.transpose(ps[0:DK, 4 + k, tb * P:(tb + 1) * P], rq[:, s, tb, k], ident[:])
                last.then_inc(qk_tr, 1)

            def score(j, s, qb):
                if qb == 0:
                    pe.wait_ge(q_ev, JOBS * l + j + 1 + PRIME)
                    pe.wait_ge(k_ev, JOBS * l + j + 1 + PRIME)
                pe.wait_ge(s_min, MAPS * l + TB * j + qb + 1)
                nc.tensor.matmul(ps[:, qb % 2], q_t[0:DK, s, qb * P:(qb + 1) * P], k_t[0:DK, s], start=True,
                                 stop=True).then_inc(s_ps, 1)

            def turn_p(j, qb):
                pe.wait_ge(s_exp, MAPS * l + TB * j + qb + 1 + PRIME)
                for k in range(TB):
                    last = nc.tensor.transpose(ps[:, 2 + qb % 2, k * P:(k + 1) * P],
                                               probs[:, qb % 2, k * P:(k + 1) * P], ident[:])
                last.then_inc(pt_ps, 1)

            def values(j, s, qb):
                if qb == 0:
                    pe.wait_ge(o_ev, JOBS * l + j + 1)
                    pe.wait_ge(v_ready, JOBS * l + j + 1)
                if qb < 3:
                    pe.wait_ge(pt_dve, 3 * (JOBS * l + j) + qb + 1)
                else:
                    pe.wait_ge(pt_act, JOBS * l + j + 1)
                for k in range(TB):
                    last = nc.tensor.matmul(ps[:, 6 + s, qb * VD:(qb + 1) * VD], p_t[:, qb % 2, k], v_s[:, s, k],
                                            start=k == 0, stop=k == TB - 1)
                if qb == TB - 1:
                    last.then_inc(pv_done, 1)

            def job(j, s, ahead):
                score(j, s, 2)
                turn_p(j, 0)
                if ahead:
                    turn_qk(j + 1, 1 - s)
                score(j, s, 3)
                turn_p(j, 1)
                values(j, s, 0)
                if ahead:
                    score(j + 1, 1 - s, 0)
                turn_p(j, 2)
                values(j, s, 1)
                if ahead:
                    score(j + 1, 1 - s, 1)
                turn_p(j, 3)
                values(j, s, 2)
                values(j, s, 3)

            turn_qk(0, 0)
            score(0, 0, 0)
            score(0, 0, 1)
            with pe.Fori(0, JOBS // 2 - 1) as i:
                job(2 * i, 0, True)
                job(2 * i + 1, 1, True)
            job(JOBS - 2, 0, True)
            job(JOBS - 1, 1, False)
            pe.wait_ge(mix_ready, l + 1)
            turn(o_all[:, :, A_W:A_W + D])
            pe.wait_ge(tr_lo, DC * 3 * l + 2 * DC)
            for k in range(O_G):
                if k >= 2:
                    pe.wait_ge(pj_res, TB * (O_G * l + k - 1))
                group(IN_G + k, k % 2, O_N)
            pe.wait_ge(ln_done, 2 * TB * l + TB + PRIME)
            turn(x_tok)
            pe.wait_ge(tr_lo, DC * 3 * l + 3 * DC)
            pe.wait_ge(keys_lo, l + 1)
            pe.sem_inc(waited, 1)

            def stationary(m, s, dst):
                pe.wait_ge(st_l[s], ST_PER // 2 * l + m + 1 + 1)
                for c in range(DC):
                    last = product(dst, (st_hi[:, s, c], st_lo[:, s, c]), (t_hi[:, c], t_lo[:, c]), c == 0,
                                   c == DC - 1)
                last.then_inc(st_used, 1)

            def key_scores(f, s):
                pe.wait_ge(pq_l, QB * l + f + 1)
                pe.wait_ge(sc_ev, QB * l + f + 1)
                for tb in range(TB):
                    rows = slice(tb * P, (tb + 1) * P)
                    last = product(ps[:, 2 + s, tb * NK:(tb + 1) * NK], (pq_hi[:, s, rows], pq_lo[:, s, rows]),
                                   (k_hi[:, ds(f, 1)].rearrange("p o n -> p (o n)"),
                                    k_lo[:, ds(f, 1)].rearrange("p o n -> p (o n)")), True, True)
                last.then_inc(sc_ps, 1)

            with pe.Fori(0, QB // 2) as i:
                for s in range(2):
                    stationary(i, s, ps[:, s])
                for s in range(2):
                    key_scores(2 * i + s, s)

            def experts(m, s):
                pe.wait_ge(gelu_done, EB * l + 2 * m + s + 1)
                stationary(m + QB // 2, s, ps[:, s])

            with pe.Fori(0, UNITS) as i:
                for s in range(2):
                    experts(i, s)
            pe.wait_ge(gate_ready, l + 1)
            for k in range(3):
                src = e_all[:].rearrange("p u k -> p (u k)") if k == 2 else i_all[:, k]
                for tb in range(TB):
                    last = nc.tensor.transpose(ps[:, 5 + k, tb * P:(tb + 1) * P], src[:, tb * P:(tb + 1) * P], ident[:])
                last.then_inc(sel_tr, 1)

            with pe.Fori(0, WIN * BODIES) as body:
                for g in range(GROUPS):
                    if g % (GROUPS // 2) == 0:
                        experts(body + UNITS, g // (GROUPS // 2))
                    pe.wait_ge(g_ev, T // GRP * l + GROUPS * body + g + 1)
                    pe.wait_ge(oh_ready, T // GRP * l + GROUPS * body + g + 1)
                    for k in range(GRP):
                        last = nc.tensor.matmul(ps[:, 2 + g, k * P:(k + 1) * P], oh[:, GRP * g + k, 0],
                                                oh[:, GRP * g + k, 1], start=True, stop=True)
                    last.then_inc(g_tok, 1)
            pe.wait_ge(gelu_done, EB * (l + 1) + PRIME)
            pe.wait_ge(g_ev, T // GRP * (l + 1) + GROUPS)
            for bank in range(8):
                nc.tensor.matmul(ps[:, bank], zeros_bf[:, 0:P], zeros_bf[:, 0:T], start=True, stop=True,
                                 skip_group_check=True)
            with pe.Fori(0, EB // 2) as i:
                for s in range(2):
                    b = 2 * i + s
                    pe.wait_ge(st_l[s], ST_PER // 2 * l + (QB + EB) // 2 + i + 1 + 1)
                    pe.wait_ge(wt_l, EB * l + b + 1)
                    v_hi = st_hi[:, s].rearrange("p c f -> p (c f)")
                    v_lo = st_lo[:, s].rearrange("p c f -> p (c f)")
                    for tb in range(TB):
                        rows = slice(tb * P, (tb + 1) * P)
                        for w, v in ((wt_hi, v_hi), (wt_hi, v_lo), (wt_lo, v_hi)):
                            for half in range(2):
                                last = nc.tensor.matmul(ps[:, 2 * tb + half], w[:, s, rows],
                                                        v[:, half * 512:(half + 1) * 512], start=False,
                                                        stop=True, skip_group_check=True)
                    last.then_inc(st_used, 1)

    ctx.close()


def rope_table(width):
    half = width // 2
    inv = np.exp(np.float32(-math.log(10000.0)) * np.arange(half, dtype=np.float32) / np.float32(half))
    ang = np.arange(T, dtype=np.float32)[:, None] * inv.astype(np.float32)[None, :]
    cos, sin = np.cos(ang), np.sin(ang)
    both = np.stack([np.concatenate([cos, cos], 1), np.concatenate([-sin, sin], 1)])
    return np.ascontiguousarray(both.reshape(2, TB, P, width).transpose(2, 0, 1, 3).astype(np.float32))


def mask_table():
    delta = np.abs(np.arange(MASK_W)[None, :] - 3 * P - np.arange(P)[:, None])
    count = sum((delta % dil == 0) & (delta // dil <= window // (2 * dil))
                for window, dil in ((128, 1), (512, 4), (2048, 16)))
    return np.where(count > 0, -np.log(np.maximum(count, 1)), BIG).astype(np.float32)


def kernel(**inputs):
    import concourse.bacc as bacc
    from concourse.bass_utils import run_bass_kernel_spmd

    x = {k: np.asarray(v) for k, v in inputs.items()}

    def columns(w, groups):
        n_l, k, n = w.shape
        w = w.reshape(n_l, k // P, P, groups, n // groups).transpose(0, 3, 2, 1, 4)
        return w.reshape(n_l, groups, P, k // P * (n // groups))

    lam = [0.8 - 0.6 * math.exp(-0.3 * (k + 1)) for k in range(L)]
    gains = [x["mla_q_norm_g"][:, 0:P], x["mla_q_norm_g"][:, P:QR], x["mla_kv_norm_g"], x["mla_kv_norm_g"]]
    arrays = {
        "x": x["x"].reshape(TB, P, D).transpose(1, 0, 2),
        "ident": np.eye(P, dtype=np.float32),
        "iota": np.tile(np.arange(P, dtype=np.float32), (P, 1)),
        "rope32": rope_table(32), "rope64": rope_table(64), "mask": mask_table(),
        "lam_c": np.array([[-v, 1.0 - v] for v in lam], np.float32),
        "w_in": columns(x["w_in"], IN_G), "w_o": columns(x["w_o"], O_G),
        "mla_w_uq": x["mla_w_uq"].reshape(L, 2, P, UQ_W).transpose(0, 2, 1, 3),
        "mla_w_ukv": x["mla_w_ukv"], "g_lat": np.stack(gains, axis=-1),
        "diff_lambda": x["diff_lambda"], "diff_subln_g": x["diff_subln_g"],
        "ln1": np.stack([x["ln1_g"], x["ln1_b"]], 1), "ln2": np.stack([x["ln2_g"], x["ln2_b"]], 1),
        "peer_w_q": columns(x["peer_w_q"], QB),
        "peer_keys": x["peer_sub_keys"].transpose(0, 4, 1, 2, 3).reshape(L, P, QB, NK),
        "peer_u": x["peer_u"].reshape(L, EB, P, DC, P).transpose(0, 1, 4, 3, 2).reshape(L, EB, P, DC * P),
        "peer_v": x["peer_v"].reshape(L, EB, P, D),
    }
    nc = bacc.Bacc("TRN2", target_bir_lowering=False, num_devices=1)
    arrays = {f"in_{k}": np.ascontiguousarray(v) for k, v in arrays.items()}
    aps = {k[3:]: nc.dram_tensor(k, v.shape, mybir.dt.from_np(v.dtype), kind="ExternalInput").ap()
           for k, v in arrays.items()}
    out = nc.dram_tensor("out_tokens", (TB, P, D), F32, kind="ExternalOutput").ap()
    build(nc, aps, out.rearrange("t p d -> p t d"))
    r = run_bass_kernel_spmd(nc, [arrays], core_ids=[0])
    return r.results[0]["out_tokens"].reshape(1, T, D)
```

```python
import math
from contextlib import ExitStack

import numpy as np

import concourse.bass as bass
from concourse import mybir

F32 = mybir.dt.float32
F32R = mybir.dt.float32r
U32 = mybir.dt.uint32
BF16 = mybir.dt.bfloat16
ALU = mybir.AluOpType
ACT = mybir.ActivationFunctionType
AX_X = mybir.AxisListType.X
ds = bass.ds

P = 128
L = 2
T = 512
D = 1024
TB = T // P
DC = D // P
AH, ADK, ADV = 4, 32, 64
BH, BNOPE, BROPE, BV = 6, 64, 32, 64
QR, KVR = 256, 128
CH, CDK = 6, 64
A_W, C_W = AH * ADV, CH * CDK
COL_AQ, COL_AK, COL_AV = 0, 256, 512
COL_CQ = 768
COL_CKV = COL_CQ + QR
COL_KR = COL_CKV + KVR
COL_C = COL_KR + BROPE
IN_W = COL_C + 3 * C_W
UQ_W = BH * (BNOPE + BROPE)
UKV_W = BH * (BNOPE + BV)
PH, NK, TOPK = 8, 128, 16
NEXP = NK * NK
ALPHA = (2 * L) ** 0.25
LN_EPS = 1e-5

IN_G, IN_N = 8, IN_W // 8
O_G, O_N = 4, D // 4
W_PER = IN_G + O_G
JA, JB, JC = 2 * AH, BH, CH
JOBS = JA + JB + JC
DK = BNOPE + BROPE
VD = 64
MAPS = JOBS * TB
QB = 2 * PH
EB = NEXP // P
ST_PER = QB + 2 * EB
UNITS = TB * PH
WIN, WIN_T = 8, T // 8
GRP = 4
RING = 2
BODY_T = 16
GROUPS = BODY_T // GRP
BODIES = WIN_T // BODY_T
WIN_D = WIN // 2 - 1
T_D = 2 * WIN_D * WIN_T
assert IN_G * IN_N == IN_W and 2 * UNITS + 2 * WIN * BODIES == EB
PRIME = 2
LN_D = TB - 1
BIG = 1.0e30
NEG = -3.0e38
MASK_W = T + 3 * P


class Steps:

    def __init__(self, eng, sem):
        self.eng, self.sem, self.base, self.n = eng, sem, 0, 0

    def at(self, base):
        self.base, self.n = base, 0

    def done(self, ins):
        ins.then_inc(self.sem, 1)
        self.n += 1

    def wait(self):
        self.eng.wait_ge(self.sem, self.base + self.n)

    def wait_apart(self, waited):
        self.wait()
        self.eng.sem_inc(waited, 1)


def build(nc, a, out):
    ctx = ExitStack()
    base = (nc.sbuf_base + 63) // 64 * 64
    limit = nc.sbuf_usable_end

    class Region:
        def __init__(self, start):
            self.start, self.end = start, start

        def tile(self, name, shape, dt):
            size = int(np.prod(shape[1:])) * (2 if dt == BF16 else 4)
            t = nc.alloc_sbuf_tensor_at(name, list(shape), dt, offset=self.end)
            self.end += (size + 63) // 64 * 64
            assert self.end <= limit, (name, self.end, limit)
            return t

    keep = Region(base)
    x_tok = keep.tile("x_tok", [P, TB, D], F32)
    t_hi = keep.tile("t_hi", [P, DC, T], F32R)
    t_lo = keep.tile("t_lo", [P, DC, T], F32R)
    ident = keep.tile("ident", [P, P], F32)
    iota = keep.tile("iota", [P, P], F32)
    zeros = keep.tile("zeros", [P, T], F32)
    zeros_bf = zeros[:].bitcast(BF16)
    neg_max = keep.tile("neg_max", [P, 2], F32)
    row_sum = keep.tile("row_sum", [P, 2, TB], F32)
    row_inv = keep.tile("row_inv", [P, 2, TB], F32)
    lat_sq = keep.tile("lat_sq", [P, 2, TB], F32)
    lat_rms = keep.tile("lat_rms", [P, 2, TB], F32)
    lat_inv = keep.tile("lat_inv", [P, 2, TB], F32)
    sub_sq = keep.tile("sub_sq", [P, TB * AH], F32)
    sub_rms = keep.tile("sub_rms", [P, TB * AH], F32)
    sub_inv = keep.tile("sub_inv", [P, TB * AH], F32)
    lam_dot = keep.tile("lam_dot", [P, 2], F32)
    lam_exp = keep.tile("lam_exp", [P, 2], F32)
    lam_neg = keep.tile("lam_neg", [P, 2], F32)
    bn = keep.tile("bn", [P, TB, 2, 6], F32)
    mean_var = keep.tile("mean_var", [P, TB, 2], F32)
    ln_dev = keep.tile("ln_dev", [P, TB], F32)
    ln_inv = keep.tile("ln_inv", [P, TB], F32)
    ln_shift = keep.tile("ln_shift", [P, TB], F32)
    eps = keep.tile("eps", [P, 1], F32)
    warm = keep.tile("warm", [P, 1], F32)

    att = Region(keep.end)
    h = att.tile("h", [P, TB, IN_W], F32)
    w_raw = att.tile("w_raw", [P, 2, DC * IN_N], F32)
    ln_rows = nc.alloc_sbuf_tensor_at("ln_rows", [P, 2, D], F32, offset=att.end)
    ln_rows_at = att.end
    lat_n = nc.alloc_sbuf_tensor_at("lat_n", [P, TB, QR + KVR], F32, offset=att.end)
    q_b = att.tile("q_b", [P, TB, UQ_W], F32)
    kv_b = att.tile("kv_b", [P, TB, UKV_W], F32)
    o_all = att.tile("o_all", [P, TB, JOBS * VD], F32)
    w_uq = att.tile("w_uq", [P, 2, UQ_W], F32)
    w_ukv = att.tile("w_ukv", [P, UKV_W], F32)
    g_lat = att.tile("g_lat", [P, 4], F32)
    rope32 = att.tile("rope32", [P, 2, TB, 32], F32)
    rope64 = att.tile("rope64", [P, 2, TB, 64], F32)
    rope_a = att.tile("rope_a", [P, 2, TB, 2, ADK], F32)
    mask = att.tile("mask", [P, MASK_W], F32)
    lam_in = att.tile("lam_in", [P, 4, ADK], F32)
    sub_g = att.tile("sub_g", [P, ADV], F32)
    lam_c = att.tile("lam_c", [P, 2], F32)
    w_split = Region(att.end)
    w_hi = w_split.tile("w_hi", [P, 2, DC * IN_N], F32R)
    w_lo = w_split.tile("w_lo", [P, 2, DC * IN_N], F32R)
    hd = Region(att.end)
    lat_t = hd.tile("lat_t", [P, 3, T], F32)
    rq = hd.tile("rq", [P, 2, TB, 2, DK], F32)
    q_a, k_a = (nc.alloc_sbuf_tensor_at(n, [P, 2, T], F32R, offset=hd.end + k * 2 * T * 4)
                for k, n in enumerate(("q_a", "k_a")))
    q_t = hd.tile("q_t", [P, 2, T], F32)
    k_t = hd.tile("k_t", [P, 2, T], F32)
    v_s = hd.tile("v_s", [P, 2, TB, VD], F32)
    sc_s = hd.tile("sc_s", [P, 2], F32)
    masked = hd.tile("masked", [P, 2, T], F32)
    probs = hd.tile("probs", [P, 2, T], F32)
    p_t = hd.tile("p_t", [P, TB, TB, P], F32)
    rt_a = hd.tile("rt_a", [P, TB, 2, 64], F32)
    rt_b = hd.tile("rt_b", [P, TB, 2, 64], F32)
    rot = rt_a[:, :, :, 0:ADK]
    kpe = hd.tile("kpe", [P, TB, BROPE], F32)
    o_f = lat_t[:].rearrange("p t d -> p (t d)")[:, 0:TB * A_W].rearrange("p (t h d) -> p t h d", t=TB, h=AH)
    o_q = kv_b[:].rearrange("p t d -> p (t d)")[:, 0:TB * A_W].rearrange("p (t h d) -> p t h d", t=TB, h=AH)

    pr = Region(keep.end)
    st_raw = pr.tile("st_raw", [P, 2, DC * P], F32)
    st_hi = pr.tile("st_hi", [P, 2, DC, P], F32R)
    st_lo = pr.tile("st_lo", [P, 2, DC, P], F32R)
    h_out = pr.tile("h_out", [P, 2, T], F32)
    shared = pr.end
    keys = pr.tile("keys", [P, QB, NK], F32)
    pq = pr.tile("pq", [P, 2, T], F32)
    scores = pr.tile("scores", [P, UNITS, 2, NK], F32)
    tk = Region(pr.end)
    opt16 = tk.tile("opt16", [P, 2, TOPK, TOPK], BF16)
    wk = tk.tile("wk", [P, 2, NK], F32)
    wk2 = tk.tile("wk2", [P, 2, NK], F32)
    v16 = tk.tile("v16", [P, 2, TOPK], F32)
    x16 = tk.tile("x16", [P, 2, TOPK], U32)
    x16f = tk.tile("x16f", [P, 2, TOPK], F32)
    cand = tk.tile("cand", [P, TOPK, TOPK], F32)
    cand2 = tk.tile("cand2", [P, TOPK * TOPK], F32)
    c16 = tk.tile("c16", [P, TOPK], F32)
    ci = tk.tile("ci", [P, TOPK], U32)
    cab = tk.tile("cab", [P, 2, TOPK], U32)
    cabf = tk.tile("cabf", [P, 2, TOPK], BF16)
    eq = tk.tile("eq", [P, 2, TOPK, TOPK], F32)
    c_all = tk.tile("c_all", [P, UNITS, TOPK], F32)
    i_all = tk.tile("i_all", [P, 2, UNITS * TOPK], F32)
    e_all = tk.tile("e_all", [P, UNITS, TOPK], F32)
    c_top = tk.tile("c_top", [P, UNITS], F32)
    z_all = tk.tile("z_all", [P, 2, UNITS], F32)
    gb = Region(shared)
    i_t = gb.tile("i_t", [P, 2, T], F32)
    g_hi = gb.tile("g_hi", [P, T], F32R)
    g_lo = gb.tile("g_lo", [P, T], F32R)
    oh_2 = gb.tile("oh_2", [P, BODY_T, P], F32R)
    oh_1 = gb.tile("oh_1", [P, BODY_T, 2, P], F32R)
    vp = Region(ln_rows_at + 2 * D * 4)
    g_in = vp.tile("g_in", [P, 2, T_D], F32)
    h_in = vp.tile("h_in", [P, 2, T], F32)
    w_f = vp.tile("w_f", [P, 2, T], F32)
    wt_hi = vp.tile("wt_hi", [P, 2, T], F32R)
    wt_lo = vp.tile("wt_lo", [P, 2, T], F32R)
    g_rest = vp.tile("g_rest", [P, RING, NK, GRP], F32)
    ga = Region((limit - 2 * NK * WIN_T * 4) // 64 * 64)
    g_stage = ga.tile("g_stage", [P, 2, NK, WIN_T], F32)
    assert vp.end <= ga.start and gb.end <= ln_rows_at + 2 * D * 4

    ps = ctx.enter_context(nc.psum_tensor("ps", [P, 8, 512], F32))
    gates_d = nc.dram_tensor("gates_d", [EB, P, T_D], F32, kind="Internal").ap()
    gelu_d = nc.dram_tensor("gelu_d", [EB, P, T], F32, kind="Internal").ap()

    def sem(name):
        return ctx.enter_context(nc.semaphore(name))

    s_x = sem("s_x")
    consts_set = sem("consts_set")
    s_lay = sem("s_lay")
    s_keys, s_ln = sem("s_keys"), sem("s_ln")
    s_wraw = [sem(f"s_wraw{s}") for s in range(2)]
    s_straw = [sem(f"s_straw{s}") for s in range(2)]
    s_gh = [sem(f"s_gh{s}") for s in range(2)]
    s_hst = [sem(f"s_hst{s}") for s in range(2)]
    s_gst = [sem(f"s_gst{s}") for s in range(2)]
    s_out = sem("s_out")
    tr_ps, tr_hi, tr_lo = sem("tr_ps"), sem("tr_hi"), sem("tr_lo")
    wc_hi, wc_lo = sem("wc_hi"), sem("wc_lo")
    pj_ps, pj_act, pj_dve, pj_res = sem("pj_ps"), sem("pj_act"), sem("pj_dve"), sem("pj_res")
    lat_ss, lat_sd, lat_ready, lat_tr, lat_ev, lat_ps, lat_qev, lat_kev = (sem(n) for n in (
        "lat_ss", "lat_sd", "lat_ready", "lat_tr", "lat_ev", "lat_ps", "lat_qev", "lat_kev"))
    v_ready = sem("v_ready")
    rope_done, qk_tr, q_ev, k_ev, s_ps, s_min, s_exp, pt_ps, pt_dve, pt_act, pv_done, o_ev = (sem(n) for n in (
        "rope_done", "qk_tr", "q_ev", "k_ev", "s_ps", "s_min", "s_exp", "pt_ps", "pt_dve", "pt_act", "pv_done",
        "o_ev"))
    sub_q, sub_ss, sub_sd, sub_f, mix_ready = (sem(n) for n in ("sub_q", "sub_ss", "sub_sd", "sub_f", "mix_ready"))
    lam_s, lam_e = sem("lam_s"), sem("lam_e")
    ln_var, ln_sd, ln_scaled, ln_norm, ln_done, ln_tail = (sem(n) for n in (
        "ln_var", "ln_sd", "ln_scaled", "ln_norm", "ln_done", "ln_tail"))
    st_h, st_used = sem("st_h"), sem("st_used")
    st_l = [sem(f"st_l{s}") for s in range(2)]
    pq_ready, sc_ps, sc_ev = sem("pq_ready"), sem("sc_ps"), sem("sc_ev")
    warm_done, gelu_done = sem("warm_done"), sem("gelu_done")
    gate_sub, gate_exp, gate_ready, sel_tr, sel_act = (sem(n) for n in (
        "gate_sub", "gate_exp", "gate_ready", "sel_tr", "sel_act"))
    g_sum, oh_ready, g_tok, g_ev = sem("g_sum"), sem("oh_ready"), sem("g_tok"), sem("g_ev")
    wt_f, wt_h, wt_l = sem("wt_f"), sem("wt_h"), sem("wt_l")
    v_rows, ffn_done = sem("v_rows"), sem("ffn_done")
    waited = sem("waited")
    dve_step, pool_step = sem("dve_step"), sem("pool_step")

    def parts_of(g):
        return ps[:, 2 + 2 * (g % RING):4 + 2 * (g % RING)].rearrange("p b (t k n) -> p k n (b t)", k=2, n=NK)

    block = ctx.enter_context(nc.Block())

    @block.sync
    def _(sp):
        for dst, src in ((x_tok[:], a["x"]), (ident[:], a["ident"]), (iota[:], a["iota"])):
            sp.dma_start(dst, src).then_inc(s_x, 16)
        with sp.Fori(0, L) as l:
            sp.wait_ge(st_used, ST_PER * l + PRIME)

            def w_load(n, s, src):
                sp.wait_ge(wc_lo, W_PER * l + n + 1)
                sp.dma_start(w_raw[:, s, 0:src.shape[1]], src).then_inc(s_wraw[s], 16)

            for s in range(2):
                w_load(s, s, a["w_in"][l, s])
            for dst, src in (
                (w_uq[:], a["mla_w_uq"][l]), (w_ukv[:], a["mla_w_ukv"][l]), (g_lat[:], a["g_lat"][l]),
                (lam_in[:], a["diff_lambda"][l].partition_broadcast(P)),
                (sub_g[:], a["diff_subln_g"][l].partition_broadcast(P)),
                (lam_c[:], a["lam_c"][l].partition_broadcast(P)),
                (rope32[:], a["rope32"]), (rope64[:], a["rope64"]), (rope_a[:], a["rope_a"]), (mask[:], a["mask"]),
            ):
                sp.dma_start(dst, src).then_inc(s_lay, 16)
            with sp.Fori(1, IN_G // 2) as i:
                for s in range(2):
                    w_load(2 * i + s, s, a["w_in"][l, 2 * i + s])

            def st_load(m, s, src):
                sp.wait_ge(st_l[s], ST_PER // 2 * l + m + 1)
                sp.dma_start(st_raw[:, s], src).then_inc(s_straw[s], 16)

            for k in range(O_G):
                if k == 2:
                    sp.wait_ge(v_ready, (JOBS - JA) * (l + 1))
                    sp.dma_start(ln_rows[:], a["ln1"][l].partition_broadcast(P)).then_inc(s_ln, 16)
                    sp.dma_start(keys[:], a["peer_keys"][l]).then_inc(s_keys, 16)
                    for s in range(2):
                        st_load(0, s, a["peer_w_q"][l, s])
                w_load(IN_G + k, k % 2, a["w_o"][l, k])

            def gelu_store(i, s):
                sp.wait_ge(gelu_done, EB * l + 2 * i + s + 1 + PRIME)
                sp.dma_start(gelu_d[2 * i + s], h_out[:, s]).then_inc(s_hst[s], 16)

            def gated_load(i, s):
                sp.wait_ge(wt_f, EB * l + 2 * i + s + 1)
                sp.dma_start(g_in[:, s], gates_d[2 * i + s]).then_inc(s_gh[s], 16)
                sp.dma_start(h_in[:, s], gelu_d[2 * i + s]).then_inc(s_gh[s], 16)

            with sp.Fori(1, QB // 2) as i:
                for s in range(2):
                    st_load(i, s, a["peer_w_q"][l, 2 * i + s])
            for b in range(4):
                st_load(QB // 2 + b // 2, b % 2, a["peer_u"][l, b])
            with sp.Fori(0, EB // 2 - 2) as i:
                for s in range(2):
                    gelu_store(i, s)
                    st_load(i + QB // 2 + 2, s, a["peer_u"][l, 2 * i + 4 + s])
            for s in range(2):
                gelu_store(EB // 2 - 2, s)
                st_load((QB + EB) // 2, s, a["peer_v"][l, s])
            for s in range(2):
                sp.wait_ge(s_gst[s], 16 * (BODIES * WIN_D * (l + 1) + 1))
                sp.wait_ge(s_hst[s], 16 * (EB // 2 * l + 1 + 1))
                sp.sem_inc(waited, 1)
            for s in range(2):
                gated_load(0, s)
            for s in range(2):
                gelu_store(EB // 2 - 1, s)
            sp.wait_ge(g_tok, T // GRP * (l + 1) + GROUPS)
            sp.dma_start(ln_rows[:], a["ln2"][l].partition_broadcast(P)).then_inc(s_ln, 16)
            for s in range(2):
                sp.wait_ge(s_hst[s], 16 * (EB // 2 * (l + 1) + 1))
                sp.sem_inc(waited, 1)
            with sp.Fori(1, EB // 2) as i:
                for s in range(2):
                    st_load(i + (QB + EB) // 2, s, a["peer_v"][l, 2 * i + s])
                    gated_load(i, s)
        sp.wait_ge(ln_done, LN_D * 2 * L + LN_D)
        sp.wait_ge(ln_tail, 2 * L + 1)
        sp.dma_start(out, x_tok[:]).then_inc(s_out, 16)
        sp.wait_ge(s_out, 16)

    @block.gpsimd
    def _(pool):
        step = Steps(pool, pool_step)
        pool.sem_inc(st_l[1], 1)
        pool.sem_inc(wc_lo, PRIME)
        pool.sem_inc(ln_tail, 1)
        pool.sem_inc(g_sum, RING)
        n_a, n_b, n_c = 9, 7, 4
        n_mix = 2
        per = n_a * JA + 4 + n_b * JB + 2 + n_c * JC + n_mix + 2
        with pool.Fori(0, L) as l:
            def rest_group(n, s, size):
                pool.wait_ge(wc_hi, W_PER * l + n + 1)
                nc.gpsimd.tensor_tensor(w_lo[:, s, 0:size], w_raw[:, s, 0:size], w_hi[:, s, 0:size].bitcast(F32),
                                        ALU.subtract).then_inc(wc_lo, 1)

            with pool.Fori(0, IN_G // 2) as i:
                for s in range(2):
                    rest_group(2 * i + s, s, DC * IN_N)
            pool.wait_ge(pj_act, IN_G * 2 * (l + 1) + 2 * PRIME)
            pool.wait_ge(pj_dve, IN_G * 2 * (l + 1) + 2 * PRIME)
            pool.wait_ge(s_lay, 16 * 10 * (l + 1))
            at = per * l

            def slot_free(j):
                pool.wait_ge(qk_tr, JOBS * l + j + 1)
                pool.wait_ge(q_ev, JOBS * l + j + 1)

            def rotate(dst, src, first, second, table, w):
                nk = dst.shape[2]
                cos, sin = (table[:, k] if len(table.shape) == 5 else table[:, k].unsqueeze(2).to_broadcast([P, TB, nk, w])
                            for k in range(2))
                ta, tb_ = rt_a[:, :, 0:nk, 0:w], rt_b[:, :, 0:nk, 0:w]
                step.done(nc.gpsimd.tensor_tensor(ta, src, cos, ALU.mult))
                step.done(nc.gpsimd.tensor_tensor(tb_[:, :, :, 0:w // 2], second, sin[:, :, :, 0:w // 2], ALU.mult))
                step.done(nc.gpsimd.tensor_tensor(tb_[:, :, :, w // 2:w], first, sin[:, :, :, w // 2:w], ALU.mult))
                step.wait()
                step.done(nc.gpsimd.tensor_tensor(dst, ta, tb_, ALU.add))

            def rotate_pair(dst, col, width, j, w, table):
                v = h[:, :, col:col + 2 * width].rearrange("p t (k f) -> p t k f", k=2)
                half = w // 2
                rotate(dst, v[:, :, :, ds(j * w, w)], v[:, :, :, ds(j * w, half)],
                       v[:, :, :, ds(j * w + half, half)], table, w)

            def finish(j, s, dk, v_src):
                step.wait_apart(waited)
                nc.gpsimd.memset(sc_s[:, s:s + 1], 1.0 if dk is None else -dk ** -0.5).then_inc(rope_done, 1)
                if v_src is None:
                    return
                pool.wait_ge(pv_done, JOBS * l + j + 1)
                pool.sem_inc(waited, 1)
                nc.gpsimd.tensor_copy(v_s[:, s], v_src).then_inc(v_ready, 1)

            pool.sem_inc(waited, 1)
            with pool.Fori(0, AH) as i:
                for s in range(2):
                    j = 2 * i + s
                    step.at(at + n_a * j)
                    slot_free(j)
                    rotate_pair(rot, COL_AQ, COL_AK - COL_AQ, j, ADK, rope_a)
                    step.wait_apart(waited)
                    third = [slice(k * ADK, (k + 1) * ADK) for k in range(3)]
                    step.done(nc.gpsimd.tensor_copy(rq[:, s, :, :, third[0]].bitcast(F32R), rot))
                    step.done(nc.gpsimd.tensor_copy(rq[:, s, :, 0, third[2]].bitcast(F32R), rot[:, :, 0]))
                    step.done(nc.gpsimd.tensor_copy(rq[:, s, :, 1, third[1]].bitcast(F32R), rot[:, :, 1]))
                    step.wait()
                    for k in range(2):
                        step.done(nc.gpsimd.tensor_tensor(rq[:, s, :, k, third[1 + k]], rot[:, :, k],
                                                          rq[:, s, :, k, third[0]], ALU.subtract))
                    finish(j, s, None, None)
                    assert step.n == n_a
            at = at + n_a * JA
            step.at(at)
            pool.wait_ge(lat_qev, TB * (l + 1))
            pool.wait_ge(lat_kev, TB * (l + 1))
            kr = h[:, :, COL_KR:COL_KR + BROPE].unsqueeze(2)
            rotate(kpe[:].unsqueeze(2), kr, kr[:, :, :, 0:BROPE // 2], kr[:, :, :, BROPE // 2:BROPE], rope32, BROPE)
            step.wait_apart(waited)
            at = at + 4
            with pool.Fori(0, JB // 2) as i:
                for s in range(2):
                    j = 2 * i + s
                    step.at(at + n_b * j)
                    slot_free(j + JA)
                    qv = q_b[:].unsqueeze(2)
                    q0, kv0 = j * DK, j * (BNOPE + BV)
                    rotate(rq[:, s, :, 0:1, BNOPE:DK], qv[:, :, :, ds(q0 + BNOPE, BROPE)],
                           qv[:, :, :, ds(q0 + BNOPE, BROPE // 2)],
                           qv[:, :, :, ds(q0 + BNOPE + BROPE // 2, BROPE // 2)], rope32, BROPE)
                    step.done(nc.gpsimd.tensor_copy(rq[:, s, :, 0, 0:BNOPE], q_b[:, :, ds(q0, BNOPE)]))
                    step.done(nc.gpsimd.tensor_copy(rq[:, s, :, 1, 0:BNOPE], kv_b[:, :, ds(kv0, BNOPE)]))
                    step.done(nc.gpsimd.tensor_copy(rq[:, s, :, 1, BNOPE:DK], kpe[:]))
                    finish(j + JA, s, DK, kv_b[:, :, ds(kv0 + BNOPE, BV)])
                    assert step.n == n_b
            at = at + n_b * JB
            step.at(at)
            pool.wait_ge(qk_tr, JOBS * l + JA + JB + PRIME)
            pool.sem_inc(waited, 1)
            for s in range(2):
                step.done(nc.gpsimd.memset(rq[:, s, :, :, CDK:DK], 0.0))
            step.wait_apart(waited)
            at = at + 2
            with pool.Fori(0, JC // 2) as i:
                for s in range(2):
                    j = 2 * i + s
                    step.at(at + n_c * j)
                    slot_free(j + JA + JB)
                    rotate_pair(rq[:, s, :, :, 0:CDK], COL_C, C_W, j, CDK, rope64)
                    finish(j + JA + JB, s, CDK, h[:, :, ds(j * CDK + COL_C + 2 * C_W, CDK)])
                    assert step.n == n_c
            at = at + n_c * JC
            step.at(at)
            pool.wait_ge(o_ev, JOBS * l + JA + PRIME)
            pair = o_all[:, :, 0:JA * VD].rearrange("p t (h k d) -> p t h k d", h=AH, k=2)
            lam = lam_neg[:, 1:2].unsqueeze(2).unsqueeze(3).to_broadcast([P, TB, AH, ADV])
            step.done(nc.gpsimd.tensor_tensor(o_f, pair[:, :, :, 1], lam, ALU.mult))
            step.wait()
            step.done(nc.gpsimd.tensor_tensor(o_f, o_f, pair[:, :, :, 0], ALU.add))
            step.wait()
            nc.gpsimd.tensor_tensor(o_q, o_f, o_f, ALU.mult).then_inc(sub_q, 1)
            pool.wait_ge(sub_q, l + 1)
            nc.gpsimd.tensor_tensor(o_f, o_f, sub_g[:].unsqueeze(1).unsqueeze(1).to_broadcast([P, TB, AH, ADV]),
                                    ALU.mult).then_inc(sub_f, 1)
            assert step.n == n_mix
            for k in range(O_G):
                rest_group(IN_G + k, k % 2, DC * O_N)

            def norm_tail(u):
                xs = x_tok[:, TB - 1]
                pool.wait_ge(s_ln, 16 * (2 * l + u + 1))
                pool.wait_ge(ln_norm, 2 * l + u + 1)
                step.at(per * l + per - 2 + u)
                step.done(nc.gpsimd.tensor_tensor(xs, xs, ln_rows[:, 0], ALU.mult))
                step.wait()
                nc.gpsimd.tensor_tensor(xs, xs, ln_rows[:, 1], ALU.add).then_inc(ln_tail, 1)

            norm_tail(0)

            def rest_block(m, s):
                pool.wait_ge(st_h, ST_PER * l + 2 * m + s + 1)
                nc.gpsimd.tensor_tensor(st_lo[:, s].rearrange("p c f -> p (c f)"), st_raw[:, s],
                                        st_hi[:, s].rearrange("p c f -> p (c f)").bitcast(F32),
                                        ALU.subtract).then_inc(st_l[s], 1)

            with pool.Fori(0, QB // 2 + 1) as m:
                rest_block(m, 1)
            with pool.Fori(QB // 2 + 1, QB // 2 + UNITS + 2) as m:
                for s in range(2):
                    rest_block(m, s)

            def add_rest(sw, q, body, g):
                pool.wait_ge(g_ev, T // GRP * l + GROUPS * body + g + 1 + RING)
                pool.sem_inc(waited, 1)
                dst = g_stage[:, sw, :, ds(q * BODY_T + GRP * g, GRP)]
                nc.gpsimd.tensor_tensor(dst, dst, g_rest[:, g % RING], ALU.add).then_inc(g_sum, 1)

            def sum_body(w, sw, q):
                body = w * BODIES + q
                for s in range(2):
                    for g in range(s * GROUPS // 2, (s + 1) * GROUPS // 2):
                        add_rest(sw, q, body, g)
                    rest_block(body + UNITS + QB // 2 + 2, s)

            with pool.Fori(0, WIN_D) as w2:
                for sw in range(2):
                    with pool.Fori(0, BODIES) as q:
                        sum_body(2 * w2 + sw, sw, q)
            with pool.Fori(0, BODIES) as q:
                sum_body(WIN - 2, 0, q)
            with pool.Fori(0, BODIES - 1) as q:
                sum_body(WIN - 1, 1, q)
            with pool.Fori((QB + EB) // 2 + 1, ST_PER // 2) as m:
                rest_block(m, 1)
            norm_tail(1)

    @block.scalar
    def _(act):
        act.sem_inc(q_ev, PRIME)
        act.sem_inc(pt_act, 1)
        act.sem_inc(s_exp, PRIME)
        act.sem_inc(pj_act, 2 * PRIME)
        act.sem_inc(gelu_done, PRIME)
        act.sem_inc(sc_ev, PRIME)
        act.sem_inc(g_ev, RING)
        act.sem_inc(warm_done, 1)
        for s in range(2):
            act.sem_inc(s_gst[s], 16)
            act.sem_inc(s_hst[s], 16)
        act.wait_ge(consts_set, 1)
        with act.Fori(0, L) as l:

            def round_chunks(u):
                for c in range(DC):
                    act.wait_ge(tr_ps, DC * (3 * l + u) + c + 1)
                    nc.scalar.copy(t_hi[:, c], ps[:, c]).then_inc(tr_hi, 1)

            def round_group(n, s, size):
                act.wait_ge(s_wraw[s], 16 * (W_PER // 2 * l + (n - s) // 2 + 1))
                act.wait_ge(pj_ps, TB * (W_PER * l + n + 1))
                nc.scalar.copy(w_hi[:, s, 0:size], w_raw[:, s, 0:size]).then_inc(wc_hi, 1)

            def keep_h(n, s):
                for tb in range(TB // 2):
                    act.wait_ge(pj_ps, (W_PER * l + n) * TB + tb + 1 + PRIME * TB)
                    nc.scalar.copy(h[:, tb, ds(n * IN_N, IN_N)], ps[:, TB * s + tb, 0:IN_N]).then_inc(pj_act, 1)

            round_group(0, 0, DC * IN_N)
            round_chunks(0)
            with act.Fori(0, IN_G // 2 - 1) as i:
                round_group(2 * i + 1, 1, DC * IN_N)
                keep_h(2 * i, 0)
                round_group(2 * i + 2, 0, DC * IN_N)
                keep_h(2 * i + 1, 1)
            round_group(IN_G - 1, 1, DC * IN_N)
            act.wait_ge(lat_ss, l + 1)
            nc.scalar.activation(lat_rms[:, 0], lat_sq[:, 0], ACT.Sqrt, bias=eps[:], scale=1.0 / QR)
            nc.scalar.activation(lat_rms[:, 1], lat_sq[:, 1], ACT.Sqrt, bias=eps[:], scale=1.0 / KVR).then_inc(lat_sd, 1)
            keep_h(IN_G - 2, 0)
            keep_h(IN_G - 1, 1)
            act.wait_ge(s_lay, 16 * 10 * (l + 1))
            for k in range(3):
                act.wait_ge(lat_tr, 3 * l + k + 1)
                nc.scalar.activation(lat_t[:, k], ps[:, k], ACT.Copy, scale=g_lat[:, k:k + 1]).then_inc(lat_ev, 1)
            for tb in range(TB):
                bank = 4 * ((tb + 1) % 2)
                act.wait_ge(lat_ps, 2 * TB * l + 2 * tb + 1)
                nc.scalar.copy(q_b[:, tb].rearrange("p (k f) -> p k f", k=2),
                               ps[:, bank:bank + 2, 0:UQ_W // 2]).then_inc(lat_qev, 1)
            act.wait_ge(lam_s, l + 1)
            nc.scalar.activation(lam_exp[:], lam_dot[:], ACT.Exp).then_inc(lam_e, 1)

            def scale_q(j, s, split):
                act.wait_ge(qk_tr, JOBS * l + j + 1 + PRIME)
                nc.scalar.activation((q_a if split else q_t)[0:DK, s], ps[0:DK, 4], ACT.Copy,
                                     scale=sc_s[0:DK, s:s + 1]).then_inc(q_ev, 1)

            def exponent(j, s, qb):
                n = TB * j + qb
                act.wait_ge(s_min, MAPS * l + n + 1 + PRIME)
                act.wait_ge(pt_ps, MAPS * l + n + 1)
                nc.scalar.activation(probs[:, qb % 2], masked[:, qb % 2], ACT.Exp, bias=neg_max[:, qb % 2:qb % 2 + 1],
                                     scale=-1.0, accum_out=row_sum[:, s, qb:qb + 1]).then_inc(s_exp, 1)

            def keep_pt(j, qb):
                act.wait_ge(pt_ps, MAPS * l + TB * j + qb + 1 + PRIME)
                nc.scalar.copy(p_t[:, qb].rearrange("p k q -> p (k q)"), ps[:, 2 + qb % 2]).then_inc(pt_act, 1)

            def job(j, s, ahead):
                exponent(j, s, 2)
                if ahead is not None:
                    scale_q(j + 1, 1 - s, ahead)
                exponent(j, s, 3)
                keep_pt(j, 1)
                if ahead is not None:
                    exponent(j + 1, 1 - s, 0)
                    exponent(j + 1, 1 - s, 1)
                keep_pt(j, 3)

            scale_q(0, 0, True)
            exponent(0, 0, 0)
            exponent(0, 0, 1)
            with act.Fori(0, JA // 2 - 1) as i:
                job(2 * i, 0, True)
                job(2 * i + 1, 1, True)
            job(JA - 2, 0, True)
            job(JA - 1, 1, False)
            with act.Fori(JA // 2, JOBS // 2 - 1) as i:
                job(2 * i, 0, False)
                job(2 * i + 1, 1, False)
            job(JOBS - 2, 0, False)
            job(JOBS - 1, 1, None)
            act.wait_ge(sub_ss, l + 1)
            nc.scalar.activation(sub_rms[:], sub_sq[:], ACT.Sqrt, bias=eps[:], scale=1.0 / ADV).then_inc(sub_sd, 1)
            act.wait_ge(mix_ready, l + 1)
            round_group(IN_G, 0, DC * O_N)
            round_chunks(1)
            for k in range(1, O_G):
                round_group(IN_G + k, k % 2, DC * O_N)

            def round_block(m, s):
                act.wait_ge(s_straw[s], (ST_PER // 2 * l + m + 1) * 16)
                act.wait_ge(st_used, ST_PER * l + 2 * m + s + 1)
                nc.scalar.copy(st_hi[:, s].rearrange("p c f -> p (c f)"), st_raw[:, s]).then_inc(st_h, 1)

            round_block(0, 0)

            def deviation(u):
                act.wait_ge(ln_var, 2 * l + u + 1)
                nc.scalar.activation(ln_dev[:], mean_var[:, :, 1], ACT.Sqrt, bias=eps[:]).then_inc(ln_sd, 1)
                act.wait_ge(ln_scaled, 2 * l + u + 1)
                nc.scalar.activation(x_tok[:, TB - 1], x_tok[:, TB - 1], ACT.Identity, bias=ln_shift[:, TB - 1:TB],
                                     scale=ln_inv[:, TB - 1:TB]).then_inc(ln_norm, 1)

            deviation(0)
            round_chunks(2)

            def keep_query(f, s):
                act.wait_ge(st_used, ST_PER * l + f + 1 + PRIME)
                nc.scalar.copy(pq[:, s], ps[:, s]).then_inc(pq_ready, 1)

            def keep_scores(f, s):
                act.wait_ge(sc_ps, QB * l + f + 1)
                dst = scores[:].rearrange("p (t h) k n -> p t (h k) n", t=TB)[:, :, ds(f, 1), :]
                nc.scalar.copy(dst, ps[:, 2 + s].rearrange("p (t o n) -> p t o n", t=TB, o=1)).then_inc(sc_ev, 1)

            def gelu(m, s):
                b = 2 * m + s
                act.wait_ge(st_used, ST_PER * l + QB + b + 1 + PRIME)
                act.wait_ge(s_hst[s], (EB // 2 * l + m + 1) * 16)
                nc.scalar.activation(h_out[:, s], ps[:, s], ACT.Gelu).then_inc(gelu_done, 1)

            with act.Fori(0, QB // 2) as i:
                round_block(i, 1)
                keep_query(2 * i, 0)
                round_block(i + 1, 0)
                keep_query(2 * i + 1, 1)
                keep_scores(2 * i, 0)
                keep_scores(2 * i + 1, 1)
            def load_table(n):
                act.wait_ge(warm_done, EB // 2 * l + n + 1)
                nc.scalar.activation(warm[:], eps[:], ACT.Gelu).then_inc(warm_done, 1)

            round_block(QB // 2, 1)
            with act.Fori(0, UNITS) as i:
                load_table(i)
                for s in range(2):
                    gelu(i, s)
                    round_block(i + QB // 2 + 1, s)
            act.wait_ge(gate_sub, l + 1)
            nc.scalar.activation(e_all[:], c_all[:], ACT.Exp).then_inc(gate_exp, 1)
            load_table(UNITS)
            gelu(UNITS, 0)
            round_block(UNITS + QB // 2 + 1, 0)
            for k in range(3):
                act.wait_ge(sel_tr, 3 * l + k + 1)
                nc.scalar.copy(g_hi[:] if k == 2 else i_t[:, k], ps[:, 5 + k]).then_inc(sel_act, 1)
            gelu(UNITS, 1)
            round_block(UNITS + QB // 2 + 1, 1)

            def keep_gates(sw, q, body, g):
                act.wait_ge(g_tok, T // GRP * l + GROUPS * body + g + 1 + GROUPS)
                act.wait_ge(g_sum, T // GRP * l + GROUPS * body + g + 1)
                parts = parts_of(g)
                nc.scalar.copy(g_stage[:, sw, :, ds(q * BODY_T + GRP * g, GRP)], parts[:, 0])
                nc.scalar.copy(g_rest[:, g % RING], parts[:, 1]).then_inc(g_ev, 1)

            def stage_body(w, sw, q, store):
                body = w * BODIES + q
                load_table(body + UNITS + 1)
                if store:
                    n_q = NK // BODIES
                    act.wait_ge(g_sum, T // GRP * l + WIN_T // GRP * w + RING)
                    act.dma_start(gates_d[ds(q * n_q, n_q), :, ds(w * WIN_T - WIN_T, WIN_T)].rearrange("n p t -> p n t"),
                                  g_stage[:, 1 - sw, ds(q * n_q, n_q)]).then_inc(s_gst[1 - sw], 16)
                act.wait_ge(s_gst[sw], (BODIES * (WIN_D * l + (w - sw) // 2) + 1) * 16)
                for s in range(2):
                    for g in range(s * GROUPS // 2, (s + 1) * GROUPS // 2):
                        keep_gates(sw, q, body, g)
                    gelu(body + UNITS + 1, s)
                    round_block(body + UNITS + QB // 2 + 2, s)

            with act.Fori(0, BODIES) as q:
                stage_body(0, 0, q, False)
            with act.Fori(0, WIN_D) as w2:
                with act.Fori(0, BODIES) as q:
                    stage_body(2 * w2 + 1, 1, q, True)
                with act.Fori(0, BODIES) as q:
                    stage_body(2 * w2 + 2, 0, q, True)
            with act.Fori(0, BODIES - 1) as q:
                stage_body(WIN - 1, 1, q, False)
            for g in range(GROUPS):
                act.wait_ge(g_tok, T // GRP * (l + 1) - GROUPS + g + 1 + GROUPS)
                nc.scalar.copy(g_stage[:, 1, :, (BODIES - 1) * BODY_T + GRP * g:(BODIES - 1) * BODY_T + GRP * (g + 1)],
                               parts_of(g)[:, 0]).then_inc(g_ev, 1)

            def round_gated(b, s):
                act.wait_ge(wt_f, EB * l + b + 1 + PRIME)
                act.wait_ge(st_used, ST_PER * l + QB + EB + b + 1)
                nc.scalar.copy(wt_hi[:, s], w_f[:, s]).then_inc(wt_h, 1)

            round_gated(0, 0)
            with act.Fori(0, EB // 2 - 1) as i:
                for s in range(2):
                    round_gated(2 * i + s + 1, 1 - s)
                    round_block(i + (QB + EB) // 2 + 1, s)
            round_gated(EB - 1, 1)
            deviation(1)

    @block.vector
    def _(dve):
        step = Steps(dve, dve_step)
        dve.sem_inc(pj_dve, 2 * PRIME)
        dve.sem_inc(k_ev, PRIME)
        dve.sem_inc(pt_dve, 1)
        dve.sem_inc(s_min, PRIME)
        dve.sem_inc(o_ev, PRIME)
        dve.sem_inc(st_l[0], 1)
        dve.sem_inc(wt_f, PRIME)
        dve.sem_inc(ln_done, LN_D)
        nc.vector.memset(eps[:], LN_EPS).then_inc(consts_set, 1)
        nc.vector.memset(zeros[:], 0.0).then_inc(consts_set, 1)
        n_pre, n_sub, n_ln, n_unit, n_gate = 4, 1, 2 + LN_D, 25, 4
        per = n_pre + JOBS + n_sub + 2 * n_ln + 1 + UNITS * n_unit + n_gate
        with dve.Fori(0, L) as l:
            at = per * l

            def rest_chunks(u):
                for c in range(DC):
                    dve.wait_ge(tr_hi, DC * (3 * l + u) + c + 1)
                    nc.vector.tensor_tensor(t_lo[:, c], ps[:, c], t_hi[:, c].bitcast(F32),
                                            ALU.subtract).then_inc(tr_lo, 1)

            def rest_block(n):
                dve.wait_ge(st_h, ST_PER * l + n + 1)
                nc.vector.tensor_tensor(st_lo[:, 0].rearrange("p c f -> p (c f)"), st_raw[:, 0],
                                        st_hi[:, 0].rearrange("p c f -> p (c f)").bitcast(F32),
                                        ALU.subtract).then_inc(st_l[0], 1)

            def keep_h(n, s):
                for tb in range(TB // 2, TB):
                    dve.wait_ge(pj_ps, (W_PER * l + n) * TB + tb + 1 + PRIME * TB)
                    nc.vector.tensor_copy(h[:, tb, ds(n * IN_N, IN_N)], ps[:, TB * s + tb, 0:IN_N]).then_inc(pj_dve, 1)

            rest_chunks(0)
            with dve.Fori(0, IN_G // 2 - 1) as i:
                keep_h(2 * i, 0)
                keep_h(2 * i + 1, 1)
            step.at(at)
            dve.wait_ge(s_lay, 16 * 10 * (l + 1))
            for k in range(2):
                ins = nc.vector.tensor_tensor_reduce(out=lam_in[:, 2 * k], in0=lam_in[:, 2 * k],
                                                     in1=lam_in[:, 2 * k + 1], scale=1.0, scalar=0.0, op0=ALU.mult,
                                                     op1=ALU.add, accum_out=lam_dot[:, k:k + 1])
            ins.then_inc(lam_s, 1)
            step.done(nc.vector.tensor_scalar(sub_g[:], sub_g[:], lam_c[:, 1:2], None, ALU.mult))
            assert COL_KR <= (IN_G - 2) * IN_N
            dve.wait_ge(pj_act, 2 * (IN_G * (l + 1) - 2) + 2 * PRIME)
            dve.wait_ge(pj_dve, 2 * (IN_G * (l + 1) - 2) + 2 * PRIME)
            for tb in range(TB):
                for k, (c0, w) in enumerate(((COL_CQ, QR), (COL_CKV, KVR))):
                    src = h[:, tb, c0:c0 + w]
                    ins = nc.vector.tensor_tensor_reduce(out=lat_n[:, tb, k * QR:k * QR + w], in0=src, in1=src,
                                                         scale=1.0, scalar=0.0, op0=ALU.mult, op1=ALU.add,
                                                         accum_out=lat_sq[:, k, tb:tb + 1])
            ins.then_inc(lat_ss, 1)
            dve.wait_ge(lat_sd, l + 1)
            step.done(nc.vector.reciprocal(lat_inv[:], lat_rms[:]))
            step.wait()
            for tb in range(TB):
                for k, (c0, w) in enumerate(((COL_CQ, QR), (COL_CKV, KVR))):
                    ins = nc.vector.tensor_scalar(lat_n[:, tb, k * QR:k * QR + w], h[:, tb, c0:c0 + w],
                                                  lat_inv[:, k, tb:tb + 1], None, ALU.mult)
            ins.then_inc(lat_ready, 1)
            keep_h(IN_G - 2, 0)
            keep_h(IN_G - 1, 1)
            for tb in range(TB):
                bank = 4 * ((tb + 1) % 2) + 2
                dve.wait_ge(lat_ps, 2 * TB * l + 2 * tb + 2)
                nc.vector.tensor_copy(kv_b[:, tb].rearrange("p (k f) -> p k f", k=2),
                                      ps[:, bank:bank + 2, 0:UKV_W // 2]).then_inc(lat_kev, 1)
            dve.wait_ge(lam_e, l + 1)
            step.done(nc.vector.tensor_tensor(lam_neg[:, 0:1], lam_exp[:, 1:2], lam_exp[:, 0:1], ALU.subtract))
            step.wait()
            step.done(nc.vector.tensor_scalar(lam_neg[:, 1:2], lam_neg[:, 0:1], lam_c[:, 0:1], None, ALU.add))
            assert step.n == n_pre
            at = at + n_pre

            def keep_k(j, s, kind):
                dve.wait_ge(qk_tr, JOBS * l + j + 1 + PRIME)
                nc.vector.tensor_copy((k_a if kind == "A" else k_t)[0:DK, s], ps[0:DK, 5]).then_inc(k_ev, 1)

            def score(j, qb, kind):
                n = TB * j + qb
                table = mask[:, (TB - 1 - qb) * P:(TB - 1 - qb) * P + T] if kind == "C" else zeros[:]
                dve.wait_ge(s_exp, MAPS * l + n + 1)
                dve.wait_ge(s_ps, MAPS * l + n + 1)
                dve.sem_inc(waited, 1)
                nc.vector.tensor_tensor_reduce(out=masked[:, qb % 2], in0=ps[:, qb % 2], in1=table, scale=1.0,
                                               scalar=-NEG, op0=ALU.add, op1=ALU.min,
                                               accum_out=neg_max[:, qb % 2:qb % 2 + 1]).then_inc(s_min, 1)

            def keep_pt(j, qb):
                dve.wait_ge(pt_ps, MAPS * l + TB * j + qb + 1 + PRIME)
                nc.vector.tensor_copy(p_t[:, qb].rearrange("p k q -> p (k q)"),
                                      ps[:, 2 + qb % 2]).then_inc(pt_dve, 1)

            def invert_sums(j, s):
                step.at(at + j)
                dve.wait_ge(s_exp, MAPS * l + TB * j + TB + PRIME)
                step.done(nc.vector.reciprocal(row_inv[:, s], row_sum[:, s]))

            def finish(j, s):
                step.wait()
                dve.wait_ge(pv_done, JOBS * l + j + 1 + PRIME)
                nc.vector.tensor_tensor(o_all[:, :, ds(j * VD, VD)],
                                        ps[:, 6 + s, 0:TB * VD].rearrange("p (t d) -> p t d", t=TB),
                                        row_inv[:, s].unsqueeze(2).to_broadcast([P, TB, VD]),
                                        ALU.mult).then_inc(o_ev, 1)

            def job(j, s, kind, ahead, before=True):
                score(j, 2, kind)
                keep_pt(j, 0)
                if ahead is not None:
                    keep_k(j + 1, 1 - s, ahead)
                score(j, 3, kind)
                if before:
                    invert_sums(j - 1, 1 - s)
                if ahead is not None:
                    score(j + 1, 0, ahead)
                if before:
                    finish(j - 1, 1 - s)
                keep_pt(j, 2)
                if ahead is not None:
                    score(j + 1, 1, ahead)

            keep_k(0, 0, "A")
            score(0, 0, "A")
            score(0, 1, "A")
            job(0, 0, "A", "A", before=False)
            job(1, 1, "A", "A")
            first = 1
            for kind, after, end in (("A", "B", JA // 2), ("B", "C", (JA + JB) // 2), ("C", None, JOBS // 2)):
                with dve.Fori(first, end - 1) as i:
                    job(2 * i, 0, kind, kind)
                    job(2 * i + 1, 1, kind, kind)
                job(2 * end - 2, 0, kind, kind)
                job(2 * end - 1, 1, kind, after)
                first = end
            dve.wait_ge(sub_q, l + 1)
            nc.vector.tensor_reduce(sub_sq[:], o_q.rearrange("p t h d -> p (t h) d"), AX_X, ALU.add).then_inc(sub_ss, 1)
            invert_sums(JOBS - 1, 1)
            finish(JOBS - 1, 1)
            at = at + JOBS
            step.at(at)
            dve.wait_ge(sub_sd, l + 1)
            step.done(nc.vector.reciprocal(sub_inv[:], sub_rms[:]))
            step.wait()
            dve.wait_ge(sub_f, l + 1)
            nc.vector.tensor_tensor(o_all[:, :, A_W:2 * A_W].rearrange("p t (h d) -> p t h d", h=AH), o_f,
                                    sub_inv[:].rearrange("p (t h) -> p t h", t=TB).unsqueeze(3).to_broadcast(
                                        [P, TB, AH, ADV]), ALU.mult).then_inc(mix_ready, 1)
            assert step.n == n_sub
            at = at + n_sub

            def row_stats(tb, half):
                return nc.vector.bn_stats(bn[:, tb, half], x_tok[:, tb, half * 512:(half + 1) * 512])

            rest_chunks(1)
            for k in range(O_G):
                if k == O_G // 2:
                    dve.wait_ge(pj_res, TB * (O_G * l + k))
                    for tb in range(TB):
                        row_stats(tb, 0)
                if k == O_G - 1:
                    rest_block(0)
                for tb in range(TB):
                    dve.wait_ge(pj_ps, (W_PER * l + IN_G + k) * TB + tb + 1 + PRIME * TB)
                    xs = x_tok[:, tb, k * O_N:(k + 1) * O_N]
                    nc.vector.scalar_tensor_tensor(out=xs, in0=xs, scalar=ALPHA, in1=ps[:, TB * (k % 2) + tb, 0:O_N],
                                                   op0=ALU.mult, op1=ALU.add).then_inc(pj_res, 1)
                    if k == O_G - 1:
                        dve.wait_ge(pj_res, TB * (O_G * l + k) + tb + 1)
                        last = row_stats(tb, 1)

            def layer_norm(u, at, last):
                step.at(at)
                step.done(last)
                step.wait_apart(waited)
                for tb in range(TB):
                    ins = nc.vector.bn_aggr(mean_var[:, tb], bn[:, tb])
                ins.then_inc(ln_var, 1)
                dve.wait_ge(ln_sd, 2 * l + u + 1)
                step.done(nc.vector.reciprocal(ln_inv[:], ln_dev[:]))
                step.wait()
                nc.vector.scalar_tensor_tensor(out=ln_shift[:], in0=mean_var[:, :, 0], scalar=-1.0, in1=ln_inv[:],
                                               op0=ALU.mult, op1=ALU.mult).then_inc(ln_scaled, 1)
                dve.wait_ge(s_ln, 16 * (2 * l + u + 1))
                for tb in range(LN_D):
                    xs = x_tok[:, tb]
                    step.done(nc.vector.scalar_tensor_tensor(out=xs, in0=xs, scalar=mean_var[:, tb, 0:1],
                                                             in1=ln_rows[:, 0], op0=ALU.subtract, op1=ALU.mult))
                step.wait()
                for tb in range(LN_D):
                    xs = x_tok[:, tb]
                    nc.vector.scalar_tensor_tensor(out=xs, in0=xs, scalar=ln_inv[:, tb:tb + 1], in1=ln_rows[:, 1],
                                                   op0=ALU.mult, op1=ALU.add).then_inc(ln_done, 1)
                assert step.n == n_ln

            layer_norm(0, at, last)
            at = at + n_ln
            rest_chunks(2)

            step.at(at)
            step.done(nc.vector.tensor_copy(opt16[:].rearrange("p a b c -> p (a b) c"),
                                            iota[:, 0:TOPK].unsqueeze(1).to_broadcast([P, 2 * TOPK, TOPK])))
            at = at + 1
            with dve.Fori(0, QB // 2) as i:
                rest_block(2 * i + 2)
            dve.wait_ge(sc_ev, QB * (l + 1) + PRIME)
            dve.sem_inc(waited, 1)

            def top16(sets):
                for values, idx, spare, src in sets:
                    step.done(nc.vector.max(values[:, 0:8], src))
                step.wait_apart(waited)
                for values, idx, spare, src in sets:
                    step.done(nc.vector.max_index(idx[:, 0:8], values[:, 0:8], src))
                    step.done(nc.vector.match_replace(spare, values[:, 0:8], src, NEG))
                step.wait_apart(waited)
                for values, idx, spare, src in sets:
                    step.done(nc.vector.max(values[:, 8:16], spare))
                step.wait_apart(waited)
                for values, idx, spare, src in sets:
                    step.done(nc.vector.max_index(idx[:, 8:16], values[:, 8:16], spare))

            with dve.Fori(0, UNITS) as i:
                step.at(at + n_unit * i)
                step.done(nc.vector.tensor_copy(wk[:].rearrange("p a b -> p (a b)"),
                                                scores[:, ds(i, 1)].rearrange("p u a b -> p (u a b)")))
                step.wait_apart(waited)
                top16([(v16[:, k], x16[:, k], wk2[:, k], wk[:, k]) for k in range(2)])
                step.wait()
                step.done(nc.vector.tensor_copy(x16f[:].rearrange("p a b -> p (a b)"),
                                                x16[:].rearrange("p a b -> p (a b)")))
                step.done(nc.vector.tensor_tensor(cand[:], v16[:, 0].unsqueeze(2).to_broadcast([P, TOPK, TOPK]),
                                                  v16[:, 1].unsqueeze(1).to_broadcast([P, TOPK, TOPK]), ALU.add))
                step.wait_apart(waited)
                top16([(c16, ci, cand2[:], cand[:].rearrange("p a b -> p (a b)"))])
                step.wait()
                step.done(nc.vector.tensor_scalar(cab[:, 0], ci[:], 4, None, ALU.logical_shift_right))
                step.done(nc.vector.tensor_scalar(cab[:, 1], ci[:], TOPK - 1, None, ALU.bitwise_and))
                step.done(nc.vector.tensor_copy(c_all[:, ds(i, 1)], c16[:].unsqueeze(1)))
                step.wait()
                step.done(nc.vector.tensor_copy(cabf[:].rearrange("p a b -> p (a b)"),
                                                cab[:].rearrange("p a b -> p (a b)")))
                step.wait()
                ab = "p a b c -> p (a b) c"
                step.done(nc.vector.tensor_tensor(
                    eq[:].rearrange(ab), opt16[:].rearrange(ab),
                    cabf[:].rearrange("p a b -> p (a b)").unsqueeze(2).to_broadcast([P, 2 * TOPK, TOPK]),
                    ALU.is_equal))
                step.wait()
                step.done(nc.vector.tensor_tensor(
                    eq[:], eq[:], x16f[:].unsqueeze(2).to_broadcast([P, 2, TOPK, TOPK]), ALU.mult))
                step.wait()
                step.done(nc.vector.tensor_reduce(i_all[:, :, ds(i * TOPK, TOPK)], eq[:], AX_X, ALU.add))
                step.wait()
                assert step.n == n_unit
            at = at + n_unit * UNITS
            step.at(at)
            step.done(nc.vector.tensor_copy(c_top[:].unsqueeze(2), c_all[:, :, 0:1]))
            step.wait()
            nc.vector.tensor_tensor(c_all[:], c_all[:], c_top[:].unsqueeze(2).to_broadcast([P, UNITS, TOPK]),
                                    ALU.subtract).then_inc(gate_sub, 1)
            dve.wait_ge(gate_exp, l + 1)
            step.done(nc.vector.tensor_reduce(z_all[:, 0], e_all[:], AX_X, ALU.add))
            step.wait()
            step.done(nc.vector.reciprocal(z_all[:, 1], z_all[:, 0]))
            step.wait()
            nc.vector.tensor_tensor(e_all[:], e_all[:], z_all[:, 1].unsqueeze(2).to_broadcast([P, UNITS, TOPK]),
                                    ALU.mult).then_inc(gate_ready, 1)
            dve.wait_ge(sel_act, 3 * (l + 1))
            step.done(nc.vector.tensor_tensor(g_lo[:], ps[:, 7], g_hi[:].bitcast(F32), ALU.subtract))
            step.wait_apart(waited)
            assert step.n == n_gate
            at = at + n_gate
            with dve.Fori(0, WIN * BODIES) as body:
                for g in range(GROUPS):
                    dve.wait_ge(g_tok, T // GRP * l + GROUPS * body + g + 1)
                    dve.sem_inc(waited, 1)
                    nc.vector.tensor_tensor(
                        oh_2[:, GRP * g:GRP * (g + 1)], iota[:].unsqueeze(1).to_broadcast([P, GRP, P]),
                        i_t[:, 1, ds(body * BODY_T + GRP * g, GRP)].unsqueeze(2).to_broadcast([P, GRP, P]),
                        ALU.is_equal)
                    for k in range(GRP * g, GRP * (g + 1)):
                        t = body * BODY_T + k
                        for half, gate in enumerate((g_hi, g_lo)):
                            last = nc.vector.tensor_scalar(oh_1[:, k, half], iota[:], i_t[:, 0, ds(t, 1)],
                                                           gate[:, ds(t, 1)].bitcast(F32), ALU.is_equal, ALU.mult)
                    last.then_inc(oh_ready, 1)

            dve.wait_ge(g_sum, T // GRP * (l + 1) - GROUPS + RING)
            for g in range(GROUPS):
                dve.wait_ge(g_ev, T // GRP * (l + 1) - GROUPS + g + 1 + RING)
                t0 = (BODIES - 1) * BODY_T + GRP * g
                dst = g_stage[:, 1, :, t0:t0 + GRP]
                nc.vector.tensor_tensor(dst, dst, parts_of(g)[:, 1], ALU.add).then_inc(g_sum, 1)

            def gated(b, s):
                i = (b - s) // 2
                dve.wait_ge(s_gh[s], (EB // 2 * l + i + 1) * 32)
                dve.wait_ge(g_sum, T // GRP * (l + 1) + RING)
                nc.vector.tensor_tensor(w_f[:, s, 0:T_D], g_in[:, s], h_in[:, s, 0:T_D], ALU.mult)
                nc.vector.tensor_tensor(
                    w_f[:, s, T_D:T].rearrange("p (w o t) -> p w o t", w=2, o=1), g_stage[:, :, ds(b, 1), :],
                    h_in[:, s, T_D:T].rearrange("p (w o t) -> p w o t", w=2, o=1), ALU.mult).then_inc(wt_f, 1)
                dve.wait_ge(wt_h, EB * l + b + 1)
                nc.vector.tensor_tensor(wt_lo[:, s], w_f[:, s], wt_hi[:, s].bitcast(F32), ALU.subtract).then_inc(wt_l, 1)

            gated(0, 0)
            with dve.Fori(0, EB // 2 - 1) as i:
                gated(2 * i + 1, 1)
                rest_block(2 * i + QB + EB + 2)
                gated(2 * i + 2, 0)
            gated(EB - 1, 1)
            for tb in range(TB + 1):
                if tb < TB:
                    if tb < TB - 1:
                        dve.wait_ge(v_rows, (TB - 1) * l + tb + 1)
                    else:
                        dve.wait_ge(st_used, ST_PER * (l + 1) + PRIME)
                    xs = x_tok[:, tb]
                    nc.vector.scalar_tensor_tensor(
                        out=xs, in0=xs, scalar=ALPHA, in1=ps[:, 2 * tb:2 * tb + 2].rearrange("p b n -> p (b n)"),
                        op0=ALU.mult, op1=ALU.add).then_inc(ffn_done, 1)
                if tb > 0:
                    dve.wait_ge(ffn_done, TB * l + tb)
                    for half in range(2):
                        last = row_stats(tb - 1, half)
            layer_norm(1, at, last)

    @block.tensor
    def _(pe):
        pe.sem_inc(pj_ps, PRIME * TB)
        pe.sem_inc(qk_tr, PRIME)
        pe.sem_inc(pt_ps, PRIME)
        pe.sem_inc(pv_done, PRIME)
        pe.sem_inc(st_used, PRIME)
        pe.sem_inc(g_tok, GROUPS)
        pe.wait_ge(s_x, 3 * 16)
        pe.wait_ge(consts_set, 2)

        def product(dst, lhs, rhs, first, last):
            nc.tensor.matmul(dst, lhs[0], rhs[0], start=first, stop=False)
            nc.tensor.matmul(dst, lhs[0], rhs[1], start=False, stop=False)
            return nc.tensor.matmul(dst, lhs[1], rhs[0], start=False, stop=last)

        with pe.Fori(0, L) as l:

            def turn(src, norms=None):
                for tb in range(TB):
                    if norms is not None and tb < LN_D:
                        pe.wait_ge(ln_done, LN_D * norms + tb + 1)
                    elif norms is not None:
                        pe.wait_ge(ln_tail, norms + 1)
                    for c in range(DC):
                        last = nc.tensor.transpose(ps[:, c, tb * P:(tb + 1) * P], src[:, tb, c * P:(c + 1) * P],
                                                   ident[:])
                        if tb == TB - 1:
                            last.then_inc(tr_ps, 1)

            def split_chunk(u, c):
                pe.wait_ge(tr_lo, DC * (3 * l + u) + c + 1)

            def group(n, s, width, operand=None):
                pe.wait_ge(wc_lo, W_PER * l + n + 1 + PRIME)
                for tb in range(TB):
                    rows = slice(tb * P, (tb + 1) * P)
                    for c in range(DC):
                        if operand is not None and tb == 0:
                            split_chunk(operand, c)
                        cols = slice(c * width, (c + 1) * width)
                        last = product(ps[:, TB * s + tb, 0:width], (t_hi[:, c, rows], t_lo[:, c, rows]),
                                       (w_hi[:, s, cols], w_lo[:, s, cols]), c == 0, c == DC - 1)
                    last.then_inc(pj_ps, 1)

            turn(x_tok, 2 * l)
            def in_pair(i, operand=None):
                for s in range(2):
                    n = 2 * i + s
                    pe.wait_ge(pj_act, 2 * (IN_G * l + n + 1))
                    pe.wait_ge(pj_dve, 2 * (IN_G * l + n + 1))
                    group(n, s, IN_N, operand if s == 0 else None)

            in_pair(0, 0)
            with pe.Fori(1, IN_G // 2) as i:
                in_pair(i)
            pe.wait_ge(lat_ready, l + 1)
            pe.wait_ge(pj_act, 2 * (IN_G * (l + 1) - 1) + 2 * PRIME)
            pe.wait_ge(pj_dve, 2 * (IN_G * (l + 1) - 1) + 2 * PRIME)
            for k in range(3):
                for tb in range(TB):
                    last = nc.tensor.transpose(ps[:, k, tb * P:(tb + 1) * P], lat_n[:, tb, k * P:(k + 1) * P], ident[:])
                last.then_inc(lat_tr, 1)
            pe.wait_ge(s_lay, 16 * 10 * (l + 1))
            pe.wait_ge(lat_ev, 3 * (l + 1))
            pe.wait_ge(pj_act, 2 * IN_G * (l + 1) + 2 * PRIME)
            pe.wait_ge(pj_dve, 2 * IN_G * (l + 1) + 2 * PRIME)
            for tb in range(TB):
                bank = 4 * ((tb + 1) % 2)
                rows = slice(tb * P, (tb + 1) * P)
                if tb >= 2:
                    pe.wait_ge(lat_qev, TB * l + tb - 1)
                    pe.wait_ge(lat_kev, TB * l + tb - 1)
                w = UQ_W // 2
                for half in range(2):
                    for k in range(2):
                        last = nc.tensor.matmul(ps[:, bank + half, 0:w], lat_t[:, k, rows],
                                                w_uq[:, k, half * w:(half + 1) * w], start=k == 0, stop=k == 1)
                last.then_inc(lat_ps, 1)
                w = UKV_W // 2
                for half in range(2):
                    last = nc.tensor.matmul(ps[:, bank + 2 + half, 0:w], lat_t[:, 2, rows],
                                            w_ukv[:, half * w:(half + 1) * w], start=True, stop=True)
                last.then_inc(lat_ps, 1)
            pe.wait_ge(lat_qev, TB * (l + 1))
            pe.wait_ge(lat_kev, TB * (l + 1))

            def turn_qk(j, s):
                pe.wait_ge(rope_done, JOBS * l + j + 1)
                for k in range(2):
                    for tb in range(TB):
                        last = nc.tensor.transpose(ps[0:DK, 4 + k, tb * P:(tb + 1) * P], rq[:, s, tb, k], ident[:])
                last.then_inc(qk_tr, 1)

            def score(j, s, qb, split):
                if qb == 0:
                    pe.wait_ge(q_ev, JOBS * l + j + 1 + PRIME)
                    pe.wait_ge(k_ev, JOBS * l + j + 1 + PRIME)
                pe.wait_ge(s_min, MAPS * l + TB * j + qb + 1)
                q, k = (q_a, k_a) if split else (q_t, k_t)
                nc.tensor.matmul(ps[:, qb % 2], q[0:DK, s, qb * P:(qb + 1) * P], k[0:DK, s], start=True,
                                 stop=True).then_inc(s_ps, 1)

            def turn_p(j, qb):
                pe.wait_ge(s_exp, MAPS * l + TB * j + qb + 1 + PRIME)
                pe.wait_ge((pt_dve, pt_act)[qb % 2], 2 * (JOBS * l + j) + qb // 2 + 1)
                for k in range(TB):
                    last = nc.tensor.transpose(ps[:, 2 + qb % 2, k * P:(k + 1) * P],
                                               probs[:, qb % 2, k * P:(k + 1) * P], ident[:])
                last.then_inc(pt_ps, 1)

            def values(i, s, qb, split):
                j = 2 * i + s
                if qb == 0:
                    pe.wait_ge(o_ev, JOBS * l + j + 1)
                    if not split:
                        pe.wait_ge(v_ready, (JOBS - JA) * l + (j - JA) + 1)
                pe.wait_ge((pt_dve, pt_act)[qb % 2], 2 * (JOBS * l + j) + qb // 2 + 1 + 1)
                for k in range(TB):
                    v = h[:, k, ds(i * ADV + COL_AV, ADV)] if split else v_s[:, s, k]
                    last = nc.tensor.matmul(ps[:, 6 + s, qb * VD:(qb + 1) * VD], p_t[:, qb, k], v, start=k == 0, stop=k == TB - 1)
                if qb == TB - 1:
                    last.then_inc(pv_done, 1)

            def job(i, s, split, ahead, before=None):
                j = 2 * i + s
                last_i = i if s else i - 1
                score(j, s, 2, split)
                turn_p(j, 0)
                if before is not None:
                    values(last_i, 1 - s, 2, before)
                if ahead is not None:
                    turn_qk(j + 1, 1 - s)
                score(j, s, 3, split)
                turn_p(j, 1)
                if before is not None:
                    values(last_i, 1 - s, 3, before)
                if ahead is not None:
                    score(j + 1, 1 - s, 0, ahead)
                turn_p(j, 2)
                values(i, s, 0, split)
                if ahead is not None:
                    score(j + 1, 1 - s, 1, ahead)
                turn_p(j, 3)
                values(i, s, 1, split)

            turn_qk(0, 0)
            score(0, 0, 0, True)
            score(0, 0, 1, True)
            job(0, 0, True, True)
            job(0, 1, True, True, True)
            with pe.Fori(1, JA // 2 - 1) as i:
                job(i, 0, True, True, True)
                job(i, 1, True, True, True)
            job(JA // 2 - 1, 0, True, True, True)
            job(JA // 2 - 1, 1, True, False, True)
            job(JA // 2, 0, False, False, True)
            job(JA // 2, 1, False, False, False)
            with pe.Fori(JA // 2 + 1, JOBS // 2 - 1) as i:
                job(i, 0, False, False, False)
                job(i, 1, False, False, False)
            job(JOBS // 2 - 1, 0, False, False, False)
            job(JOBS // 2 - 1, 1, False, None, False)
            values(JOBS // 2 - 1, 1, 2, False)
            values(JOBS // 2 - 1, 1, 3, False)
            pe.wait_ge(mix_ready, l + 1)
            turn(o_all[:, :, A_W:A_W + D])
            for k in range(O_G):
                if k >= 2:
                    pe.wait_ge(pj_res, TB * (O_G * l + k - 1))
                group(IN_G + k, k % 2, O_N, 1 if k == 0 else None)
            turn(x_tok, 2 * l + 1)
            pe.wait_ge(s_keys, 16 * (l + 1))

            def stationary(m, s, dst, operand=None):
                pe.wait_ge(st_l[s], ST_PER // 2 * l + m + 1 + 1)
                for c in range(DC):
                    if operand is not None:
                        split_chunk(operand, c)
                    last = product(dst, (st_hi[:, s, c], st_lo[:, s, c]), (t_hi[:, c], t_lo[:, c]), c == 0,
                                   c == DC - 1)
                last.then_inc(st_used, 1)

            def key_scores(f, s):
                pe.wait_ge(pq_ready, QB * l + f + 1)
                pe.wait_ge(sc_ev, QB * l + f + 1)
                for tb in range(TB):
                    rows = slice(tb * P, (tb + 1) * P)
                    last = nc.tensor.matmul(ps[:, 2 + s, tb * NK:(tb + 1) * NK], pq[:, s, rows],
                                            keys[:, ds(f, 1)].rearrange("p o n -> p (o n)"), start=True, stop=True)
                last.then_inc(sc_ps, 1)

            def query_pair(i, operand=None):
                for s in range(2):
                    stationary(i, s, ps[:, s], operand if s == 0 else None)
                for s in range(2):
                    key_scores(2 * i + s, s)

            query_pair(0, 2)
            with pe.Fori(1, QB // 2) as i:
                query_pair(i)

            def experts(m, s):
                pe.wait_ge(gelu_done, EB * l + 2 * m + s + 1)
                stationary(m + QB // 2, s, ps[:, s])

            with pe.Fori(0, UNITS) as i:
                for s in range(2):
                    experts(i, s)
            experts(UNITS, 0)
            pe.wait_ge(gate_ready, l + 1)
            for k in range(3):
                src = e_all[:].rearrange("p u k -> p (u k)") if k == 2 else i_all[:, k]
                for tb in range(TB):
                    last = nc.tensor.transpose(ps[:, 5 + k, tb * P:(tb + 1) * P], src[:, tb * P:(tb + 1) * P], ident[:])
                last.then_inc(sel_tr, 1)

            experts(UNITS, 1)

            def spread(body, g, last=False):
                if last and g >= RING:
                    pe.wait_ge(g_sum, T // GRP * l + GROUPS * body + g + 1)
                else:
                    pe.wait_ge(g_ev, T // GRP * l + GROUPS * body + g + 1)
                pe.wait_ge(oh_ready, T // GRP * l + GROUPS * body + g + 1)
                for k in range(GRP):
                    dst = ps[:, 2 + 2 * (g % RING) + k // 2, k % 2 * 2 * P:(k % 2 + 1) * 2 * P]
                    last = nc.tensor.matmul(dst, oh_2[:, GRP * g + k],
                                            oh_1[:, GRP * g + k].rearrange("p h n -> p (h n)"), start=True, stop=True)
                last.then_inc(g_tok, 1)

            with pe.Fori(0, WIN * BODIES - 1) as body:
                for g in range(GROUPS):
                    spread(body, g)
                    if g % (GROUPS // 2) == 1:
                        experts(body + UNITS + 1, g // (GROUPS // 2))
            for g in range(GROUPS):
                spread(WIN * BODIES - 1, g, last=True)
            pe.wait_ge(gelu_done, EB * (l + 1) + PRIME)
            pe.wait_ge(g_sum, T // GRP * (l + 1) + RING)
            for bank in range(8):
                nc.tensor.matmul(ps[:, bank], zeros_bf[:, 0:P], zeros_bf[:, 0:T], start=True, stop=True,
                                 skip_group_check=True)

            def gather(i, s, final=False):
                pe.wait_ge(st_l[s], ST_PER // 2 * l + (QB + EB) // 2 + i + 1 + 1)
                pe.wait_ge(wt_l, EB * l + 2 * i + s + 1)
                v_hi = st_hi[:, s].rearrange("p c f -> p (c f)")
                v_lo = st_lo[:, s].rearrange("p c f -> p (c f)")
                for tb in range(TB):
                    rows = slice(tb * P, (tb + 1) * P)
                    for w, v in ((wt_hi, v_hi), (wt_hi, v_lo), (wt_lo, v_hi)):
                        for half in range(2):
                            last = nc.tensor.matmul(ps[:, 2 * tb + half], w[:, s, rows],
                                                    v[:, half * 512:(half + 1) * 512], start=False, stop=True,
                                                    skip_group_check=True)
                    if final and tb < TB - 1:
                        last.then_inc(v_rows, 1)
                last.then_inc(st_used, 1)

            with pe.Fori(0, EB // 2 - 1) as i:
                for s in range(2):
                    gather(i, s)
            gather(EB // 2 - 1, 0)
            gather(EB // 2 - 1, 1, final=True)

    ctx.close()


def rope_table(width):
    half = width // 2
    inv = np.exp(np.float32(-math.log(10000.0)) * np.arange(half, dtype=np.float32) / np.float32(half))
    ang = np.arange(T, dtype=np.float32)[:, None] * inv.astype(np.float32)[None, :]
    cos, sin = np.cos(ang), np.sin(ang)
    both = np.stack([np.concatenate([cos, cos], 1), np.concatenate([-sin, sin], 1)])
    return np.ascontiguousarray(both.reshape(2, TB, P, width).transpose(2, 0, 1, 3).astype(np.float32))


def mask_table():
    delta = np.abs(np.arange(MASK_W)[None, :] - 3 * P - np.arange(P)[:, None])
    count = sum((delta % dil == 0) & (delta // dil <= window // (2 * dil))
                for window, dil in ((128, 1), (512, 4), (2048, 16)))
    return np.where(count > 0, -np.log(np.maximum(count, 1)), BIG).astype(np.float32)


def kernel(**inputs):
    import concourse.bacc as bacc
    from concourse.bass_utils import run_bass_kernel_spmd

    x = {k: np.asarray(v) for k, v in inputs.items()}

    def columns(w, groups):
        n_l, k, n = w.shape
        w = w.reshape(n_l, k // P, P, groups, n // groups).transpose(0, 3, 2, 1, 4)
        return w.reshape(n_l, groups, P, k // P * (n // groups))

    lam = [0.8 - 0.6 * math.exp(-0.3 * (k + 1)) for k in range(L)]
    gains = [x["mla_q_norm_g"][:, 0:P], x["mla_q_norm_g"][:, P:QR], x["mla_kv_norm_g"], x["mla_kv_norm_g"]]
    arrays = {
        "x": x["x"].reshape(TB, P, D).transpose(1, 0, 2),
        "ident": np.eye(P, dtype=np.float32),
        "iota": np.tile(np.arange(P, dtype=np.float32), (P, 1)),
        "rope_a": np.stack([rope_table(ADK) * np.float32(-ADK ** -0.5), rope_table(ADK)], axis=3),
        "rope32": rope_table(32), "rope64": rope_table(64), "mask": mask_table(),
        "lam_c": np.array([[-v, 1.0 - v] for v in lam], np.float32),
        "w_in": columns(x["w_in"], IN_G), "w_o": columns(x["w_o"], O_G),
        "mla_w_uq": x["mla_w_uq"].reshape(L, 2, P, UQ_W).transpose(0, 2, 1, 3),
        "mla_w_ukv": x["mla_w_ukv"], "g_lat": np.stack(gains, axis=-1),
        "diff_lambda": x["diff_lambda"], "diff_subln_g": x["diff_subln_g"],
        "ln1": np.stack([x["ln1_g"], x["ln1_b"]], 1), "ln2": np.stack([x["ln2_g"], x["ln2_b"]], 1),
        "peer_w_q": columns(x["peer_w_q"], QB),
        "peer_keys": x["peer_sub_keys"].transpose(0, 4, 1, 2, 3).reshape(L, P, QB, NK),
        "peer_u": x["peer_u"].reshape(L, EB, P, DC, P).transpose(0, 1, 4, 3, 2).reshape(L, EB, P, DC * P),
        "peer_v": x["peer_v"].reshape(L, EB, P, D),
    }
    nc = bacc.Bacc("TRN2", target_bir_lowering=False, num_devices=1)
    arrays = {f"in_{k}": np.ascontiguousarray(v) for k, v in arrays.items()}
    aps = {k[3:]: nc.dram_tensor(k, v.shape, mybir.dt.from_np(v.dtype), kind="ExternalInput").ap()
           for k, v in arrays.items()}
    out = nc.dram_tensor("out_tokens", (TB, P, D), F32, kind="ExternalOutput").ap()
    build(nc, aps, out.rearrange("t p d -> p t d"))
    r = run_bass_kernel_spmd(nc, [arrays], core_ids=[0])
    return r.results[0]["out_tokens"].reshape(1, T, D)
```
